# Optimizing a Trainium2 kernel written in Bass

```python
import jax
import jax.numpy as jnp
from jax import lax
import numpy as np

D_MODEL = 1024
BATCH = 1
SEQ = 128
DEPTH = 1
DEC_BATCH = 1
DEC_SEQ = 256
PAST_LEN = 128

GRID_W = 64
D_CONV = D_MODEL
D_RNN = D_MODEL
N_RNN_HEADS = 8
RNN_HEAD_DIM = D_RNN // N_RNN_HEADS
CONV_MIX_W = 3
CONV_MIX_LEFT = 1
RNN_CONV_W = 4
RNN_CONV_LEFT = 2
RG_C = 8.0
N_GROUPS = 4
EXPERTS_PER_GROUP = 8
N_EXPERTS = N_GROUPS * EXPERTS_PER_GROUP
TOP_K = 2
D_EXPERT = 512
EPS = 1e-6
D_IN = 3 * D_CONV + 2 * D_RNN + 2 * D_MODEL
IN_SPLITS = (D_CONV, 2 * D_CONV, 3 * D_CONV, 3 * D_CONV + D_RNN, 3 * D_CONV + 2 * D_RNN,
             3 * D_CONV + 2 * D_RNN + D_MODEL)
F32 = jnp.float32

kernel_name = 'hybrid_conv_rglru_hmoe_diffusion_step'

def rmsnorm(x, g):
    xf = x.astype(F32)
    y = xf * lax.rsqrt(jnp.mean(xf * xf, axis=-1, keepdims=True) + EPS)
    return (y * g.astype(F32)).astype(x.dtype)

def dwconv(x, w, left):
    k_w = w.shape[0]
    n_pos = x.shape[1]
    xp = jnp.pad(x, ((0, 0), (left, k_w - 1 - left), (0, 0)))
    y = xp[:, 0:n_pos] * w[0]
    for k in range(1, k_w):
        y = y + xp[:, k:k + n_pos] * w[k]
    return y

def conv_over_tokens(x, w, left, on_grid):
    if on_grid:
        b, n, ch = x.shape
        rows = n // GRID_W
        return dwconv(x.reshape(b * rows, GRID_W, ch), w, left).reshape(b, n, ch)
    return dwconv(x, w, left)

def linear_scan(a, u, h0, reverse):
    first = -1 if reverse else 0
    u = u.at[:, first].add(a[:, first] * h0)

    def combine(l, r):
        a_l, u_l = l
        a_r, u_r = r
        return a_l * a_r, a_r * u_l + u_r

    _, h = lax.associative_scan(combine, (a, u), axis=1, reverse=reverse)
    return h

def rg_lru(xc, h0, w_a, b_a, w_x, b_x, lam, reverse):
    bsz, n, _ = xc.shape
    xh = xc.reshape(bsz, n, N_RNN_HEADS, RNN_HEAD_DIM)
    r = jax.nn.sigmoid(jnp.einsum('bnhi,hij->bnhj', xh, w_a).reshape(bsz, n, D_RNN) + b_a).astype(F32)
    i = jax.nn.sigmoid(jnp.einsum('bnhi,hij->bnhj', xh, w_x).reshape(bsz, n, D_RNN) + b_x).astype(F32)
    log_a = -RG_C * r * jax.nn.softplus(-lam.astype(F32))
    a = jnp.exp(log_a)
    u = jnp.sqrt(-jnp.expm1(2.0 * log_a)) * (i * xc.astype(F32))
    h = linear_scan(a, u, h0.astype(F32), reverse)
    h_last = h[:, 0] if reverse else h[:, -1]
    return h, h_last

def token_mixer(h, h0, on_grid, p):
    u = h @ p['w_in']
    b_c, c_c, v_c, x_r, g_r, m_a, m_b = jnp.split(u, IN_SPLITS, axis=-1)
    y_a = (b_c * conv_over_tokens(c_c * v_c, p['conv_w'], CONV_MIX_LEFT, on_grid)) @ p['w_conv_out']
    x_c = conv_over_tokens(x_r, p['rnn_conv_w'], RNN_CONV_LEFT, False) + p['rnn_conv_b']
    h_f, last_f = rg_lru(x_c, h0[:, 0], p['w_gate_a'][0], p['b_gate_a'][0], p['w_gate_x'][0],
                         p['b_gate_x'][0], p['lam'][0], False)
    h_b, last_b = rg_lru(x_c, h0[:, 1], p['w_gate_a'][1], p['b_gate_a'][1], p['w_gate_x'][1],
                         p['b_gate_x'][1], p['lam'][1], True)
    y_b = ((h_f + h_b).astype(h.dtype) * jax.nn.gelu(g_r)) @ p['w_rnn_out']
    merged = jax.nn.sigmoid(m_a) * y_a + jax.nn.sigmoid(m_b) * y_b
    return merged @ p['w_o'], jnp.stack([last_f, last_b], axis=1)

def hier_moe(h, p):
    bsz, n, d = h.shape
    t = h.reshape(bsz * n, d)
    lg = (t @ p['w_router_group'] + p['b_router_group']).astype(F32)
    pg = jax.nn.softmax(lg, axis=-1)
    grp = jnp.argmax(lg, axis=-1)
    p_grp = jnp.take_along_axis(pg, grp[:, None], axis=-1)
    le = (t @ p['w_router_expert'] + p['b_router_expert']).astype(F32)
    le = le.reshape(-1, N_GROUPS, EXPERTS_PER_GROUP)
    le_g = jnp.take_along_axis(le, grp[:, None, None], axis=1)[:, 0]
    pe = jax.nn.softmax(le_g, axis=-1)
    top_p, top_i = lax.top_k(pe, TOP_K)
    wts = p_grp * top_p / jnp.sum(top_p, axis=-1, keepdims=True)
    ids = grp[:, None] * EXPERTS_PER_GROUP + top_i
    gates = jnp.sum(jax.nn.one_hot(ids, N_EXPERTS, dtype=F32) * wts[..., None], axis=1).astype(t.dtype)
    y = jnp.zeros_like(t)
    for e in range(N_EXPERTS):
        z = jax.nn.silu(t @ p['w1'][e]) * (t @ p['w3'][e])
        y = y + gates[:, e:e + 1] * (z @ p['w2'][e])
    return y.reshape(bsz, n, d)

def layer(x, cond, h0, on_grid, p):
    mod = (jax.nn.silu(cond) @ p['w_ada'] + p['b_ada'])[:, None, :]
    sh1, sc1, g1, sh2, sc2, g2 = jnp.split(mod, 6, axis=-1)
    h = rmsnorm(x, p['g_norm1']) * (1 + sc1) + sh1
    mix, h_last = token_mixer(h, h0, on_grid, p)
    x = x + g1 * mix
    h = rmsnorm(x, p['g_norm2']) * (1 + sc2) + sh2
    x = x + g2 * hier_moe(h, p)
    return x, h_last

def setup_inputs(seed: int = 0) -> dict:
    key = jax.random.key(seed)
    ks = jax.random.split(key, 32)
    nrm = jax.random.normal
    s_d = D_MODEL ** -0.5
    a0 = jax.random.uniform(ks[14], (DEPTH, 2, D_RNN), F32, minval=0.9, maxval=0.999)
    s = a0 ** (1.0 / RG_C)
    lam = jnp.log(s) - jnp.log1p(-s)
    return {
        'x_prompt': nrm(ks[0], (BATCH, SEQ, D_MODEL), F32),
        'x_sample': nrm(ks[1], (DEC_BATCH, DEC_SEQ, D_MODEL), F32),
        'state_rnn': 0.5 * nrm(ks[2], (DEC_BATCH, DEPTH, 2, D_RNN), F32),
        'c': nrm(ks[3], (DEC_BATCH, D_MODEL), F32),
        'c_ctx': nrm(ks[4], (D_MODEL,), F32),
        'w_ada': s_d * nrm(ks[5], (DEPTH, D_MODEL, 6 * D_MODEL), F32),
        'b_ada': 0.02 * nrm(ks[6], (DEPTH, 6 * D_MODEL), F32),
        'g_norm1': 1.0 + 0.02 * nrm(ks[7], (DEPTH, D_MODEL), F32),
        'g_norm2': 1.0 + 0.02 * nrm(ks[8], (DEPTH, D_MODEL), F32),
        'w_in': s_d * nrm(ks[9], (DEPTH, D_MODEL, D_IN), F32),
        'conv_w': (CONV_MIX_W ** -0.5) * nrm(ks[10], (DEPTH, CONV_MIX_W, D_CONV), F32),
        'w_conv_out': (D_CONV ** -0.5) * nrm(ks[11], (DEPTH, D_CONV, D_MODEL), F32),
        'rnn_conv_w': (RNN_CONV_W ** -0.5) * nrm(ks[12], (DEPTH, RNN_CONV_W, D_RNN), F32),
        'rnn_conv_b': 0.02 * nrm(ks[13], (DEPTH, D_RNN), F32),
        'w_gate_a': (RNN_HEAD_DIM ** -0.5) * nrm(ks[15], (DEPTH, 2, N_RNN_HEADS, RNN_HEAD_DIM, RNN_HEAD_DIM), F32),
        'b_gate_a': 0.02 * nrm(ks[16], (DEPTH, 2, D_RNN), F32),
        'w_gate_x': (RNN_HEAD_DIM ** -0.5) * nrm(ks[17], (DEPTH, 2, N_RNN_HEADS, RNN_HEAD_DIM, RNN_HEAD_DIM), F32),
        'b_gate_x': 0.02 * nrm(ks[18], (DEPTH, 2, D_RNN), F32),
        'lam': lam,
        'w_rnn_out': (D_RNN ** -0.5) * nrm(ks[19], (DEPTH, D_RNN, D_MODEL), F32),
        'w_o': s_d * nrm(ks[20], (DEPTH, D_MODEL, D_MODEL), F32),
        'w_router_group': s_d * nrm(ks[21], (DEPTH, D_MODEL, N_GROUPS), F32),
        'b_router_group': 0.01 * nrm(ks[22], (DEPTH, N_GROUPS), F32),
        'w_router_expert': s_d * nrm(ks[23], (DEPTH, D_MODEL, N_EXPERTS), F32),
        'b_router_expert': 0.01 * nrm(ks[24], (DEPTH, N_EXPERTS), F32),
        'w1': s_d * nrm(ks[25], (DEPTH, N_EXPERTS, D_MODEL, D_EXPERT), F32),
        'w3': s_d * nrm(ks[26], (DEPTH, N_EXPERTS, D_MODEL, D_EXPERT), F32),
        'w2': (D_EXPERT ** -0.5) * nrm(ks[27], (DEPTH, N_EXPERTS, D_EXPERT, D_MODEL), F32),
        'g_final': 1.0 + 0.02 * nrm(ks[28], (D_MODEL,), F32),
    }

def reference(x_prompt, x_sample, state_rnn, c, c_ctx, w_ada, b_ada, g_norm1, g_norm2, w_in,
              conv_w, w_conv_out, rnn_conv_w, rnn_conv_b, w_gate_a, b_gate_a, w_gate_x, b_gate_x,
              lam, w_rnn_out, w_o, w_router_group, b_router_group, w_router_expert,
              b_router_expert, w1, w3, w2, g_final):
    layers = [dict(w_ada=w_ada[l], b_ada=b_ada[l], g_norm1=g_norm1[l], g_norm2=g_norm2[l],
                   w_in=w_in[l], conv_w=conv_w[l], w_conv_out=w_conv_out[l],
                   rnn_conv_w=rnn_conv_w[l], rnn_conv_b=rnn_conv_b[l], w_gate_a=w_gate_a[l],
                   b_gate_a=b_gate_a[l], w_gate_x=w_gate_x[l], b_gate_x=b_gate_x[l], lam=lam[l],
                   w_rnn_out=w_rnn_out[l], w_o=w_o[l], w_router_group=w_router_group[l],
                   b_router_group=b_router_group[l], w_router_expert=w_router_expert[l],
                   b_router_expert=b_router_expert[l], w1=w1[l], w3=w3[l], w2=w2[l])
              for l in range(DEPTH)]

    cond_ctx = c_ctx[None, :]
    h0_ctx = jnp.zeros((x_prompt.shape[0], 2, D_RNN), F32)
    xp = x_prompt
    finals = []
    for l in range(DEPTH):
        xp, h_last = layer(xp, cond_ctx, h0_ctx, False, layers[l])
        finals.append(h_last)
    state_rnn_new = jnp.stack(finals, axis=1).astype(x_prompt.dtype)
    y_prompt = rmsnorm(xp, g_final)

    xs = x_sample
    for l in range(DEPTH):
        xs, _ = layer(xs, c, state_rnn[:, l], True, layers[l])
    y_sample = rmsnorm(xs, g_final)

    return (y_prompt, y_sample, state_rnn_new)


_drawn_inputs = setup_inputs


def setup_inputs(seed=0):
    import zlib

    import numpy as np

    out = dict(_drawn_inputs(seed))
    spreads = {}
    factors = {'b_gate_a': 21.615,
     'b_gate_x': 6.456,
     'b_router_group': 4.497,
     'b_router_expert': 6.658,
     'g_norm2': 3.017}
    for name, (base, spread) in spreads.items():
        noise = np.random.default_rng([zlib.crc32(name.encode()), seed]).standard_normal(out[name].shape)
        drawn = base * np.exp(spread * noise) if base else spread * noise
        out[name] = jnp.asarray(drawn.astype(out[name].dtype))
    for name, factor in factors.items():
        out[name] = (out[name] * factor).astype(out[name].dtype)
    return out
```

```python
from contextlib import ExitStack

import concourse.bass as bass
from concourse import mybir

F32 = mybir.dt.float32
U32 = mybir.dt.uint32
I32 = mybir.dt.int32
ALU = mybir.AluOpType
ACT = mybir.ActivationFunctionType
AX_X = mybir.AxisListType.X

P = 128
EPS = 1e-6
RG_C = 8.0
GRID_W = 64


def layer_program(nc, x_prompt, x_sample, state_rnn, c, c_ctx, w_ada, b_ada, g_norm1, g_norm2, w_in,
                  conv_w, w_conv_out, rnn_conv_w, rnn_conv_b, w_gate_a, b_gate_a, w_gate_x, b_gate_x,
                  lam, w_rnn_out, w_o, w_router_group, b_router_group, w_router_expert,
                  b_router_expert, w1, w3, w2, g_final, y_prompt, y_sample, state_new):
    D = w_o.shape[1]
    NP_TOK = x_prompt.shape[1]
    NS_TOK = x_sample.shape[1]
    T = NP_TOK + NS_TOK
    TT = T // P
    KD = D // P
    NG = w_router_group.shape[2]
    NE = w_router_expert.shape[2]
    EG = NE // NG
    FE = w1.shape[3]
    JF = FE // P
    assert NP_TOK == P and D == 1024 and FE == 512 and NS_TOK % GRID_W == 0

    CW = 512
    CT = CW // P
    SLOTS = 6
    BANKS = 6

    GAP = 3
    S0 = NP_TOK + GAP
    TG = S0 + NS_TOK
    ROWS = NS_TOK // GRID_W
    CG = 1 + NP_TOK + 1 + ROWS * (GRID_W + 1)

    CAP = 80
    OB = 4
    OC = (T - CAP) // OB
    OT = OB * OC
    assert CAP + OT == T

    BADA, CCTX, CSMP, GN1, GN2, STF, STB = 0, 48, 56, 64, 72, 80, 88
    CVW, RCW, RCB, BGA, BGX, LAM, NPAR = 96, 120, 152, 160, 176, 192, 208
    NPA = 96

    rowvec = nc.dram_tensor("mod_rows", [8, D], F32).ap()
    h2_dram = nc.dram_tensor("h2_rows", [T, D], F32).ap()
    y_dram = nc.dram_tensor("expert_rows", [NE * CAP, D], F32).ap()
    oy_dram = nc.dram_tensor("overflow_rows", [NE * OT, D], F32).ap()

    ada_v = w_ada[0].rearrange("(k p) n -> p k n", p=P)
    win_v = w_in[0].rearrange("(k p) n -> p k n", p=P)
    wco_v = w_conv_out[0].rearrange("(k p) n -> p k n", p=P)
    wro_v = w_rnn_out[0].rearrange("(k p) n -> p k n", p=P)
    wo_v = w_o[0].rearrange("(k p) n -> p k n", p=P)
    w1_v = w1[0].rearrange("e (p k) n -> e p (k n)", p=P)
    w3_v = w3[0].rearrange("e (p k) n -> e p (k n)", p=P)
    w2_v = w2[0].rearrange("e (j p) n -> e p j n", p=P)
    U_COL = {"b": 0, "c": D, "v": 2 * D, "xr": 3 * D, "g": 4 * D, "ma": 5 * D, "mb": 6 * D}

    stream, chunks = [], []

    def add_chunk(kind, half):
        chunks.append((kind, half))
        for m in range(CT):
            stream.append((kind, CT * half + m))

    def add_gates(b):
        for h in (2 * b, 2 * b + 1):
            for d in range(2):
                for x in range(2):
                    stream.append(("gate", h, d, x))

    stream += [("par", 0), ("par", 1)] + [("xT", k) for k in range(KD)]
    for j in range(4):
        chunks.append(("ada", j))
        stream.append(("ada", j))
    add_chunk("xr", 0)
    add_chunk("xr", 1)
    add_gates(0)
    add_chunk("c", 0)
    add_gates(1)
    add_chunk("v", 0)
    add_gates(2)
    add_chunk("g", 0)
    add_gates(3)
    for kind, half in (("b", 0), ("c", 1), ("v", 1), ("b", 1), ("g", 1), ("ma", 0), ("ma", 1),
                       ("mb", 0), ("mb", 1)):
        add_chunk(kind, half)
    for j in range(4, 12):
        chunks.append(("ada", j))
        stream.append(("ada", j))
    stream += [("rows",), ("state",)]
    for kind in ("ya", "yb"):
        add_chunk(kind, 0)
        add_chunk(kind, 1)
    chunks += [("wo", 0), ("wo", 1)]
    for t in range(TT):
        stream += [("wo", t, 0), ("wo", t, 1)]
        if t >= 1:
            stream += [("h2T", t - 1, 0), ("h2T", t - 1, 1), ("route", t - 1)]
    stream += [("h2T", TT - 1, 0), ("h2T", TT - 1, 1), ("route", TT - 1)]
    stream += [("rank", t) for t in range(TT)] + [("count",), ("list",)]
    N_OF = {s: n for n, s in enumerate(stream)}
    C_OF = {s: n for n, s in enumerate(chunks)}
    N1 = len(chunks)
    PAIRS = NE // 2
    assert len(N_OF) == len(stream) and SLOTS == 6

    with ExitStack() as ctx:
        def sb(name, shape, dt=F32):
            return ctx.enter_context(nc.sbuf_tensor(name, shape, dt))

        def sem(name):
            return ctx.enter_context(nc.semaphore(name))

        ring = sb("ring", [P, SLOTS, KD * CW])
        x_rows = sb("x_rows", [P, TT, D])
        early = sb("early", [P, KD * T + 32 * P])
        xcy = sb("xcy", [P, KD * TG])
        hg = sb("hg", [P, KD * TG])
        lru = sb("lru", [P, 4 * 4 * TG])
        cp = sb("cp", [P, 2 * 4 * CG])
        xrp = sb("xrp", [P, 2, TG + 3])
        pT = sb("pT", [P, NPAR])
        ident = sb("ident", [P, P])
        ones = sb("ones", [P, P])
        before = sb("before", [P, P])
        iota = sb("iota", [P, T])
        tok = sb("tok", [P, TT])
        cvec = sb("cvec", [P, KD, 2])
        mod = sb("mod", [P, 6 * KD, 2])
        A1 = sb("A1", [P, KD, 2])
        rowsrc = sb("rowsrc", [P, 8, KD])
        sp = sb("sp", [P, 6, 16])
        rate = sb("rate", [P, 2, 16])
        stc = sb("stc", [P, 16])
        stat = sb("stat", [P, 3, 3, TT])
        wr = sb("wr", [P, KD, NG + NE])
        br = sb("br", [P, NG + NE])
        lg = sb("lg", [P, TT, 8])
        rt = sb("rt", [P, TT, 64])
        rti = sb("rti", [P, TT, 16], U32)
        rank = sb("rank", [P, TT, 2])
        wts = sb("wts", [P, TT, 2])
        slot_f = sb("slot_f", [P, TT, 2])
        slot_u = sb("slot_u", [P, TT, 2], U32)
        main_w = sb("main_w", [P, TT, 2])
        lists = sb("lists", [CAP, NE], U32)
        idx = [sb(f"idx{s}", [CAP, 1], U32) for s in range(2)]
        cmax = sb("cmax", [P, 1])
        flag = sb("flag", [P, 1], I32)
        oidx = [sb(f"oidx{b}", [OC, 1], U32) for b in range(OB)]
        bank = [ctx.enter_context(nc.psum_tensor(f"bank{i}", [P, 512], F32)) for i in range(BANKS)]

        par_rows = hg[:, 0:2 * P].rearrange("p (j n) -> p j n", j=2)
        rows_sb = xrp[0:64, 0, 0:P]
        st_sb = xrp[0:16, 1, 0:P]
        oh = early[:, 6 * D:]
        oh_u = oh.bitcast(U32)
        n_oh = TT * 2 * NE
        pick = oh[:, 0:n_oh].rearrange("p (t k e) -> p t k e", t=TT, k=2)
        tok_oh = oh[:, n_oh:2 * n_oh].rearrange("p (t k e) -> p t k e", t=TT, k=2)
        both = oh[:, 2 * n_oh:2 * n_oh + TT * NE].rearrange("p (t e) -> p t e", t=TT)
        rank_oh = oh[:, 2 * n_oh + TT * NE:2 * n_oh + TT * NE + TT * 2 * CAP]\
            .rearrange("p (t k r) -> p t k r", t=TT, k=2)
        hT = early[:, 0:KD * T].rearrange("p (k t) -> p k t", k=KD)
        gw = early[:, KD * T:].rearrange("p (x d h j) -> p x d h j", x=2, d=2, h=KD)
        G1 = early[:, 0:2 * D].rearrange("p (c d) -> p c d", c=2)
        A2 = early[:, 2 * D:4 * D].rearrange("p (c d) -> p c d", c=2)
        B2 = early[:, 4 * D:6 * D].rearrange("p (c d) -> p c d", c=2)
        xc = xcy[:, :].rearrange("p (k t) -> p k t", k=KD)
        ya_in = xcy[:, 0:KD * T].rearrange("p (k t) -> p k t", k=KD)
        hs = hg[:, 0:KD * T].rearrange("p (k t) -> p k t", k=KD)
        lru_v = lru[:, :].rearrange("p (b d h t) -> p b d h t", b=4, d=2, h=2)
        r_b, i_b, a_b, q_b = (lru_v[:, n] for n in range(4))
        lru_f = lru[:, :].rearrange("p (b n) -> p b n", b=4)
        r_f, i_f, a_f, q_f = (lru_f[:, n] for n in range(4))
        xs = lru[:, 0:TT * D].rearrange("p (t d) -> p t d", t=TT)
        junk = lru[:, TT * D:TT * D + D]
        SA = lru[:, 0:KD * T].rearrange("p (k t) -> p k t", k=KD)
        SB = lru[:, KD * T:2 * KD * T].rearrange("p (k t) -> p k t", k=KD)
        cpad = cp[:, 0:4 * CG].rearrange("p (m t) -> p m t", m=4)
        ycv = cp[:, 4 * CG:].rearrange("p (m t) -> p m t", m=4)
        G2 = cp[:, 0:2 * D].rearrange("p (c d) -> p c d", c=2)
        gfin = cp[:, 2 * D:3 * D]
        gtmp = xrp[:, :, 0:T]
        wo_tmp = hg[:, 0:CW]
        le = hg[:, CW + D:CW + D + TT * NE].rearrange("p (t e) -> p t e", t=TT)
        rank_m = hg[:, CW + D + TT * NE:CW + D + TT * NE + 2 * NE].rearrange("p (k e) -> p k e", k=2)
        olist = hg[0:OC, 0:OB * NE].bitcast(U32).rearrange("p (b e) -> p b e", b=OB)
        h2 = xcy[:, 0:2 * D].rearrange("p (b d) -> p b d", b=2)
        h2T = xcy[:, 2 * D:3 * D].rearrange("p (k t) -> p k t", k=KD)
        xg = hg[:, 0:2 * D].rearrange("p (b d) -> p b d", b=2)
        sil = hg[:, 2 * D:2 * D + JF * CAP]
        z = hg[:, 2 * D + JF * CAP:2 * D + 3 * JF * CAP].rearrange("p (b n) -> p b n", b=2)
        xgT = lru[:, 0:2 * KD * CAP].rearrange("p (b k t) -> p b k t", b=2, k=KD)
        y_sb = lru[:, 2 * KD * CAP:2 * KD * CAP + 2 * D].rearrange("p (b d) -> p b d", b=2)
        oxg = ring[:, 3, :].rearrange("p (b d) -> p b d", b=OB)
        oxgT = ring[:, 4, 0:KD * OT].rearrange("p (k t) -> p k t", k=KD)
        oz = ring[:, 5, 0:JF * OT].rearrange("p (j t) -> p j t", j=JF)
        osil = ring[:, 5, JF * OT:JF * OT + OT]
        oy = ring[:, 5, 2048:2048 + D]
        orank = ring[:, 4, 0:OT]
        yg = early[:, 0:4 * D].rearrange("p (b k d) -> p b k d", b=2, k=2)
        o_rows = early[:, 4 * D:6 * D].rearrange("p (b d) -> p b d", b=2)

        landed = [sem(f"chunk_landed{s}") for s in range(SLOTS)]
        tile_done = sem("tile_done")
        bank_free = [sem(f"bank_free{s}") for s in range(BANKS)]
        params_in = [sem("params_a_in"), sem("params_b_in")]
        x_in = sem("x_in")
        gate_w_in = sem("gate_w_in")
        router_in = sem("router_in")
        consts = sem("consts")
        cvec_ready = sem("cvec_ready")
        lam_exp = sem("lam_exp")
        rate_ready = sem("rate_ready")
        ssq_ready = sem("ssq_ready")
        mean_ready = sem("mean_ready")
        rms_ready = sem("rms_ready")
        xs_ready = sem("xs_ready")
        xT_ready = sem("xT_ready")
        h_ready = sem("h_ready")
        pads_zero = sem("pads_zero")
        xr_ready = sem("xr_ready")
        xc_ready = sem("xc_ready")
        sig_done = sem("gate_sigmoids")
        exp_done = sem("gate_exps")
        q_ready = sem("one_minus_a2")
        root_done = sem("gate_roots")
        batch_done = sem("scans_done")
        c_ready = sem("c_ready")
        conv_done = sem("conv_done")
        hg_ready = sem("hg_ready")
        merged_ready = sem("merged_ready")
        rowsrc_ready = sem("rowsrc_ready")
        rows_out = sem("rows_out")
        bcast_in = sem("bcast_in")
        state_out = sem("state_out")
        x1_ready = sem("x1_ready")
        h2_ready = sem("h2_ready")
        h2_out = [sem(f"h2_out{t}") for t in range(TT)]
        tops_ready = sem("tops_ready")
        texp_ready = sem("top_exps_ready")
        both_ready = sem("both_ready")
        onehots_ready = sem("onehots_ready")
        slots_ready = sem("slots_ready")
        bias_in = sem("router_bias_in")
        flag_ready = sem("flag_ready")
        idx_ready = sem("idx_ready")
        gathers_begun = sem("gathers_begun")
        xg_in = [sem(f"xg_in{s}") for s in range(2)]
        xg_used = sem("xg_transposed")
        xgT_a = sem("xgT_by_scalar")
        xgT_v = sem("xgT_by_vector")
        up_done = sem("w1_product")
        gate_done = sem("w3_product")
        silu_done = sem("silu_done")
        z_ready = sem("z_ready")
        down_done = sem("w2_product")
        y_a = sem("y_by_scalar")
        y_v = sem("y_by_vector")
        y_out = [sem(f"y_out{s}") for s in range(2)]
        step_v = sem("vector_step")
        step_a = sem("scalar_step")
        step_o = sem("overflow_vector_step")
        yg_in = [sem(f"yg_in{s}") for s in range(TT)]
        res_ready = sem("residual_ready")
        out_ready = sem("out_ready")
        out_sent = [sem(f"out_sent{t}") for t in range(TT)]
        o_landed = [sem(f"overflow_w{n}") for n in range(3)]
        o_onehot = sem("overflow_onehots")
        o_table = sem("overflow_table")
        o_list = sem("overflow_lists")
        o_idx = sem("overflow_idx")
        o_xg_in = sem("overflow_xg_in")
        o_trans = sem("overflow_transposed")
        o_xgT = sem("overflow_xgT")
        o_prod = sem("overflow_product")
        o_silu = sem("overflow_silu")
        o_z = sem("overflow_z")
        o_down = sem("overflow_down")
        o_y = sem("overflow_y")
        o_yout = sem("overflow_y_out")
        o_end = sem("overflow_expert_end")
        o_slots = sem("overflow_slots")
        o_yg_in = [sem(f"overflow_yg_in{t}") for t in range(TT)]
        o_added = sem("overflow_added")

        y_rows = y_dram.rearrange("(e r) d -> e r d", e=NE)
        oy_rows = oy_dram.rearrange("(e r) d -> e r d", e=NE)
        norm_junk = hg[:, CW:CW + D]
        o_junk = hg[:, 0:D]
        oslot_f, oslot_u, over_w = slot_f, oh_u[:, 0:TT * 2].rearrange("p (t k) -> p t k", t=TT), \
            oh[:, TT * 2:TT * 4].rearrange("p (t k) -> p t k", t=TT)

        block = ctx.enter_context(nc.Block())

        def wait_tile(eng, name):
            eng.wait_ge(tile_done, N_OF[name] + 1)

        def wait_read(eng, name):
            n = N_OF[name]
            eng.wait_ge(bank_free[n % BANKS], n // BANKS + 1)

        def last_tile(chunk):
            kind, half = chunk
            if kind == "ada":
                return chunk
            return ("wo", TT - 1, 1) if kind == "wo" else (kind, CT * half + CT - 1)

        def chunk_src(kind, half):
            if kind == "ada":
                return ada_v[:, :, CW * half:CW * (half + 1)]
            if kind in U_COL:
                a = U_COL[kind] + CW * half
                return win_v[:, :, a:a + CW]
            src = {"ya": wco_v, "yb": wro_v, "wo": wo_v}[kind]
            return src[:, :, CW * half:CW * (half + 1)]

        def slot_k(n):
            return ring[:, n % SLOTS, :].rearrange("p (k n) -> p k n", k=KD)

        def moe_slot(q):
            return (N1 + q) % SLOTS

        def moe_landed(i, q):
            return 16 * (i + (N1 + q) // SLOTS + 1)

        @block.sync
        def _(eng):
            for n, (kind, half) in enumerate(chunks):
                if n >= SLOTS:
                    wait_tile(eng, last_tile(chunks[n - SLOTS]))
                eng.dma_start(slot_k(n), chunk_src(kind, half)).then_inc(landed[n % SLOTS], 16)

            def load_pair(i, first):
                for s in range(2):
                    for m, (src, used) in enumerate(((w1_v, up_done), (w3_v, gate_done), (w2_v, down_done))):
                        q = 3 * s + m
                        if first:
                            wait_tile(eng, last_tile(chunks[N1 - SLOTS + q]))
                        else:
                            eng.wait_ge(used, i * 2 + (s - 1))
                        dst = ring[:, moe_slot(q), :]
                        part = src[i * 2 + s]
                        if m == 2:
                            dst = dst.rearrange("p (j n) -> p j n", j=JF)
                        eng.dma_start(dst, part).then_inc(landed[moe_slot(q)], 16)

            load_pair(0, True)
            with eng.Fori(1, PAIRS) as i:
                load_pair(i, False)
            eng.wait_ge(flag_ready, 1)
            most = eng.value_load(flag[0:1, 0:1], min_val=0, max_val=T)
            with eng.If(most > CAP):
                with eng.Fori(0, NE) as e:
                    eng.wait_ge(o_end, e + 1)
                    eng.dma_start(ring[:, 0, :], w1_v[e, :, :]).then_inc(o_landed[0], 16)
                    eng.dma_start(ring[:, 1, :], w3_v[e, :, :]).then_inc(o_landed[1], 16)
                    eng.dma_start(ring[:, 2, :].rearrange("p (j n) -> p j n", j=JF),
                                  w2_v[e, :, :, :]).then_inc(o_landed[2], 16)

        @block.gpsimd
        def _(eng):
            eng.memset(ident[:, :], 0.0).then_inc(consts, 1)
            eng.memset(ones[:, :], 1.0).then_inc(consts, 1)
            eng.wait_ge(consts, 2)
            eng.affine_select(out=ident[:, :], in_=ident[:, :], compare_op=ALU.not_equal, fill=1.0,
                              base=0, pattern=[[-1, P]], channel_multiplier=1).then_inc(consts, 1)
            eng.affine_select(out=before[:, :], in_=ones[:, :], compare_op=ALU.is_gt, fill=0.0,
                              base=0, pattern=[[1, P]], channel_multiplier=-1).then_inc(consts, 1)
            eng.iota(iota[:, :], pattern=[[1, T]], base=0, channel_multiplier=0,
                     allow_small_or_imprecise_dtypes=True).then_inc(consts, 1)
            eng.iota(tok[:, :], pattern=[[P, TT]], base=0, channel_multiplier=1,
                     allow_small_or_imprecise_dtypes=True).then_inc(consts, 1)

            def gather(e, s):
                eng.tensor_copy(idx[s][:, :], lists[:, bass.ds(e, 1)]).then_inc(idx_ready, 1)
                eng.wait_ge(idx_ready, e + 1)
                eng.sem_inc(gathers_begun, 1)
                eng.indirect_dma_start(out=xg[0:CAP, s, :], out_offset=None, in_=h2_dram[:, :],
                                       in_offset=bass.IndirectOffsetOnAxis(ap=idx[s][:, 0:1], axis=0),
                                       ).then_inc(xg_in[s], 16)

            wait_read(eng, ("list",))
            for t in range(TT):
                eng.wait_ge(h2_out[t], 16)
            for s in range(2):
                gather(s, s)
            with eng.Fori(1, PAIRS) as i:
                for s in range(2):
                    eng.wait_ge(xg_used, i * 2 + (s - 1))
                    gather(i * 2 + s, s)

            eng.wait_ge(flag_ready, 1)
            most = eng.value_load(flag[0:1, 0:1], min_val=0, max_val=T)
            with eng.If(most > CAP):
                eng.wait_ge(o_list, 1)
                with eng.Fori(0, NE) as e:
                    eng.wait_ge(o_end, e + 1)
                    for b in range(OB):
                        eng.tensor_copy(oidx[b][:, :], olist[:, b, bass.ds(e, 1)]).then_inc(o_idx, 1)
                    eng.wait_ge(o_idx, e * OB + OB)
                    eng.sem_inc(gathers_begun, 1)
                    for b in range(OB):
                        eng.indirect_dma_start(
                            out=oxg[0:OC, b, :], out_offset=None, in_=h2_dram[:, :],
                            in_offset=bass.IndirectOffsetOnAxis(ap=oidx[b][:, 0:1], axis=0),
                        ).then_inc(o_xg_in, 16)
                eng.wait_ge(o_yout, 16 * NE * OB)
                eng.wait_ge(o_slots, 1)
                for t in range(TT):
                    if t >= 2:
                        eng.wait_ge(o_added, t - 1)
                    for k in range(2):
                        eng.indirect_dma_start(
                            out=yg[:, t % 2, k, :], out_offset=None, in_=oy_dram[:, :],
                            in_offset=bass.IndirectOffsetOnAxis(ap=oslot_u[:, t, k:k + 1], axis=0),
                        ).then_inc(o_yg_in[t], 16)
                eng.wait_ge(o_added, TT)
            eng.wait_ge(slots_ready, TT)
            for s in range(2):
                eng.wait_ge(y_out[s], 16 * PAIRS)
            for t in range(TT):
                if t >= 2:
                    eng.wait_ge(res_ready, t - 1)
                for k in range(2):
                    eng.indirect_dma_start(
                        out=yg[:, t % 2, k, :], out_offset=None, in_=y_dram[:, :],
                        in_offset=bass.IndirectOffsetOnAxis(ap=slot_u[:, t, k:k + 1], axis=0),
                    ).then_inc(yg_in[t], 16)

        @block.tensor
        def _(eng):
            def open_tile(name):
                n = N_OF[name]
                if n >= BANKS:
                    eng.wait_ge(bank_free[n % BANKS], n // BANKS)
                return bank[n % BANKS]

            def wait_chunk(n):
                eng.wait_ge(landed[n % SLOTS], 16 * (n // SLOTS + 1))

            def transpose_params(j, rows):
                ps = open_tile(("par", j))
                eng.wait_ge(params_in[j], 16 * (7 if j == 0 else 6))
                eng.transpose(ps[:, 0:rows], par_rows[0:rows, j, :], ident[0:rows, 0:rows])\
                    .then_inc(tile_done, 1)

            def transpose_x(k):
                ps = open_tile(("xT", k))
                for t in range(TT):
                    mm = eng.transpose(ps[:, t * P:(t + 1) * P], xs[:, t, k * P:(k + 1) * P], ident[:, :])
                mm.then_inc(tile_done, 1)

            def ada(j):
                ps = open_tile(("ada", j))
                n = C_OF[("ada", j)]
                wait_chunk(n)
                for m in range(CT):
                    for k in range(KD):
                        mm = eng.matmul(ps[:, 2 * m:2 * m + 2], slot_k(n)[:, k, m * P:(m + 1) * P],
                                        cvec[:, k, :], start=(k == 0), stop=(k == KD - 1))
                mm.then_inc(tile_done, 1)

            def project(kind, half, src, ready=None):
                n = C_OF[(kind, half)]
                wait_chunk(n)
                for m in range(CT):
                    ps = open_tile((kind, CT * half + m))
                    for k in range(KD):
                        if ready is not None and m == 0:
                            eng.wait_ge(ready, k + 1)
                        mm = eng.matmul(ps[:, 0:T], slot_k(n)[:, k, m * P:(m + 1) * P], src[:, k, :],
                                        start=(k == 0), stop=(k == KD - 1))
                    mm.then_inc(tile_done, 1)

            def gates(b):
                for h in (2 * b, 2 * b + 1):
                    eng.wait_ge(xc_ready, h + 1)
                    for d in range(2):
                        for x in range(2):
                            ps = open_tile(("gate", h, d, x))
                            eng.matmul(ps[:, 0:TG], gw[:, x, d, h, :], xc[:, h, :],
                                       start=True, stop=True).then_inc(tile_done, 1)

            eng.wait_ge(consts, 6)
            transpose_params(0, NPA)
            transpose_params(1, NPAR - NPA)
            eng.wait_ge(xs_ready, TT)
            for k in range(KD):
                transpose_x(k)
            eng.wait_ge(cvec_ready, 1)
            for j in range(4):
                ada(j)
            project("xr", 0, hT, h_ready)
            project("xr", 1, hT)
            eng.wait_ge(gate_w_in, 64)
            gates(0)
            project("c", 0, hT)
            gates(1)
            project("v", 0, hT)
            gates(2)
            project("g", 0, hT)
            gates(3)
            for kind, half in (("b", 0), ("c", 1), ("v", 1), ("b", 1), ("g", 1), ("ma", 0), ("ma", 1),
                               ("mb", 0), ("mb", 1)):
                project(kind, half, hT)
            for j in range(4, 12):
                ada(j)
            ps = open_tile(("rows",))
            eng.wait_ge(rowsrc_ready, 1)
            eng.transpose(ps[0:64, 0:P], rowsrc[:, :, :].rearrange("p v k -> p (v k)"), ident[:, :])\
                .then_inc(tile_done, 1)
            ps = open_tile(("state",))
            eng.wait_ge(batch_done, 4)
            eng.transpose(ps[0:16, 0:P], stc[:, :], ident[:, :]).then_inc(tile_done, 1)
            for k in range(KD):
                wait_read(eng, ("b", k))
            project("ya", 0, ya_in)
            project("ya", 1, ya_in)
            eng.wait_ge(hg_ready, KD)
            project("yb", 0, hs)
            project("yb", 1, hs)

            def out_rows(t):
                for half in range(2):
                    ps = open_tile(("wo", t, half))
                    n = C_OF[("wo", half)]
                    wait_chunk(n)
                    for k in range(KD):
                        if t == 0 and half == 0:
                            eng.wait_ge(merged_ready, k + 1)
                        mm = eng.matmul(ps[:, :], SA[:, k, t * P:(t + 1) * P], slot_k(n)[:, k, :],
                                        start=(k == 0), stop=(k == KD - 1))
                    mm.then_inc(tile_done, 1)

            def route(t):
                for half in range(2):
                    ps = open_tile(("h2T", t, half))
                    if half == 0:
                        eng.wait_ge(h2_ready, t + 1)
                    for m in range(4):
                        k = 4 * half + m
                        mm = eng.transpose(ps[:, m * P:(m + 1) * P], h2[:, t % 2, k * P:(k + 1) * P],
                                           ident[:, :])
                    mm.then_inc(tile_done, 1)
                ps = open_tile(("route", t))
                eng.wait_ge(router_in, 32)
                wait_read(eng, ("h2T", t, 0))
                wait_read(eng, ("h2T", t, 1))
                for k in range(KD):
                    mm = eng.matmul(ps[:, 0:NG + NE], h2T[:, k, :], wr[:, k, :],
                                    start=(k == 0), stop=(k == KD - 1))
                mm.then_inc(tile_done, 1)

            for t in range(TT):
                out_rows(t)
                if t >= 1:
                    route(t - 1)
            route(TT - 1)
            for t in range(TT):
                ps = open_tile(("rank", t))
                eng.wait_ge(both_ready, t + 1)
                for u in range(t):
                    eng.matmul(ps[:, 0:NE], ones[:, :], both[:, u, :], start=(u == 0), stop=False)
                eng.matmul(ps[:, 0:NE], before[:, :], both[:, t, :], start=(t == 0), stop=True)\
                    .then_inc(tile_done, 1)
            ps = open_tile(("count",))
            for t in range(TT):
                mm = eng.matmul(ps[:, 0:NE], ones[:, :], both[:, t, :], start=(t == 0), stop=(t == TT - 1))
            mm.then_inc(tile_done, 1)
            ps = open_tile(("list",))
            eng.wait_ge(onehots_ready, TT)
            for t in range(TT):
                for k in range(2):
                    mm = eng.matmul(ps[0:CAP, 0:NE], rank_oh[:, t, k, :], tok_oh[:, t, k, :],
                                    start=(t == 0 and k == 0), stop=(t == TT - 1 and k == 1))
            mm.then_inc(tile_done, 1)

            for b in range(BANKS):
                uses = (len(stream) - b + BANKS - 1) // BANKS
                eng.wait_ge(bank_free[b], uses)

            def transpose_rows(e, s, land):
                eng.wait_ge(xg_in[s], land)
                rows = xg[0:CAP, s, :].rearrange("t (p k) -> t k p", k=KD)
                for k in range(KD):
                    b, m = k // 4, k % 4
                    mm = eng.transpose(bank[b][:, m * CAP:(m + 1) * CAP], rows[:, k, :],
                                       ident[0:CAP, 0:CAP])
                mm.then_inc(xg_used, 1)

            def expert(i, s, first, last):
                e = i * 2 + s
                eng.wait_ge(xgT_a, e + 1)
                eng.wait_ge(xgT_v, e + 1)
                for m, (b, done) in enumerate(((2, up_done), (3, gate_done))):
                    q = 3 * s + m
                    w = ring[:, moe_slot(q), :].rearrange("p (k n) -> p k n", k=KD)
                    eng.wait_ge(landed[moe_slot(q)], moe_landed(i, q))
                    for j in range(JF):
                        for k in range(KD):
                            mm = eng.matmul(bank[b][:, j * CAP:(j + 1) * CAP],
                                            w[:, k, j * P:(j + 1) * P], xgT[:, s, k, :],
                                            start=(k == 0), stop=(k == KD - 1))
                    mm.then_inc(done, 1)
                if not last:
                    transpose_rows(e + 1, 1 - s, 16 * (i + s + 1))
                q = 3 * s + 2
                w = ring[:, moe_slot(q), :].rearrange("p (j n) -> p j n", j=JF)
                eng.wait_ge(landed[moe_slot(q)], moe_landed(i, q))
                eng.wait_ge(z_ready, e + 1)
                if not first:
                    eng.wait_ge(y_a, e)
                    eng.wait_ge(y_v, e)
                for half in range(2):
                    for j in range(JF):
                        mm = eng.matmul(bank[4 + half][0:CAP, :], z[:, s, j * CAP:(j + 1) * CAP],
                                        w[:, j, half * 512:(half + 1) * 512],
                                        start=(j == 0), stop=(j == JF - 1))
                mm.then_inc(down_done, 1)

            transpose_rows(0, 0, 16)
            for s in range(2):
                expert(0, s, s == 0, False)
            with eng.Fori(1, PAIRS - 1) as i:
                for s in range(2):
                    expert(i, s, False, False)
            for s in range(2):
                expert(PAIRS - 1, s, False, s == 1)

            eng.wait_ge(flag_ready, 1)
            most = eng.value_load(flag[0:1, 0:1], min_val=0, max_val=T)
            with eng.If(most > CAP):
                eng.wait_ge(y_a, NE)
                eng.wait_ge(y_v, NE)
                for b in range(OB):
                    for t in range(TT):
                        for k in range(2):
                            eng.wait_ge(o_onehot, (b * TT + t) * 2 + k + 1)
                            mm = eng.matmul(bank[0][0:OC, b * NE:(b + 1) * NE],
                                            orank[:, b * OC:(b + 1) * OC], tok_oh[:, t, k, :],
                                            start=(t == 0 and k == 0), stop=(t == TT - 1 and k == 1))
                            mm.then_inc(o_table, 1)
                eng.wait_ge(o_list, 1)
                with eng.Fori(0, NE) as e:
                    eng.wait_ge(o_xg_in, e * (16 * OB) + 16 * OB)
                    for b in range(OB):
                        rows = oxg[0:OC, b, :].rearrange("t (p k) -> t k p", k=KD)
                        eng.wait_ge(o_xgT, e * (2 * OB) + 2 * b + 1)
                        for k in range(KD):
                            mm = eng.transpose(bank[k // 4][:, (k % 4) * OC:(k % 4 + 1) * OC],
                                               rows[:, k, :], ident[0:OC, 0:OC])
                        mm.then_inc(o_trans, 1)
                    eng.wait_ge(o_xgT, e * (2 * OB) + 2 * OB + 1)
                    eng.wait_ge(o_landed[0], e * 16 + 16)
                    eng.wait_ge(o_landed[1], e * 16 + 16)
                    for j in range(JF):
                        eng.wait_ge(o_z, e * JF + j + 1)
                        for m in range(2):
                            w = ring[:, m, :].rearrange("p (k n) -> p k n", k=KD)
                            for k in range(KD):
                                mm = eng.matmul(bank[2 + m][:, 0:OT], w[:, k, j * P:(j + 1) * P],
                                                oxgT[:, k, :], start=(k == 0), stop=(k == KD - 1))
                            mm.then_inc(o_prod, 1)
                    eng.wait_ge(o_z, e * JF + JF + 1)
                    eng.wait_ge(o_landed[2], e * 16 + 16)
                    w = ring[:, 2, :].rearrange("p (j n) -> p j n", j=JF)
                    for b in range(OB):
                        eng.wait_ge(o_y, e * (2 * OB) + 2 * b + 1)
                        for half in range(2):
                            for j in range(JF):
                                mm = eng.matmul(bank[4 + half][0:OC, :], oz[:, j, b * OC:(b + 1) * OC],
                                                w[:, j, half * 512:(half + 1) * 512],
                                                start=(j == 0), stop=(j == JF - 1))
                        mm.then_inc(o_down, 1)

        @block.scalar
        def _(eng):
            steps = [0]

            def then(ins):
                ins.then_inc(step_a, 1)
                steps[0] += 1
                eng.wait_ge(step_a, steps[0])

            def tile(name):
                n = N_OF[name]
                eng.wait_ge(tile_done, n + 1)
                return bank[n % BANKS], bank_free[n % BANKS]

            def rows_of(dst, src, sem_):
                eng.dma_start(dst, src).then_inc(sem_, 16)

            a, b = par_rows[:, 0, :], par_rows[:, 1, :]
            rows_of(a[BADA:48, :], b_ada[0].rearrange("(r p) -> r p", p=P), params_in[0])
            rows_of(a[CCTX:CCTX + KD, :], c_ctx.rearrange("(r p) -> r p", p=P), params_in[0])
            rows_of(a[CSMP:CSMP + KD, :], c[0].rearrange("(r p) -> r p", p=P), params_in[0])
            rows_of(x_rows[:, 0, :], x_prompt[0], x_in)
            rows_of(x_rows[:, 1:TT, :], x_sample[0].rearrange("(t p) d -> p t d", p=P), x_in)
            rows_of(a[GN1:GN1 + KD, :], g_norm1[0].rearrange("(r p) -> r p", p=P), params_in[0])
            rows_of(a[GN2:GN2 + KD, :], g_norm2[0].rearrange("(r p) -> r p", p=P), params_in[0])
            for d in range(2):
                rows_of(a[STF + KD * d:STF + KD * (d + 1), :],
                        state_rnn[0, 0, d].rearrange("(r p) -> r p", p=P), params_in[0])
            o = CVW
            for src in (conv_w[0], rnn_conv_w[0]):
                n = src.shape[0] * KD
                rows_of(b[o - CVW:o - CVW + n, :], src.rearrange("w (r p) -> (w r) p", p=P), params_in[1])
                o += n
            rows_of(b[RCB - CVW:RCB - CVW + KD, :], rnn_conv_b[0].rearrange("(r p) -> r p", p=P), params_in[1])
            for at, src in ((BGA, b_gate_a), (BGX, b_gate_x), (LAM, lam)):
                rows_of(b[at - CVW:at - CVW + 2 * KD, :], src[0].rearrange("d (r p) -> (d r) p", p=P),
                        params_in[1])
            for x, src in enumerate((w_gate_a, w_gate_x)):
                for d in range(2):
                    rows_of(gw[:, x, d, :, :], src[0, d].rearrange("h i j -> i h j"), gate_w_in)
            rows_of(wr[:, :, 0:NG], w_router_group[0].rearrange("(k p) n -> p k n", p=P), router_in)
            rows_of(wr[:, :, NG:], w_router_expert[0].rearrange("(k p) n -> p k n", p=P), router_in)
            rows_of(br[:, 0:NG], b_router_group[0].partition_broadcast(P), bias_in)
            rows_of(br[:, NG:], b_router_expert[0].partition_broadcast(P), bias_in)

            eng.wait_ge(x_in, 32)
            for t in range(TT):
                if t:
                    eng.wait_ge(ssq_ready, t)
                eng.activation(junk, x_rows[:, t, :], ACT.Square, accum_out=stat[:, 0, 0, t:t + 1])\
                    .then_inc(ssq_ready, 1)
            eng.wait_ge(mean_ready, 1)
            eng.activation(stat[:, 0, 2, :], stat[:, 0, 1, :], ACT.Sqrt).then_inc(rms_ready, 1)
            wait_read(eng, ("par", 0))
            wait_read(eng, ("par", 1))
            then(eng.activation(sp[:, 0, :], pT[:, LAM:NPAR], ACT.Abs))
            eng.activation(sp[:, 1, :], sp[:, 0, :], ACT.Exp, scale=-1.0).then_inc(lam_exp, 1)
            eng.activation(cvec[:, :, :], pT[:, CCTX:CCTX + 2 * KD].rearrange("p (c k) -> p k c", c=2),
                           ACT.Silu).then_inc(cvec_ready, 1)
            for k in range(KD):
                ps, free = tile(("xT", k))
                eng.activation(hT[:, k, :], ps[:, 0:T], ACT.Copy).then_inc(free, 1)

            eng.wait_ge(pads_zero, 2)
            for h in range(KD):
                ps, free = tile(("xr", h))
                if h >= 2:
                    eng.wait_ge(xc_ready, h - 1)
                eng.activation(xrp[:, h % 2, 2:2 + NP_TOK], ps[:, 0:NP_TOK], ACT.Copy)
                eng.activation(xrp[:, h % 2, 2 + S0:2 + TG], ps[:, NP_TOK:T], ACT.Copy)\
                    .then_inc(free, 1)

            def gate_sigmoids(b):
                if b >= 1:
                    eng.wait_ge(batch_done, b)
                for h in (2 * b, 2 * b + 1):
                    for d in range(2):
                        for x, (dst, bias) in enumerate(((r_b, BGA), (i_b, BGX))):
                            ps, free = tile(("gate", h, d, x))
                            col = bias + d * KD + h
                            eng.activation(dst[:, d, h % 2, :], ps[:, 0:TG], ACT.Sigmoid,
                                           bias=pT[:, col:col + 1]).then_inc(free, 1)

            def gate_exps(b):
                for h in (2 * b, 2 * b + 1):
                    for d in range(2):
                        for x in range(2):
                            n = N_OF[("gate", h, d, x)]
                            eng.wait_ge(bank_free[n % BANKS], n // BANKS + 1)
                if b == 0:
                    eng.wait_ge(rate_ready, 1)
                for h in (2 * b, 2 * b + 1):
                    for d in range(2):
                        col = d * KD + h
                        eng.activation(a_b[:, d, h % 2, :], r_b[:, d, h % 2, :], ACT.Exp,
                                       scale=rate[:, 0, col:col + 1]).then_inc(exp_done, 1)
                for h in (2 * b, 2 * b + 1):
                    for d in range(2):
                        col = d * KD + h
                        eng.activation(r_b[:, d, h % 2, :], r_b[:, d, h % 2, :], ACT.Tanh,
                                       scale=rate[:, 1, col:col + 1]).then_inc(exp_done, 1)

            def gate_roots(b):
                eng.wait_ge(q_ready, b + 1)
                eng.activation(r_f, r_f, ACT.Sqrt).then_inc(root_done, 1)

            def copy_c(half):
                for m in range(CT):
                    ps, free = tile(("c", CT * half + m))
                    if half:
                        eng.wait_ge(conv_done, m + 1)
                    eng.activation(cpad[:, m, 1:1 + NP_TOK], ps[:, 0:NP_TOK], ACT.Copy)
                    eng.activation(cpad[:, m, 2 + NP_TOK:].rearrange("p (r q) -> p r q", r=ROWS)[:, :, 0:GRID_W],
                                   ps[:, NP_TOK:T].rearrange("p (r q) -> p r q", r=ROWS), ACT.Copy)\
                        .then_inc(free, 1)

            def gelus(half):
                for m in range(CT):
                    k = CT * half + m
                    ps, free = tile(("g", k))
                    if k >= 2:
                        eng.wait_ge(hg_ready, k - 1)
                    else:
                        eng.wait_ge(xc_ready, KD)
                    eng.activation(gtmp[:, k % 2, :], ps[:, 0:T], ACT.Gelu_apprx_tanh).then_inc(free, 1)

            gate_sigmoids(0)
            gate_exps(0)
            copy_c(0)
            gate_roots(0)
            gate_sigmoids(1)
            gate_exps(1)
            gate_roots(1)
            gate_sigmoids(2)
            gate_exps(2)
            gate_roots(2)
            gelus(0)
            gate_sigmoids(3)
            gate_exps(3)
            gate_roots(3)
            copy_c(1)
            gelus(1)
            eng.wait_ge(batch_done, 4)
            for kind, dst in (("ma", SA), ("mb", SB)):
                for k in range(KD):
                    ps, free = tile((kind, k))
                    eng.activation(dst[:, k, :], ps[:, 0:T], ACT.Sigmoid).then_inc(free, 1)

            ps, free = tile(("rows",))
            eng.activation(rows_sb, ps[0:64, 0:P], ACT.Copy).then_inc(free, 1)
            wait_read(eng, ("rows",))
            eng.dma_start(rowvec.rearrange("v (k p) -> (v k) p", p=P), rows_sb).then_inc(rows_out, 16)
            ps, free = tile(("state",))
            eng.activation(st_sb, ps[0:16, 0:P], ACT.Copy).then_inc(free, 1)
            wait_read(eng, ("state",))
            eng.dma_start(state_new[0, 0].rearrange("d (k p) -> (d k) p", p=P), st_sb)\
                .then_inc(state_out, 16)
            eng.wait_ge(rows_out, 16)
            for v, dst in enumerate((G1, A2, B2, G2)):
                for cnd in range(2):
                    eng.dma_start(dst[:, cnd, :], rowvec[2 * v + cnd].partition_broadcast(P))\
                        .then_inc(bcast_in, 16)
            eng.dma_start(gfin, g_final.partition_broadcast(P)).then_inc(bcast_in, 16)

            def route_copies(t):
                for half in range(2):
                    ps, free = tile(("h2T", t, half))
                    if half == 0 and t >= 1:
                        wait_tile(eng, ("route", t - 1))
                    eng.activation(h2T[:, 4 * half:4 * half + 4, :].rearrange("p k t -> p (k t)"),
                                   ps[:, :], ACT.Copy).then_inc(free, 1)

            def norm_rows(t):
                eng.wait_ge(x1_ready, t + 1)
                eng.activation(norm_junk, x_rows[:, t, :], ACT.Square, accum_out=stat[:, 1, 0, t:t + 1])\
                    .then_inc(ssq_ready, 1)
                eng.wait_ge(mean_ready, t + 2)
                eng.activation(stat[:, 1, 2, t:t + 1], stat[:, 1, 1, t:t + 1], ACT.Sqrt)\
                    .then_inc(rms_ready, 1)
                eng.wait_ge(h2_ready, t + 1)
                eng.dma_start(h2_dram[t * P:(t + 1) * P, :], h2[:, t % 2, :]).then_inc(h2_out[t], 16)

            def top_exps(t):
                eng.wait_ge(tops_ready, t + 1)
                eng.activation(rt[:, t, 0:NG], lg[:, t, 0:NG], ACT.Exp, bias=rt[:, t, 32:33],
                               accum_out=rt[:, t, 33:34])
                eng.activation(rt[:, t, 34:35], rt[:, t, 35:36], ACT.Exp).then_inc(texp_ready, 1)

            for t in range(TT):
                norm_rows(t)
                if t >= 1:
                    route_copies(t - 1)
                    top_exps(t - 1)
            route_copies(TT - 1)
            top_exps(TT - 1)

            def transposed(e, s):
                eng.wait_ge(xg_used, e + 1)
                eng.activation(xgT[:, s, 0:4, :].rearrange("p k t -> p (k t)"), bank[0][:, 0:4 * CAP],
                               ACT.Copy).then_inc(xgT_a, 1)

            def expert_pair(i, first, last):
                for s in range(2):
                    e = i * 2 + s
                    eng.wait_ge(up_done, e + 1)
                    eng.activation(sil, bank[2][:, 0:JF * CAP], ACT.Silu).then_inc(silu_done, 1)
                    if not (last and s == 1):
                        transposed(e + 1, 1 - s)
                    eng.wait_ge(down_done, e + 1)
                    if not first:
                        eng.wait_ge(y_out[s], i * 16)
                    eng.activation(y_sb[0:CAP, s, 0:512], bank[4][0:CAP, :], ACT.Copy).then_inc(y_a, 1)
                    eng.wait_ge(y_a, e + 1)
                    eng.wait_ge(y_v, e + 1)
                    eng.dma_start(y_rows[e, 0:CAP, :], y_sb[0:CAP, s, :]).then_inc(y_out[s], 16)

            transposed(0, 0)
            expert_pair(0, True, False)
            with eng.Fori(1, PAIRS - 1) as i:
                expert_pair(i, False, False)
            expert_pair(PAIRS - 1, False, True)

            eng.wait_ge(flag_ready, 1)
            most = eng.value_load(flag[0:1, 0:1], min_val=0, max_val=T)
            with eng.If(most > CAP):
                with eng.Fori(0, NE) as e:
                    for b in range(OB):
                        eng.wait_ge(o_trans, e * OB + b + 1)
                        eng.activation(oxgT[:, 0:4, b * OC:(b + 1) * OC],
                                       bank[0][:, 0:4 * OC].rearrange("p (k t) -> p k t", k=4),
                                       ACT.Copy).then_inc(o_xgT, 1)
                    for j in range(JF):
                        eng.wait_ge(o_prod, e * (2 * JF) + 2 * j + 1)
                        eng.wait_ge(o_z, e * JF + j + 1)
                        eng.activation(osil, bank[2][:, 0:OT], ACT.Silu).then_inc(o_silu, 1)
                    for b in range(OB):
                        eng.wait_ge(o_down, e * OB + b + 1)
                        eng.activation(oy[0:OC, 0:512], bank[4][0:OC, :], ACT.Copy).then_inc(o_y, 1)
                        eng.wait_ge(o_y, e * (2 * OB) + 2 * b + 3)
                        eng.dma_start(oy_rows[e, b * OC:(b + 1) * OC, :], oy[0:OC, :]).then_inc(o_yout, 16)
                        eng.wait_ge(o_yout, e * (16 * OB) + 16 * b + 16)
                    eng.sem_inc(o_end, 1)

            for t in range(TT):
                eng.wait_ge(res_ready, t + 1)
                eng.activation(o_junk, x_rows[:, t, :], ACT.Square, accum_out=stat[:, 2, 0, t:t + 1])\
                    .then_inc(ssq_ready, 1)
                eng.wait_ge(mean_ready, TT + t + 2)
                eng.activation(stat[:, 2, 2, t:t + 1], stat[:, 2, 1, t:t + 1], ACT.Sqrt)\
                    .then_inc(rms_ready, 1)
                eng.wait_ge(out_ready, t + 1)
                dst = y_prompt[0] if t == 0 else y_sample[0, (t - 1) * P:t * P, :]
                eng.dma_start(dst, o_rows[:, t % 2, :]).then_inc(out_sent[t], 16)
            for t in range(TT):
                eng.wait_ge(out_sent[t], 16)
            eng.wait_ge(state_out, 16)

        @block.vector
        def _(eng):
            steps = [0]

            def then(ins):
                ins.then_inc(step_v, 1)
                steps[0] += 1
                eng.wait_ge(step_v, steps[0])

            def tile(name):
                n = N_OF[name]
                eng.wait_ge(tile_done, n + 1)
                return bank[n % BANKS], bank_free[n % BANKS]

            eng.memset(xrp[:, :, :], 0.0).then_inc(pads_zero, 1)
            eng.memset(cpad, 0.0).then_inc(pads_zero, 1)
            eng.memset(lg[:, :, :], -3.0e38)

            def mean_square(norm, sl):
                eng.tensor_scalar(stat[:, norm, 1, sl], stat[:, norm, 0, sl], 1.0 / D, EPS,
                                  ALU.mult, ALU.add).then_inc(mean_ready, 1)

            eng.wait_ge(ssq_ready, TT)
            mean_square(0, slice(0, TT))
            eng.wait_ge(rms_ready, 1)
            then(eng.reciprocal(stat[:, 0, 0, :], stat[:, 0, 2, :]))
            for t in range(TT):
                eng.tensor_scalar(xs[:, t, :], x_rows[:, t, :], stat[:, 0, 0, t:t + 1], None, ALU.mult)\
                    .then_inc(xs_ready, 1)
            for j, (a, b) in enumerate(((0, NPA), (NPA, NPAR))):
                ps, free = tile(("par", j))
                eng.tensor_copy(pT[:, a:b], ps[:, 0:b - a]).then_inc(free, 1)
                wait_read(eng, ("par", j))

            eng.wait_ge(lam_exp, 1)
            then(eng.tensor_scalar(sp[:, 2, :], sp[:, 1, :], 2.0, None, ALU.add))
            then(eng.reciprocal(sp[:, 3, :], sp[:, 2, :]))
            then(eng.tensor_tensor(sp[:, 2, :], sp[:, 1, :], sp[:, 3, :], ALU.mult))
            then(eng.tensor_tensor(sp[:, 3, :], sp[:, 2, :], sp[:, 2, :], ALU.mult))
            then(eng.tensor_scalar(sp[:, 4, :], sp[:, 3, :], 1.0 / 17, None, ALU.mult))
            for odd in (15, 13, 11, 9, 7, 5, 3):
                then(eng.scalar_tensor_tensor(out=sp[:, 4, :], in0=sp[:, 4, :], scalar=1.0 / odd,
                                              in1=sp[:, 3, :], op0=ALU.add, op1=ALU.mult))
            then(eng.scalar_tensor_tensor(out=sp[:, 4, :], in0=sp[:, 4, :], scalar=1.0,
                                          in1=sp[:, 2, :], op0=ALU.add, op1=ALU.mult))
            then(eng.tensor_scalar(sp[:, 5, :], pT[:, LAM:NPAR], -1.0, 0.0, ALU.mult, ALU.max))
            then(eng.scalar_tensor_tensor(out=sp[:, 5, :], in0=sp[:, 4, :], scalar=2.0,
                                          in1=sp[:, 5, :], op0=ALU.mult, op1=ALU.add))
            eng.tensor_scalar(rate[:, 0, :], sp[:, 5, :], -RG_C, None, ALU.mult)
            eng.tensor_scalar(rate[:, 1, :], sp[:, 5, :], RG_C, None, ALU.mult).then_inc(rate_ready, 1)

            def ada(j):
                ps, free = tile(("ada", j))
                bias = pT[:, BADA + CT * j:BADA + CT * (j + 1)]
                for cnd in range(2):
                    last = eng.tensor_tensor(
                        mod[:, CT * j:CT * (j + 1), cnd],
                        ps[:, 0:2 * CT].rearrange("p (m c) -> p m c", c=2)[:, :, cnd], bias, ALU.add)
                last.then_inc(free, 1)
                return free, N_OF[("ada", j)] // BANKS + 1

            for j in range(4):
                free, count = ada(j)
            eng.wait_ge(free, count)
            for cnd in range(2):
                last = eng.scalar_tensor_tensor(out=A1[:, :, cnd], in0=mod[:, KD:2 * KD, cnd], scalar=1.0,
                                                in1=pT[:, GN1:GN1 + KD], op0=ALU.add, op1=ALU.mult)
            then(last)
            for k in range(KD):
                n = N_OF[("xT", k)]
                eng.wait_ge(bank_free[n % BANKS], n // BANKS + 1)
                for cnd, (a, b) in enumerate(((0, NP_TOK), (NP_TOK, T))):
                    last = eng.tensor_scalar(hT[:, k, a:b], hT[:, k, a:b], A1[:, k, cnd:cnd + 1],
                                             mod[:, k, cnd:cnd + 1], ALU.mult, ALU.add)
                last.then_inc(h_ready, 1)

            for h in range(KD):
                n = N_OF[("xr", h)]
                eng.wait_ge(bank_free[n % BANKS], n // BANKS + 1)
                src = xrp[:, h % 2, :]
                then(eng.tensor_scalar(xc[:, h, :], src[:, 0:TG], pT[:, RCW + h:RCW + h + 1],
                                       pT[:, RCB + h:RCB + h + 1], ALU.mult, ALU.add))
                for tap in range(1, 4):
                    col = RCW + tap * KD + h
                    ins = eng.scalar_tensor_tensor(out=xc[:, h, :], in0=src[:, tap:tap + TG],
                                                   scalar=pT[:, col:col + 1], in1=xc[:, h, :],
                                                   op0=ALU.mult, op1=ALU.add)
                    if tap < 3:
                        then(ins)
                ins.then_inc(xc_ready, 1)

            def gate_inputs(b):
                for h in (2 * b, 2 * b + 1):
                    for d in range(2):
                        n = N_OF[("gate", h, d, 1)]
                        eng.wait_ge(bank_free[n % BANKS], n // BANKS + 1)
                eng.wait_ge(xc_ready, KD)
                for d in range(2):
                    eng.tensor_tensor(i_b[:, d, :, :], i_b[:, d, :, :], xc[:, 2 * b:2 * b + 2, :], ALU.mult)
                eng.wait_ge(exp_done, 8 * (b + 1))
                then(eng.tensor_tensor(q_f, a_f, a_f, ALU.mult))
                eng.scalar_tensor_tensor(out=r_f, in0=q_f, scalar=1.0, in1=r_f, op0=ALU.add,
                                         op1=ALU.mult).then_inc(q_ready, 1)

            def scans(b):
                eng.wait_ge(root_done, b + 1)
                then(eng.tensor_tensor(i_f, i_f, r_f, ALU.mult))
                eng.memset(a_b[:, :, :, NP_TOK:S0], 0.0)
                then(eng.memset(i_b[:, :, :, NP_TOK:S0], 0.0))
                then(eng.tensor_copy(i_b[:, 0, :, S0 - 1], pT[:, STF + 2 * b:STF + 2 * b + 2]))
                for hh in range(2):
                    h = 2 * b + hh
                    eng.tensor_tensor_scan(r_b[:, 0, hh, :], a_b[:, 0, hh, :], i_b[:, 0, hh, :], 0.0,
                                           ALU.mult, ALU.add)
                    last = eng.tensor_tensor_scan(r_b[:, 1, hh, ::-1], a_b[:, 1, hh, ::-1],
                                                  i_b[:, 1, hh, ::-1], pT[:, STB + h:STB + h + 1],
                                                  ALU.mult, ALU.add)
                then(last)
                for a, z0, n in ((0, 0, NP_TOK), (NP_TOK, S0, NS_TOK)):
                    eng.tensor_tensor(hs[:, 2 * b:2 * b + 2, a:a + n], r_b[:, 0, :, z0:z0 + n],
                                      r_b[:, 1, :, z0:z0 + n], ALU.add)
                eng.tensor_copy(stc[:, 2 * b:2 * b + 2], r_b[:, 0, :, NP_TOK - 1])
                eng.tensor_copy(stc[:, KD + 2 * b:KD + 2 * b + 2], r_b[:, 1, :, 0]).then_inc(batch_done, 1)

            def conv_grid(half):
                for m in range(CT):
                    k = CT * half + m
                    n = N_OF[("c", k)]
                    eng.wait_ge(bank_free[n % BANKS], n // BANKS + 1)
                    ps, free = tile(("v", k))
                    src = cpad[:, m, :]
                    grid = src[:, 2 + NP_TOK:].rearrange("p (r q) -> p r q", r=ROWS)[:, :, 0:GRID_W]
                    eng.tensor_tensor(src[:, 1:1 + NP_TOK], ps[:, 0:NP_TOK], src[:, 1:1 + NP_TOK], ALU.mult)
                    eng.tensor_tensor(grid, ps[:, NP_TOK:T].rearrange("p (r q) -> p r q", r=ROWS), grid,
                                      ALU.mult).then_inc(free, 1)
                    eng.wait_ge(free, N_OF[("v", k)] // BANKS + 1)
                    if half:
                        wait_read(eng, ("b", m))
                    dst = ycv[:, m, 0:CG - 2]
                    then(eng.tensor_scalar(dst, src[:, 0:CG - 2], pT[:, CVW + k:CVW + k + 1], None, ALU.mult))
                    for tap in range(1, 3):
                        col = CVW + tap * KD + k
                        ins = eng.scalar_tensor_tensor(out=dst, in0=src[:, tap:tap + CG - 2],
                                                       scalar=pT[:, col:col + 1], in1=dst,
                                                       op0=ALU.mult, op1=ALU.add)
                        if tap < 2:
                            then(ins)
                    ins.then_inc(conv_done, 1)

            def times_b(half):
                for m in range(CT):
                    k = CT * half + m
                    eng.wait_ge(conv_done, k + 1)
                    ps, free = tile(("b", k))
                    y = ycv[:, m, :]
                    eng.tensor_tensor(ya_in[:, k, 0:NP_TOK], ps[:, 0:NP_TOK], y[:, 0:NP_TOK], ALU.mult)
                    eng.tensor_tensor(
                        ya_in[:, k, NP_TOK:T].rearrange("p (r q) -> p r q", r=ROWS),
                        ps[:, NP_TOK:T].rearrange("p (r q) -> p r q", r=ROWS),
                        y[:, 1 + NP_TOK:1 + NP_TOK + ROWS * (GRID_W + 1)]
                        .rearrange("p (r q) -> p r q", r=ROWS)[:, :, 0:GRID_W], ALU.mult)\
                        .then_inc(free, 1)

            def times_gelu(half):
                for m in range(CT):
                    k = CT * half + m
                    n = N_OF[("g", k)]
                    eng.wait_ge(bank_free[n % BANKS], n // BANKS + 1)
                    eng.wait_ge(batch_done, k // 2 + 1)
                    eng.tensor_tensor(hs[:, k, :], hs[:, k, :], gtmp[:, k % 2, :], ALU.mult)\
                        .then_inc(hg_ready, 1)

            gate_inputs(0)
            scans(0)
            gate_inputs(1)
            scans(1)
            conv_grid(0)
            gate_inputs(2)
            scans(2)
            times_gelu(0)
            gate_inputs(3)
            scans(3)
            times_b(0)
            conv_grid(1)
            times_b(1)
            times_gelu(1)

            for j in range(4, 12):
                free, count = ada(j)
                if j % 4 == 3 or j == 11:
                    eng.wait_ge(free, count)
            for cnd in range(2):
                for v, col in ((0, 2), (2, 3), (3, 5)):
                    eng.tensor_copy(rowsrc[:, 2 * v + cnd, :], mod[:, col * KD:(col + 1) * KD, cnd])
                last = eng.scalar_tensor_tensor(out=rowsrc[:, 2 + cnd, :], in0=mod[:, 4 * KD:5 * KD, cnd],
                                                scalar=1.0, in1=pT[:, GN2:GN2 + KD],
                                                op0=ALU.add, op1=ALU.mult)
            last.then_inc(rowsrc_ready, 1)

            for k in range(KD):
                ps, free = tile(("ya", k))
                n = N_OF[("ma", k)]
                eng.wait_ge(bank_free[n % BANKS], n // BANKS + 1)
                eng.tensor_tensor(SA[:, k, :], ps[:, 0:T], SA[:, k, :], ALU.mult).then_inc(free, 1)
            for k in range(KD):
                ps, free = tile(("yb", k))
                n = N_OF[("mb", k)]
                eng.wait_ge(bank_free[n % BANKS], n // BANKS + 1)
                eng.tensor_tensor(SB[:, k, :], ps[:, 0:T], SB[:, k, :], ALU.mult).then_inc(free, 1)
                n = N_OF[("yb", k)]
                eng.wait_ge(free, n // BANKS + 1)
                eng.tensor_tensor(SA[:, k, :], SA[:, k, :], SB[:, k, :], ALU.add).then_inc(merged_ready, 1)

            def residual(t):
                cnd = 0 if t == 0 else 1
                for half in range(2):
                    cols = slice(half * CW, (half + 1) * CW)
                    ps, free = tile(("wo", t, half))
                    eng.tensor_tensor(wo_tmp, ps[:, :], G1[:, cnd, cols], ALU.mult).then_inc(free, 1)
                    eng.wait_ge(free, N_OF[("wo", t, half)] // BANKS + 1)
                    ins = eng.tensor_tensor(x_rows[:, t, cols], x_rows[:, t, cols], wo_tmp, ALU.add)
                    if half == 0:
                        then(ins)
                ins.then_inc(x1_ready, 1)
                eng.wait_ge(ssq_ready, TT + t + 1)
                mean_square(1, slice(t, t + 1))

            def norm2(t):
                cnd = 0 if t == 0 else 1
                eng.wait_ge(rms_ready, t + 2)
                then(eng.reciprocal(stat[:, 1, 0, t:t + 1], stat[:, 1, 2, t:t + 1]))
                if t >= 2:
                    eng.wait_ge(h2_out[t - 2], 16)
                    eng.wait_ge(tile_done, N_OF[("h2T", t - 2, 1)] + 1)
                then(eng.scalar_tensor_tensor(out=h2[:, t % 2, :], in0=x_rows[:, t, :],
                                              scalar=stat[:, 1, 0, t:t + 1], in1=A2[:, cnd, :],
                                              op0=ALU.mult, op1=ALU.mult))
                eng.tensor_tensor(h2[:, t % 2, :], h2[:, t % 2, :], B2[:, cnd, :], ALU.add)\
                    .then_inc(h2_ready, 1)

            def choose(t):
                r, u = rt[:, t, :], rti[:, t, :]
                ps, free = tile(("route", t))
                eng.wait_ge(bias_in, 32)
                eng.tensor_tensor(lg[:, t, 0:NG], ps[:, 0:NG], br[:, 0:NG], ALU.add)
                eng.tensor_tensor(le[:, t, :], ps[:, NG:NG + NE], br[:, NG:], ALU.add).then_inc(free, 1)
                wait_read(eng, ("route", t))
                then(eng.max(r[:, 8:16], lg[:, t, :]))
                then(eng.max_index(u[:, 0:8], r[:, 8:16], lg[:, t, :]))
                then(eng.tensor_copy(r[:, 36:37], u[:, 0:1]))
                then(eng.tensor_scalar(r[:, 40:40 + NG], iota[:, 0:NG], r[:, 36:37], None, ALU.is_equal))
                then(eng.tensor_scalar(r[:, 16:24], le[:, t, 0:EG], r[:, 40:41], None, ALU.mult))
                for g in range(1, NG):
                    then(eng.scalar_tensor_tensor(out=r[:, 16:24], in0=le[:, t, g * EG:(g + 1) * EG],
                                                  scalar=r[:, 40 + g:41 + g], in1=r[:, 16:24],
                                                  op0=ALU.mult, op1=ALU.add))
                then(eng.max(r[:, 24:32], r[:, 16:24]))
                then(eng.max_index(u[:, 8:16], r[:, 24:32], r[:, 16:24]))
                eng.tensor_scalar(r[:, 32:33], r[:, 8:9], -1.0, None, ALU.mult)
                eng.tensor_tensor(r[:, 35:36], r[:, 25:26], r[:, 24:25], ALU.subtract)\
                    .then_inc(tops_ready, 1)
                eng.tensor_scalar(r[:, 37:38], r[:, 36:37], float(EG), None, ALU.mult)
                then(eng.tensor_copy(r[:, 44:46], u[:, 8:10]))
                then(eng.tensor_scalar(r[:, 46:48], r[:, 44:46], r[:, 37:38], None, ALU.add))
                for k in range(2):
                    last = eng.tensor_scalar(pick[:, t, k, :], iota[:, 0:NE], r[:, 46 + k:47 + k], None,
                                             ALU.is_equal)
                then(last)
                eng.tensor_tensor(both[:, t, :], pick[:, t, 0, :], pick[:, t, 1, :], ALU.add)\
                    .then_inc(both_ready, 1)
                eng.wait_ge(texp_ready, t + 1)
                then(eng.tensor_scalar(r[:, 48:49], r[:, 34:35], 1.0, None, ALU.add))
                then(eng.tensor_tensor(r[:, 49:50], r[:, 48:49], r[:, 33:34], ALU.mult))
                then(eng.reciprocal(wts[:, t, 0:1], r[:, 49:50]))
                eng.tensor_tensor(wts[:, t, 1:2], wts[:, t, 0:1], r[:, 34:35], ALU.mult)
                for k in range(2):
                    last = eng.tensor_scalar(tok_oh[:, t, k, :], pick[:, t, k, :], tok[:, t:t + 1], None,
                                             ALU.mult)

            def place(t):
                ps, free = tile(("rank", t))
                for k in range(2):
                    ins = eng.tensor_tensor(rank_m[:, k, :], ps[:, 0:NE], pick[:, t, k, :], ALU.mult)
                ins.then_inc(free, 1)
                wait_read(eng, ("rank", t))
                then(eng.reduce_sum(rank[:, t, :], rank_m[:, :, :], AX_X))
                for k in range(2):
                    last = eng.tensor_scalar(rank_oh[:, t, k, :], iota[:, 0:CAP], rank[:, t, k:k + 1],
                                             None, ALU.is_equal)
                last.then_inc(onehots_ready, 1)
                eng.scalar_tensor_tensor(out=main_w[:, t, :], in0=rank[:, t, :], scalar=float(CAP),
                                         in1=wts[:, t, :], op0=ALU.is_lt, op1=ALU.mult)
                then(eng.tensor_scalar(slot_f[:, t, :], rank[:, t, :], float(CAP - 1), None, ALU.min))
                then(eng.scalar_tensor_tensor(out=slot_f[:, t, :], in0=rt[:, t, 46:48], scalar=float(CAP),
                                              in1=slot_f[:, t, :], op0=ALU.mult, op1=ALU.add))
                eng.tensor_copy(slot_u[:, t, :], slot_f[:, t, :]).then_inc(slots_ready, 1)

            eng.wait_ge(bcast_in, 16 * 9)
            eng.wait_ge(consts, 6)
            for t in range(TT):
                residual(t)
                norm2(t)
                if t >= 1:
                    choose(t - 1)
            choose(TT - 1)
            for t in range(TT):
                place(t)
            ps, free = tile(("count",))
            eng.reduce_max(cmax[:, :], ps[:, 0:NE], AX_X).then_inc(free, 1)
            wait_read(eng, ("count",))
            eng.tensor_copy(flag[:, :], cmax[:, :]).then_inc(flag_ready, 1)
            ps, free = tile(("list",))
            eng.tensor_copy(lists[:, :], ps[0:CAP, 0:NE]).then_inc(free, 1)

            def transposed(e, s):
                eng.wait_ge(xg_used, e + 1)
                eng.tensor_copy(xgT[:, s, 4:8, :].rearrange("p k t -> p (k t)"), bank[1][:, 0:4 * CAP])\
                    .then_inc(xgT_v, 1)

            def expert_pair(i, first, last):
                for s in range(2):
                    e = i * 2 + s
                    eng.wait_ge(silu_done, e + 1)
                    eng.wait_ge(gate_done, e + 1)
                    eng.tensor_tensor(z[:, s, :], bank[3][:, 0:JF * CAP], sil, ALU.mult).then_inc(z_ready, 1)
                    if not (last and s == 1):
                        transposed(e + 1, 1 - s)
                    eng.wait_ge(down_done, e + 1)
                    if not first:
                        eng.wait_ge(y_out[s], i * 16)
                    eng.tensor_copy(y_sb[0:CAP, s, 512:D], bank[5][0:CAP, :]).then_inc(y_v, 1)

            transposed(0, 0)
            expert_pair(0, True, False)
            with eng.Fori(1, PAIRS - 1) as i:
                expert_pair(i, False, False)
            expert_pair(PAIRS - 1, False, True)

            def add_experts(t, w, done, then):
                y0, y1 = yg[:, t % 2, 0, :], yg[:, t % 2, 1, :]
                then(eng.tensor_scalar(y0, y0, w[:, t, 0:1], None, ALU.mult))
                then(eng.scalar_tensor_tensor(out=y0, in0=y1, scalar=w[:, t, 1:2], in1=y0,
                                              op0=ALU.mult, op1=ALU.add))
                then(eng.tensor_tensor(y0, y0, G2[:, 0 if t == 0 else 1, :], ALU.mult))
                eng.tensor_tensor(x_rows[:, t, :], x_rows[:, t, :], y0, ALU.add).then_inc(done, 1)

            eng.wait_ge(flag_ready, 1)
            most = eng.value_load(flag[0:1, 0:1], min_val=0, max_val=T)
            with eng.If(most > CAP):
                for b in range(OB):
                    for t in range(TT):
                        for k in range(2):
                            n = (b * TT + t) * 2 + k
                            if n:
                                eng.wait_ge(o_table, n)
                            eng.tensor_scalar(orank[:, b * OC:(b + 1) * OC],
                                              iota[:, CAP + b * OC:CAP + (b + 1) * OC],
                                              rank[:, t, k:k + 1], None, ALU.is_equal)\
                                .then_inc(o_onehot, 1)
                eng.wait_ge(o_table, OB * TT * 2)
                eng.tensor_copy(hg[0:OC, 0:OB * NE].bitcast(U32), bank[0][0:OC, 0:OB * NE])\
                    .then_inc(o_list, 1)
                eng.wait_ge(o_list, 1)
                eng.sem_inc(o_end, 1)
                eng.sem_inc(o_xgT, 1)
                eng.sem_inc(o_z, 1)
                eng.sem_inc(o_y, 1)
                with eng.Fori(0, NE) as e:
                    for b in range(OB):
                        eng.wait_ge(o_xgT, e * (2 * OB) + 2 * b + 2)
                        eng.tensor_copy(oxgT[:, 4:8, b * OC:(b + 1) * OC],
                                        bank[1][:, 0:4 * OC].rearrange("p (k t) -> p k t", k=4))\
                            .then_inc(o_xgT, 1)
                    for j in range(JF):
                        eng.wait_ge(o_silu, e * JF + j + 1)
                        eng.wait_ge(o_prod, e * (2 * JF) + 2 * j + 2)
                        eng.tensor_tensor(oz[:, j, :], bank[3][:, 0:OT], osil, ALU.mult).then_inc(o_z, 1)
                    for b in range(OB):
                        eng.wait_ge(o_y, e * (2 * OB) + 2 * b + 2)
                        eng.tensor_copy(oy[0:OC, 512:D], bank[5][0:OC, :]).then_inc(o_y, 1)
                o_steps = [0]

                def then_o(ins):
                    ins.then_inc(step_o, 1)
                    o_steps[0] += 1
                    eng.wait_ge(step_o, o_steps[0])

                for t in range(TT):
                    then_o(eng.tensor_scalar(oslot_f[:, t, :], rank[:, t, :], float(CAP), 0.0,
                                           ALU.subtract, ALU.max))
                    then_o(eng.scalar_tensor_tensor(out=oslot_f[:, t, :], in0=rt[:, t, 46:48],
                                                  scalar=float(OT), in1=oslot_f[:, t, :],
                                                  op0=ALU.mult, op1=ALU.add))
                    then_o(eng.scalar_tensor_tensor(out=over_w[:, t, :], in0=rank[:, t, :],
                                                  scalar=float(CAP), in1=wts[:, t, :],
                                                  op0=ALU.is_ge, op1=ALU.mult))
                eng.tensor_copy(oslot_u, oslot_f[:, :, :]).then_inc(o_slots, 1)
                for t in range(TT):
                    eng.wait_ge(o_yg_in[t], 32)
                    add_experts(t, over_w, o_added, then_o)

            for t in range(TT):
                eng.wait_ge(yg_in[t], 32)
                add_experts(t, main_w, res_ready, then)
                eng.wait_ge(ssq_ready, 2 * TT + t + 1)
                mean_square(2, slice(t, t + 1))
                eng.wait_ge(rms_ready, TT + t + 2)
                then(eng.reciprocal(stat[:, 2, 0, t:t + 1], stat[:, 2, 2, t:t + 1]))
                if t >= 2:
                    eng.wait_ge(out_sent[t - 2], 16)
                eng.scalar_tensor_tensor(out=o_rows[:, t % 2, :], in0=x_rows[:, t, :],
                                         scalar=stat[:, 2, 0, t:t + 1], in1=gfin,
                                         op0=ALU.mult, op1=ALU.mult).then_inc(out_ready, 1)


_INS = ['x_prompt', 'x_sample', 'state_rnn', 'c', 'c_ctx', 'w_ada', 'b_ada', 'g_norm1', 'g_norm2', 'w_in',
        'conv_w', 'w_conv_out', 'rnn_conv_w', 'rnn_conv_b', 'w_gate_a', 'b_gate_a', 'w_gate_x',
        'b_gate_x', 'lam', 'w_rnn_out', 'w_o', 'w_router_group', 'b_router_group', 'w_router_expert',
        'b_router_expert', 'w1', 'w3', 'w2', 'g_final']


def kernel(**inputs):
    import numpy as _np
    import concourse.bacc as _bacc
    from concourse import mybir as _mybir
    from concourse.bass_utils import run_bass_kernel_spmd as _run

    nc = _bacc.Bacc("TRN2", target_bir_lowering=False, num_devices=1)
    arrays, args = {}, []
    for name in _INS:
        a = _np.ascontiguousarray(inputs[name])
        arrays[f"in_{name}"] = a
        args.append(nc.dram_tensor(f"in_{name}", a.shape, _mybir.dt.from_np(a.dtype), kind="ExternalInput").ap())
    d = inputs["c"].shape[1]
    outs = [inputs["x_prompt"].shape, inputs["x_sample"].shape, (inputs["x_prompt"].shape[0], 1, 2, d)]
    for i, shape in enumerate(outs):
        args.append(nc.dram_tensor(f"out_{i}", shape, _mybir.dt.float32, kind="ExternalOutput").ap())
    layer_program(nc, *args)
    r = _run(nc, [arrays], core_ids=[0])
    return tuple(r.results[0][f"out_{i}"] for i in range(len(outs)))
```

```python
from contextlib import ExitStack

import concourse.bass as bass
from concourse import mybir

F32 = mybir.dt.float32
F32R = mybir.dt.float32r
U32 = mybir.dt.uint32
I32 = mybir.dt.int32
ALU = mybir.AluOpType
ACT = mybir.ActivationFunctionType
AX_X = mybir.AxisListType.X

P = 128
EPS = 1e-6
RG_C = 8.0
GRID_W = 64


def layer_program(nc, x_prompt, x_sample, state_rnn, c, c_ctx, w_ada, b_ada, g_norm1, g_norm2, w_in,
                  conv_w, w_conv_out, rnn_conv_w, rnn_conv_b, w_gate_a, b_gate_a, w_gate_x, b_gate_x,
                  lam, w_rnn_out, w_o, w_router_group, b_router_group, w_router_expert,
                  b_router_expert, w1, w3, w2, g_final, y_prompt, y_sample, state_new):
    D = w_o.shape[1]
    NP_TOK = x_prompt.shape[1]
    NS_TOK = x_sample.shape[1]
    T = NP_TOK + NS_TOK
    TT = T // P
    KD = D // P
    NG = w_router_group.shape[2]
    NE = w_router_expert.shape[2]
    EG = NE // NG
    FE = w1.shape[3]
    JF = FE // P
    assert NP_TOK == P and D == 1024 and FE == 512 and NS_TOK % GRID_W == 0

    CW = 512
    CT = CW // P
    SLOTS = 4
    MSLOTS = 6
    SUBS = 3
    QUART = KD * CW // 4
    BANKS = 6

    GAP = 3
    S0 = NP_TOK + GAP
    TG = S0 + NS_TOK
    ROWS = NS_TOK // GRID_W
    CG = 1 + NP_TOK + 1 + ROWS * (GRID_W + 1)

    CAP = 80
    OB = 4
    OC = (T - CAP) // OB
    OT = OB * OC
    assert CAP + OT == T

    BADA, CCTX, CSMP, GN1, GN2, STF, STB = 0, 48, 56, 64, 72, 80, 88
    CVW, RCW, RCB, BGA, BGX, LAM, NPAR = 96, 120, 152, 160, 176, 192, 208
    NPA = 96

    h2_dram = nc.dram_tensor("h2_rows", [T, D], F32).ap()
    y_dram = nc.dram_tensor("expert_rows", [NE * CAP, D], F32).ap()
    oy_dram = nc.dram_tensor("overflow_rows", [NE * OT, D], F32).ap()

    ada_v = w_ada[0].rearrange("(k p) n -> p k n", p=P)
    win_v = w_in[0].rearrange("(k p) n -> p k n", p=P)
    wco_v = w_conv_out[0].rearrange("(k p) n -> p k n", p=P)
    wro_v = w_rnn_out[0].rearrange("(k p) n -> p k n", p=P)
    wo_v = w_o[0].rearrange("(k p) n -> p k n", p=P)
    w1_v = w1[0].rearrange("e (p k) n -> e p (k n)", p=P)
    w3_v = w3[0].rearrange("e (p k) n -> e p (k n)", p=P)
    w2_v = w2[0].rearrange("e (j p) n -> e p j n", p=P)
    U_COL = {"b": 0, "c": D, "v": 2 * D, "xr": 3 * D, "g": 4 * D, "ma": 5 * D, "mb": 6 * D}

    stream, chunks = [], []

    def add_chunk(kind, half):
        chunks.append((kind, half))
        for m in range(CT):
            stream.append((kind, CT * half + m))

    def add_gates(b):
        for h in (2 * b, 2 * b + 1):
            for d in range(2):
                for x in range(2):
                    stream.append(("gate", h, d, x))

    WO_ON = [("wo", 0, 0), ("wo", 0, 1), ("wo", 1, 0), ("h2T", 0, 0), ("h2T", 0, 1), ("wo", 1, 1), ("route", 0),
             ("wo", 2, 0), ("h2T", 1, 0), ("h2T", 1, 1), ("wo", 2, 1), ("route", 1), ("rank", 0),
             ("h2T", 2, 0), ("h2T", 2, 1), ("route", 2), ("rank", 1), ("rank", 2), ("count",), ("list",)]
    assert TT == 3
    W_IN = [("xr", 0), 0, ("xr", 1), 1, ("c", 0), ("v", 0), 2, ("g", 0), ("c", 1), 3, ("b", 0), ("v", 1),
            ("b", 1), ("g", 1), ("ma", 0), ("ma", 1), ("mb", 0), ("mb", 1)]
    stream += [("par", 0), ("par", 1)] + [("xT", k) for k in range(KD)]
    for j in range(4):
        chunks.append(("ada", j))
        stream.append(("adaR", j))
        if j:
            stream.append(("adaC", j - 1))
    stream.append(("adaC", 3))
    for item in W_IN:
        if isinstance(item, int):
            add_gates(item)
        else:
            add_chunk(*item)
    for kind in ("yb", "ya"):
        add_chunk(kind, 0)
        add_chunk(kind, 1)
    for j in range(4, 12):
        chunks.append(("ada", j))
        stream.append(("adaR", j))
        if j > 4:
            stream += [("adaB", j - 1, 0), ("adaB", j - 1, 1)]
    stream += [("adaB", 11, 0), ("adaB", 11, 1), ("state",)]
    NSPLIT = len(chunks)
    chunks += [("wo", 0), ("wo", 1)]
    stream += WO_ON
    N_OF = {s: n for n, s in enumerate(stream)}
    C_OF = {s: n for n, s in enumerate(chunks)}
    N1 = len(chunks)
    PAIRS = NE // 2
    assert len(N_OF) == len(stream) and N1 % SLOTS == 0

    with ExitStack() as ctx:
        def sb(name, shape, dt=F32):
            return ctx.enter_context(nc.sbuf_tensor(name, shape, dt))

        def sem(name):
            return ctx.enter_context(nc.semaphore(name))

        CHUNK = 4 * KD * CW
        sizes = {"ring": SLOTS * CHUNK, "gw": CHUNK, "cp": 4 * 2 * 4 * CG, "ra": 4 * 2 * KD * T,
                 "xcy": 4 * KD * TG, "hg": 4 * KD * T, "lru": 4 * 4 * 4 * TG, "xrp": 4 * 2 * (TG + 3),
                 "sub": SUBS * 2 * 4 * QUART}
        sizes = {name: -(-size // 32) * 32 for name, size in sizes.items()}
        arena = sb("arena", [P, sum(sizes.values()) // 4])
        base, at = {}, nc.sbuf_base - sum(sizes.values())
        for name, size in sizes.items():
            base[name] = at
            at += size

        def over(name, region, shape, dt=F32, offset=0):
            return nc.alloc_sbuf_tensor_at(name, shape, dt, offset=base[region] + offset)

        ring = over("ring", "ring", [P, SLOTS, KD * CW])
        gate_w = over("gate_w", "gw", [P, KD * CW])
        cp = over("cp", "cp", [P, 2 * 4 * CG])
        h_hl = over("h_hl", "ra", [P, 2, KD, T], F32R)
        mod_sb = over("mod_sb", "ra", [P, 3, 2, D])
        moe_hl = over("moe_hl", "ra", [P, 2, (KD + JF) * CAP], F32R)
        MHL = 4 * 2 * (KD + JF) * CAP
        slot5 = over("slot5", "ra", [P, KD * CW], offset=MHL)
        hs_hl = over("hs_hl", "gw", [P, 2, KD, T], F32R)
        assert MHL + CHUNK <= sizes["ra"] and 8 * KD * T <= sizes["gw"] + sizes["cp"]
        xcy = over("xcy", "xcy", [P, KD * TG])
        hg = over("hg", "hg", [P, KD * T])
        lru = over("lru", "lru", [P, 4 * 4 * TG])
        xrp = over("xrp", "xrp", [P, 2, TG + 3])
        subs = over("subs", "sub", [P, SUBS, 2, QUART], F32R)
        oh = sb("oh", [P, 2 * TT * 2 * NE + TT * NE + TT * 2 * CAP])
        pT = sb("pT", [P, NPAR])
        ident = sb("ident", [P, P])
        ones = sb("ones", [P, P])
        before = sb("before", [P, P])
        iota = sb("iota", [P, T])
        tok = sb("tok", [P, TT])
        cvec = sb("cvec", [P, KD, 2])
        cst_all = sb("cst", [P, 4 * KD + P], F32R)
        selc = sb("selc", [5, 2])
        selv = sb("selv", [5, 2])
        selb = sb("selb", [5, 2, P])
        mod = sb("mod", [P, 2 * KD, 2])
        A1 = sb("A1", [P, KD, 2])
        sp = sb("sp", [P, 6, 16])
        rate = sb("rate", [P, 2, 16])
        stc = sb("stc", [P, 16])
        stat = sb("stat", [P, 3, 3, TT])
        wr = sb("wr", [P, KD, NG + NE])
        br = sb("br", [P, NG + NE])
        lg = sb("lg", [P, TT, 8])
        rt = sb("rt", [P, TT, 64])
        rti = sb("rti", [P, TT, 16], U32)
        rank = sb("rank", [P, TT, 2])
        wts = sb("wts", [P, TT, 2])
        slot_f = sb("slot_f", [P, TT, 2])
        slot_u = sb("slot_u", [P, TT, 2], U32)
        main_w = sb("main_w", [P, TT, 2])
        lists = sb("lists", [CAP, NE], U32)
        idx = [sb(f"idx{s}", [CAP, 1], U32) for s in range(2)]
        cmax = sb("cmax", [P, 1])
        flag = sb("flag", [P, 1], I32)
        oidx = [sb(f"oidx{b}", [OC, 1], U32) for b in range(OB)]
        bank = [ctx.enter_context(nc.psum_tensor(f"bank{i}", [P, 512], F32)) for i in range(BANKS)]

        cst = cst_all[:, 0:4 * KD].rearrange("p (k n) -> p k n", k=KD)
        x_in_rows = xcy[:, 0:TT * D].rearrange("p (t d) -> p t d", t=TT)
        oh_u = oh[:, :].bitcast(U32)
        n_oh = TT * 2 * NE
        pick = oh[:, 0:n_oh].rearrange("p (t k e) -> p t k e", t=TT, k=2)
        tok_oh = oh[:, n_oh:2 * n_oh].rearrange("p (t k e) -> p t k e", t=TT, k=2)
        both = oh[:, 2 * n_oh:2 * n_oh + TT * NE].rearrange("p (t e) -> p t e", t=TT)
        rank_oh = oh[:, 2 * n_oh + TT * NE:2 * n_oh + TT * NE + TT * 2 * CAP]\
            .rearrange("p (t k r) -> p t k r", t=TT, k=2)
        xTr = hg[:, :].rearrange("p (k t) -> p k t", k=KD)
        gw = gate_w[:, :].rearrange("p (x d h j) -> p x d h j", x=2, d=2, h=KD)
        G1, A2, B2 = mod_sb[:, 0], mod_sb[:, 1], mod_sb[:, 2]
        x_rows = hg[:, :].rearrange("p (t d) -> p t d", t=TT)
        xc = xcy[:, :].rearrange("p (k t) -> p k t", k=KD)
        ya_in = xcy[:, 0:KD * T].rearrange("p (k t) -> p k t", k=KD)
        hs = hg[:, :].rearrange("p (k t) -> p k t", k=KD)
        lru_v = lru[:, :].rearrange("p (b d h t) -> p b d h t", b=4, d=2, h=2)
        r_b, i_b, a_b, q_b = (lru_v[:, n] for n in range(4))
        lru_f = lru[:, :].rearrange("p (b n) -> p b n", b=4)
        r_f, i_f, a_f, q_f = (lru_f[:, n] for n in range(4))
        xs = lru[:, 0:TT * D].rearrange("p (t d) -> p t d", t=TT)
        junk = lru[:, TT * D:TT * D + D]
        SA = lru[:, 0:KD * T].rearrange("p (k t) -> p k t", k=KD)
        SB = lru[:, KD * T:2 * KD * T].rearrange("p (k t) -> p k t", k=KD)
        cpad = cp[:, 0:4 * CG].rearrange("p (m t) -> p m t", m=4)
        ycv = cp[:, 4 * CG:].rearrange("p (m t) -> p m t", m=4)
        G2 = cp[:, 0:2 * D].rearrange("p (c d) -> p c d", c=2)
        gfin = cp[:, 2 * D:3 * D]
        gtmp = xrp[:, :, 0:T]
        xrp_f = xrp[:, :, :].rearrange("p b t -> p (b t)")
        wo_tmp = xrp_f[:, 0:CW]
        par_rows = xrp_f[:, 0:2 * P].rearrange("p (j n) -> p j n", j=2)
        ABUF = 4
        arow = xcy[0:5, 0:ABUF * CW].rearrange("p (s n) -> p s n", s=ABUF)
        st_sb = xrp_f[0:16, CW + P:CW + 2 * P]
        le = xrp_f[:, CW:CW + TT * NE].rearrange("p (t e) -> p t e", t=TT)
        rank_m = xrp_f[:, 0:2 * NE].rearrange("p (k e) -> p k e", k=2)
        h2 = xcy[:, 0:2 * D].rearrange("p (b d) -> p b d", b=2)
        h2T = xcy[:, 2 * D:3 * D].rearrange("p (k t) -> p k t", k=KD)
        row_junk = lru[:, KD * T:KD * T + D]
        xg = xcy[:, 0:2 * D].rearrange("p (b d) -> p b d", b=2)
        y_sb = lru[:, 0:2 * D].rearrange("p (b d) -> p b d", b=2)
        xgT = lru[:, 2 * D:2 * D + 2 * KD * CAP].rearrange("p (b k t) -> p b k t", b=2, k=KD)
        zs = lru[:, 2 * D + 2 * KD * CAP:2 * D + 2 * KD * CAP + 3 * JF * CAP]
        sil = zs[:, 0:JF * CAP]
        z = zs[:, JF * CAP:].rearrange("p (b n) -> p b n", b=2)
        oxg = ring[:, 3, :].rearrange("p (b d) -> p b d", b=OB)
        oxgT = gate_w[:, 0:KD * OT].rearrange("p (k t) -> p k t", k=KD)
        orank = gate_w[:, 0:OT]
        oz = slot5[:, 0:JF * OT].rearrange("p (j t) -> p j t", j=JF)
        osil = slot5[:, JF * OT:JF * OT + OT]
        oy = slot5[:, 2048:2048 + D]
        olist_f = slot5[0:OC, 2048 + D:2048 + D + OB * NE].bitcast(U32)
        olist = olist_f.rearrange("p (b e) -> p b e", b=OB)
        yg = ring[:, 0, :].rearrange("p (b k d) -> p b k d", b=2, k=2)
        o_rows = ring[:, 1, 0:2 * D].rearrange("p (b d) -> p b d", b=2)
        o_junk = ring[:, 1, 2 * D:3 * D]

        landed = [sem(f"chunk_landed{s}") for s in range(MSLOTS)]
        hi_ready = sem("hi_ready")
        lo_v = sem("lo_by_vector")
        lo_p = sem("lo_by_gpsimd")
        act_hi = sem("activation_hi")
        ada_quarter = sem("ada_quarter_used")
        tile_done = sem("tile_done")
        bank_free = [sem(f"bank_free{s}") for s in range(BANKS)]
        params_in = [sem("params_a_in"), sem("params_b_in")]
        x_in = sem("x_in")
        x_again = sem("x_rows_again")
        gate_w_in = sem("gate_w_in")
        router_in = sem("router_in")
        consts = sem("consts")
        cvec_ready = sem("cvec_ready")
        lam_exp = sem("lam_exp")
        rate_ready = sem("rate_ready")
        ssq_ready = sem("ssq_ready")
        mean_ready = sem("mean_ready")
        rms_ready = sem("rms_ready")
        xs_ready = sem("xs_ready")
        xT_ready = sem("xT_ready")
        h_ready = sem("h_ready")
        h_whole = sem("h_before_split")
        ya_split = sem("ya_split")
        hs_split = sem("hs_split")
        pads_zero = sem("pads_zero")
        xr_ready = sem("xr_ready")
        xc_ready = sem("xc_ready")
        sig_done = sem("gate_sigmoids")
        exp_done = sem("gate_exps")
        q_ready = sem("one_minus_a2")
        root_done = sem("gate_roots")
        batch_done = sem("scans_done")
        c_ready = sem("c_ready")
        conv_done = sem("conv_done")
        hg_ready = sem("hg_ready")
        merged_ready = sem("merged_ready")
        selectors = sem("selectors")
        arow_bias_in = [sem(f"ada_bias_in{s}") for s in range(ABUF)]
        gn2_in = sem("g_norm2_in")
        gfin_in = sem("g_final_in")
        state_out = sem("state_out")
        x1_ready = sem("x1_ready")
        h2_ready = sem("h2_ready")
        h2_out = [sem(f"h2_out{t}") for t in range(TT)]
        tops_ready = sem("tops_ready")
        texp_ready = sem("top_exps_ready")
        both_ready = sem("both_ready")
        onehots_ready = sem("onehots_ready")
        slots_ready = sem("slots_ready")
        bias_in = sem("router_bias_in")
        flag_ready = sem("flag_ready")
        idx_ready = sem("idx_ready")
        gathers_begun = sem("gathers_begun")
        xg_in = [sem(f"xg_in{s}") for s in range(2)]
        xg_used = sem("xg_transposed")
        xgT_a = sem("xgT_by_scalar")
        xgT_v = sem("xgT_by_vector")
        up_done = sem("w1_product")
        gate_done = sem("w3_product")
        silu_done = sem("silu_done")
        z_ready = sem("z_ready")
        down_done = sem("w2_product")
        y_a = sem("y_by_scalar")
        y_v = sem("y_by_vector")
        y_out = [sem(f"y_out{s}") for s in range(2)]
        step_v = sem("vector_step")
        step_a = sem("scalar_step")
        step_o = sem("overflow_vector_step")
        yg_in = [sem(f"yg_in{s}") for s in range(TT)]
        res_ready = sem("residual_ready")
        out_ready = sem("out_ready")
        out_sent = [sem(f"out_sent{t}") for t in range(TT)]
        o_landed = [sem(f"overflow_w{n}") for n in range(3)]
        o_onehot = sem("overflow_onehots")
        o_table = sem("overflow_table")
        o_list = sem("overflow_lists")
        o_idx = sem("overflow_idx")
        o_xg_in = sem("overflow_xg_in")
        o_trans = sem("overflow_transposed")
        o_xgT = sem("overflow_xgT")
        o_prod = sem("overflow_product")
        o_silu = sem("overflow_silu")
        o_z = sem("overflow_z")
        o_down = sem("overflow_down")
        o_y = sem("overflow_y")
        o_yout = sem("overflow_y_out")
        o_end = sem("overflow_expert_end")
        o_slots = sem("overflow_slots")
        o_yg_in = [sem(f"overflow_yg_in{t}") for t in range(TT)]
        o_added = sem("overflow_added")

        y_rows = y_dram.rearrange("(e r) d -> e r d", e=NE)
        oy_rows = oy_dram.rearrange("(e r) d -> e r d", e=NE)
        oslot_f, oslot_u, over_w = slot_f, oh_u[:, 0:TT * 2].rearrange("p (t k) -> p t k", t=TT), \
            oh[:, TT * 2:TT * 4].rearrange("p (t k) -> p t k", t=TT)

        block = ctx.enter_context(nc.Block())

        def wait_tile(eng, name):
            eng.wait_ge(tile_done, N_OF[name] + 1)

        def wait_read(eng, name):
            n = N_OF[name]
            eng.wait_ge(bank_free[n % BANKS], n // BANKS + 1)

        def quarter_of(kind, tile_):
            return 4 * C_OF[(kind, tile_ // CT)] + tile_ % CT

        def quarter(q):
            n, m = q // CT, q % CT
            pair = subs[:, q % SUBS, :, :]
            if chunks[n][0] == "ada":
                return slot_k(n)[:, 2 * m:2 * m + 2, :], pair.rearrange("p x (k n) -> p x k n", k=2)
            return slot_k(n)[:, :, m * P:(m + 1) * P], pair.rearrange("p x (k n) -> p x k n", k=KD)

        def wait_quarter_used(eng, q):
            kind, half = chunks[q // CT]
            if kind != "ada":
                wait_tile(eng, (kind, CT * half + q % CT))
            elif q % CT == CT - 1:
                wait_tile(eng, ("adaR", half))
            else:
                eng.wait_ge(ada_quarter, (CT - 1) * half + q % CT + 1)

        def ada_rows_of(eng, j, share):
            v, cols = j // 2 - 2, slice(j % 2 * CW, (j % 2 + 1) * CW)
            dst = (G1, B2, A2, G2)[v]
            scaled = v == 2
            for cnd in range(2):
                if share == (1 if scaled else cnd):
                    ps, free = bank[N_OF[("adaB", j, cnd)] % BANKS], bank_free[N_OF[("adaB", j, cnd)] % BANKS]
                    wait_tile(eng, ("adaB", j, cnd))
                    out = dst[:, cnd, cols]
                    if scaled:
                        eng.scalar_tensor_tensor(out=out, in0=ps[:, :], scalar=1.0, in1=out,
                                                 op0=ALU.add, op1=ALU.mult).then_inc(free, 1)
                    elif share == 0:
                        eng.activation(out, ps[:, :], ACT.Copy).then_inc(free, 1)
                    else:
                        eng.tensor_copy(out, ps[:, :]).then_inc(free, 1)

        VQ = [q for q in range(4 * NSPLIT) if chunks[q // CT][0] == "ada"]
        PQ = [q for q in range(4 * NSPLIT) if chunks[q // CT][0] != "ada"]

        def wait_split(eng, q):
            if q in VQ:
                eng.wait_ge(lo_v, VQ.index(q) + 1)
            else:
                eng.wait_ge(lo_p, PQ.index(q) + 1)

        def write_lo(eng, q, done):
            src, pair = quarter(q)
            eng.wait_ge(hi_ready, q + 1)
            eng.tensor_tensor(pair[:, 1], src, pair[:, 0].bitcast(F32), ALU.subtract).then_inc(done, 1)

        def wait_chunk(eng, n):
            eng.wait_ge(landed[n % SLOTS], 16 * (n // SLOTS + 1))

        def wait_chunk_used(eng, n):
            if n < NSPLIT:
                wait_split(eng, 4 * n + 3)
            else:
                wait_tile(eng, ("wo", TT - 1, chunks[n][1]))

        def chunk_src(kind, half):
            if kind == "ada":
                return ada_v[:, :, CW * half:CW * (half + 1)]
            if kind in U_COL:
                a = U_COL[kind] + CW * half
                return win_v[:, :, a:a + CW]
            src = {"ya": wco_v, "yb": wro_v, "wo": wo_v}[kind]
            return src[:, :, CW * half:CW * (half + 1)]

        def slot_k(n):
            return ring[:, n % SLOTS, :].rearrange("p (k n) -> p k n", k=KD)

        moe_slots = [ring[:, 0, :], ring[:, 1, :], gate_w[:, :], ring[:, 2, :], ring[:, 3, :], slot5[:, :]]
        moe_landed = [landed[0], landed[1], landed[4], landed[2], landed[3], landed[5]]

        def moe_count(i, q):
            before_moe = 0 if q in (2, 5) else N1 // SLOTS
            return 16 * (i + before_moe + 1)

        @block.sync
        def _(eng):
            eng.wait_ge(x_in, 32)
            for n, (kind, half) in enumerate(chunks):
                if n == 6:
                    for x, src in enumerate((w_gate_a, w_gate_x)):
                        for d in range(2):
                            eng.dma_start(gw[:, x, d, :, :], src[0, d].rearrange("h i j -> i h j"))\
                                .then_inc(gate_w_in, 16)
                if n >= SLOTS:
                    wait_chunk_used(eng, n - SLOTS)
                eng.dma_start(slot_k(n), chunk_src(kind, half)).then_inc(landed[n % SLOTS], 16)

            def load_pair(i, first):
                for s in range(2):
                    for m, (src, used) in enumerate(((w1_v, up_done), (w3_v, gate_done), (w2_v, down_done))):
                        q = 3 * s + m
                        if not first:
                            eng.wait_ge(used, i * 2 + (s - 1))
                        elif q == 2:
                            wait_tile(eng, ("yb", KD - 1))
                        elif q == 5:
                            eng.wait_ge(h2_ready, TT)
                        else:
                            wait_chunk_used(eng, N1 - SLOTS + (q if q < 2 else q - 1))
                        dst = moe_slots[q]
                        if m == 2:
                            dst = dst.rearrange("p (j n) -> p j n", j=JF)
                        eng.dma_start(dst, src[i * 2 + s]).then_inc(moe_landed[q], 16)

            load_pair(0, True)
            with eng.Fori(1, PAIRS) as i:
                load_pair(i, False)
            eng.wait_ge(flag_ready, 1)
            most = eng.value_load(flag[0:1, 0:1], min_val=0, max_val=T)
            with eng.If(most > CAP):
                with eng.Fori(0, NE) as e:
                    eng.wait_ge(o_end, e + 1)
                    eng.dma_start(ring[:, 0, :], w1_v[e, :, :]).then_inc(o_landed[0], 16)
                    eng.dma_start(ring[:, 1, :], w3_v[e, :, :]).then_inc(o_landed[1], 16)
                    eng.dma_start(ring[:, 2, :].rearrange("p (j n) -> p j n", j=JF),
                                  w2_v[e, :, :, :]).then_inc(o_landed[2], 16)

        @block.gpsimd
        def _(eng):
            eng.memset(ident[:, :], 0.0).then_inc(consts, 1)
            eng.memset(ones[:, :], 1.0).then_inc(consts, 1)
            eng.wait_ge(consts, 2)
            eng.affine_select(out=ident[:, :], in_=ident[:, :], compare_op=ALU.not_equal, fill=1.0,
                              base=0, pattern=[[-1, P]], channel_multiplier=1).then_inc(consts, 1)
            eng.affine_select(out=before[:, :], in_=ones[:, :], compare_op=ALU.is_gt, fill=0.0,
                              base=0, pattern=[[1, P]], channel_multiplier=-1).then_inc(consts, 1)
            eng.iota(iota[:, :], pattern=[[1, T]], base=0, channel_multiplier=0,
                     allow_small_or_imprecise_dtypes=True).then_inc(consts, 1)
            eng.iota(tok[:, :], pattern=[[P, TT]], base=0, channel_multiplier=1,
                     allow_small_or_imprecise_dtypes=True).then_inc(consts, 1)

            def gather(e, s):
                eng.tensor_copy(idx[s][:, :], lists[:, bass.ds(e, 1)]).then_inc(idx_ready, 1)
                eng.wait_ge(idx_ready, e + 1)
                eng.sem_inc(gathers_begun, 1)
                eng.indirect_dma_start(out=xg[0:CAP, s, :], out_offset=None, in_=h2_dram[:, :],
                                       in_offset=bass.IndirectOffsetOnAxis(ap=idx[s][:, 0:1], axis=0),
                                       ).then_inc(xg_in[s], 16)

            for q in PQ:
                write_lo(eng, q, lo_p)

            wait_read(eng, ("list",))
            for t in range(TT):
                eng.wait_ge(h2_out[t], 16)
            for s in range(2):
                gather(s, s)
            with eng.Fori(1, PAIRS) as i:
                for s in range(2):
                    eng.wait_ge(xg_used, i * 2 + (s - 1))
                    gather(i * 2 + s, s)

            eng.wait_ge(flag_ready, 1)
            most = eng.value_load(flag[0:1, 0:1], min_val=0, max_val=T)
            with eng.If(most > CAP):
                eng.wait_ge(o_list, 1)
                with eng.Fori(0, NE) as e:
                    eng.wait_ge(o_end, e + 1)
                    for b in range(OB):
                        eng.tensor_copy(oidx[b][:, :], olist[:, b, bass.ds(e, 1)]).then_inc(o_idx, 1)
                    eng.wait_ge(o_idx, e * OB + OB)
                    eng.sem_inc(gathers_begun, 1)
                    for b in range(OB):
                        eng.indirect_dma_start(
                            out=oxg[0:OC, b, :], out_offset=None, in_=h2_dram[:, :],
                            in_offset=bass.IndirectOffsetOnAxis(ap=oidx[b][:, 0:1], axis=0),
                        ).then_inc(o_xg_in, 16)
                eng.wait_ge(o_yout, 16 * NE * OB)
                eng.wait_ge(o_slots, 1)
                for t in range(TT):
                    if t >= 2:
                        eng.wait_ge(o_added, t - 1)
                    for k in range(2):
                        eng.indirect_dma_start(
                            out=yg[:, t % 2, k, :], out_offset=None, in_=oy_dram[:, :],
                            in_offset=bass.IndirectOffsetOnAxis(ap=oslot_u[:, t, k:k + 1], axis=0),
                        ).then_inc(o_yg_in[t], 16)
                eng.wait_ge(o_added, TT)
            eng.wait_ge(slots_ready, TT)
            for s in range(2):
                eng.wait_ge(y_out[s], 16 * PAIRS)
            for t in range(TT):
                if t >= 2:
                    eng.wait_ge(res_ready, t - 1)
                for k in range(2):
                    eng.indirect_dma_start(
                        out=yg[:, t % 2, k, :], out_offset=None, in_=y_dram[:, :],
                        in_offset=bass.IndirectOffsetOnAxis(ap=slot_u[:, t, k:k + 1], axis=0),
                    ).then_inc(yg_in[t], 16)

        @block.tensor
        def _(eng):
            def open_tile(name):
                n = N_OF[name]
                if n >= BANKS:
                    eng.wait_ge(bank_free[n % BANKS], n // BANKS)
                return bank[n % BANKS]

            def transpose_params(j, rows):
                ps = open_tile(("par", j))
                eng.wait_ge(params_in[j], 16 * (7 if j == 0 else 6))
                eng.transpose(ps[:, 0:rows], par_rows[0:rows, j, :], ident[0:rows, 0:rows])\
                    .then_inc(tile_done, 1)

            def transpose_x(k):
                ps = open_tile(("xT", k))
                for t in range(TT):
                    mm = eng.transpose(ps[:, t * P:(t + 1) * P], xs[:, t, k * P:(k + 1) * P], ident[:, :])
                mm.then_inc(tile_done, 1)

            def ada_rows(j):
                ps = open_tile(("adaR", j))
                for m in range(CT):
                    q = 4 * C_OF[("ada", j)] + m
                    _, pair = quarter(q)
                    wait_split(eng, q)
                    for kk in range(2):
                        k = 2 * m + kk
                        c4 = cst_all[:, 4 * k:4 * k + P]
                        eng.matmul(ps[:, :], c4, pair[:, 1, kk, :], start=(k == 0), stop=False)
                        mm = eng.matmul(ps[:, :], c4, pair[:, 0, kk, :], start=False, stop=(k == KD - 1))
                    mm.then_inc(tile_done if m == CT - 1 else ada_quarter, 1)

            def ada_columns(j):
                ps = open_tile(("adaC", j))
                wait_read(eng, ("adaR", j))
                for m in range(CT):
                    mm = eng.matmul(ps[:, 2 * m:2 * m + 2], arow[0:4, j % ABUF, m * P:(m + 1) * P],
                                    selc[0:4, :], start=True, stop=True)
                mm.then_inc(tile_done, 1)

            def ada_spread(j):
                for cnd in range(2):
                    ps = open_tile(("adaB", j, cnd))
                    if cnd == 0:
                        wait_read(eng, ("adaR", j))
                        eng.wait_ge(arow_bias_in[j % ABUF], 16 * (j // ABUF))
                    eng.matmul(ps[:, :], selb[:, cnd, :], arow[:, j % ABUF, :], start=True, stop=True)\
                        .then_inc(tile_done, 1)

            def project(kind, half, x, ready=None):
                for m in range(CT):
                    ps = open_tile((kind, CT * half + m))
                    q = quarter_of(kind, CT * half + m)
                    _, pair = quarter(q)
                    wait_split(eng, q)
                    for k in range(KD):
                        if ready is not None and m == 0:
                            eng.wait_ge(ready, k + 1)
                        eng.matmul(ps[:, 0:T], pair[:, 1, k, :], x[:, 0, k, :], start=(k == 0), stop=False)
                        eng.matmul(ps[:, 0:T], pair[:, 0, k, :], x[:, 1, k, :], start=False, stop=False)
                        mm = eng.matmul(ps[:, 0:T], pair[:, 0, k, :], x[:, 0, k, :],
                                        start=False, stop=(k == KD - 1))
                    mm.then_inc(tile_done, 1)

            def gates(b):
                for h in (2 * b, 2 * b + 1):
                    eng.wait_ge(xc_ready, h + 1)
                    for d in range(2):
                        for x in range(2):
                            ps = open_tile(("gate", h, d, x))
                            eng.matmul(ps[:, 0:TG], gw[:, x, d, h, :], xc[:, h, :],
                                       start=True, stop=True).then_inc(tile_done, 1)

            eng.wait_ge(consts, 6)
            transpose_params(0, NPA)
            transpose_params(1, NPAR - NPA)
            eng.wait_ge(xs_ready, TT)
            for k in range(KD):
                transpose_x(k)
            eng.wait_ge(cvec_ready, 3)
            eng.wait_ge(selectors, 4)
            for j in range(4):
                ada_rows(j)
                if j:
                    ada_columns(j - 1)
            ada_columns(3)
            for n, item in enumerate(W_IN):
                if isinstance(item, int):
                    if item == 0:
                        eng.wait_ge(gate_w_in, 64)
                    gates(item)
                else:
                    project(item[0], item[1], h_hl, h_ready if n == 0 else None)
            project("yb", 0, hs_hl, hs_split)
            project("yb", 1, hs_hl)
            project("ya", 0, h_hl, ya_split)
            project("ya", 1, h_hl)
            for j in range(4, 12):
                ada_rows(j)
                if j > 4:
                    ada_spread(j - 1)
            ada_spread(11)
            ps = open_tile(("state",))
            eng.wait_ge(batch_done, 4)
            eng.transpose(ps[0:16, 0:P], stc[:, :], ident[:, :]).then_inc(tile_done, 1)

            def out_rows(t, half):
                ps = open_tile(("wo", t, half))
                n = C_OF[("wo", half)]
                wait_chunk(eng, n)
                for k in range(KD):
                    if t == 0 and half == 0:
                        eng.wait_ge(merged_ready, k + 1)
                    mm = eng.matmul(ps[:, :], SA[:, k, t * P:(t + 1) * P], slot_k(n)[:, k, :],
                                    start=(k == 0), stop=(k == KD - 1))
                mm.then_inc(tile_done, 1)

            def transpose_h2(t, half):
                ps = open_tile(("h2T", t, half))
                if half == 0:
                    eng.wait_ge(h2_ready, t + 1)
                for m in range(4):
                    k = 4 * half + m
                    mm = eng.transpose(ps[:, m * P:(m + 1) * P], h2[:, t % 2, k * P:(k + 1) * P], ident[:, :])
                mm.then_inc(tile_done, 1)

            def route(t):
                ps = open_tile(("route", t))
                eng.wait_ge(router_in, 32)
                wait_read(eng, ("h2T", t, 0))
                wait_read(eng, ("h2T", t, 1))
                for k in range(KD):
                    mm = eng.matmul(ps[:, 0:NG + NE], h2T[:, k, :], wr[:, k, :],
                                    start=(k == 0), stop=(k == KD - 1))
                mm.then_inc(tile_done, 1)

            def rank_tokens(t):
                ps = open_tile(("rank", t))
                eng.wait_ge(both_ready, t + 1)
                for u in range(t):
                    eng.matmul(ps[:, 0:NE], ones[:, :], both[:, u, :], start=(u == 0), stop=False)
                eng.matmul(ps[:, 0:NE], before[:, :], both[:, t, :], start=(t == 0), stop=True)\
                    .then_inc(tile_done, 1)

            def count_tokens():
                ps = open_tile(("count",))
                for t in range(TT):
                    mm = eng.matmul(ps[:, 0:NE], ones[:, :], both[:, t, :], start=(t == 0),
                                    stop=(t == TT - 1))
                mm.then_inc(tile_done, 1)

            def list_tokens():
                ps = open_tile(("list",))
                eng.wait_ge(onehots_ready, TT)
                for t in range(TT):
                    for k in range(2):
                        mm = eng.matmul(ps[0:CAP, 0:NE], rank_oh[:, t, k, :], tok_oh[:, t, k, :],
                                        start=(t == 0 and k == 0), stop=(t == TT - 1 and k == 1))
                mm.then_inc(tile_done, 1)

            tile_work = {"wo": out_rows, "h2T": transpose_h2, "route": route, "rank": rank_tokens,
                         "count": count_tokens, "list": list_tokens}
            for name in WO_ON:
                tile_work[name[0]](*name[1:])

            for b in range(BANKS):
                uses = (len(stream) - b + BANKS - 1) // BANKS
                eng.wait_ge(bank_free[b], uses)

            def transpose_rows(e, s, land):
                eng.wait_ge(xg_in[s], land)
                rows = xg[0:CAP, s, :].rearrange("t (p k) -> t k p", k=KD)
                for k in range(KD):
                    b, m = k // 4, k % 4
                    mm = eng.transpose(bank[b][:, m * CAP:(m + 1) * CAP], rows[:, k, :],
                                       ident[0:CAP, 0:CAP])
                mm.then_inc(xg_used, 1)

            def expert(i, s, first, last):
                e = i * 2 + s
                eng.wait_ge(xgT_a, e + 1)
                eng.wait_ge(xgT_v, e + 1)
                for m, (b, done) in enumerate(((2, up_done), (3, gate_done))):
                    q = 3 * s + m
                    w = moe_slots[q].rearrange("p (k n) -> p k n", k=KD)
                    eng.wait_ge(moe_landed[q], moe_count(i, q))
                    for j in range(JF):
                        for k in range(KD):
                            mm = eng.matmul(bank[b][:, j * CAP:(j + 1) * CAP],
                                            w[:, k, j * P:(j + 1) * P], xgT[:, s, k, :],
                                            start=(k == 0), stop=(k == KD - 1))
                    mm.then_inc(done, 1)
                if not last:
                    transpose_rows(e + 1, 1 - s, 16 * (i + s + 1))
                q = 3 * s + 2
                w = moe_slots[q].rearrange("p (j n) -> p j n", j=JF)
                eng.wait_ge(moe_landed[q], moe_count(i, q))
                eng.wait_ge(z_ready, e + 1)
                if not first:
                    eng.wait_ge(y_a, e)
                    eng.wait_ge(y_v, e)
                for half in range(2):
                    for j in range(JF):
                        mm = eng.matmul(bank[4 + half][0:CAP, :], z[:, s, j * CAP:(j + 1) * CAP],
                                        w[:, j, half * 512:(half + 1) * 512],
                                        start=(j == 0), stop=(j == JF - 1))
                mm.then_inc(down_done, 1)

            transpose_rows(0, 0, 16)
            for s in range(2):
                expert(0, s, s == 0, False)
            with eng.Fori(1, PAIRS - 1) as i:
                for s in range(2):
                    expert(i, s, False, False)
            for s in range(2):
                expert(PAIRS - 1, s, False, s == 1)

            eng.wait_ge(flag_ready, 1)
            most = eng.value_load(flag[0:1, 0:1], min_val=0, max_val=T)
            with eng.If(most > CAP):
                eng.wait_ge(y_a, NE)
                eng.wait_ge(y_v, NE)
                for b in range(OB):
                    for t in range(TT):
                        for k in range(2):
                            eng.wait_ge(o_onehot, (b * TT + t) * 2 + k + 1)
                            mm = eng.matmul(bank[0][0:OC, b * NE:(b + 1) * NE],
                                            orank[:, b * OC:(b + 1) * OC], tok_oh[:, t, k, :],
                                            start=(t == 0 and k == 0), stop=(t == TT - 1 and k == 1))
                            mm.then_inc(o_table, 1)
                eng.wait_ge(o_list, 1)
                with eng.Fori(0, NE) as e:
                    eng.wait_ge(o_xg_in, e * (16 * OB) + 16 * OB)
                    for b in range(OB):
                        rows = oxg[0:OC, b, :].rearrange("t (p k) -> t k p", k=KD)
                        eng.wait_ge(o_xgT, e * (2 * OB) + 2 * b + 1)
                        for k in range(KD):
                            mm = eng.transpose(bank[k // 4][:, (k % 4) * OC:(k % 4 + 1) * OC],
                                               rows[:, k, :], ident[0:OC, 0:OC])
                        mm.then_inc(o_trans, 1)
                    eng.wait_ge(o_xgT, e * (2 * OB) + 2 * OB + 1)
                    eng.wait_ge(o_landed[0], e * 16 + 16)
                    eng.wait_ge(o_landed[1], e * 16 + 16)
                    for j in range(JF):
                        eng.wait_ge(o_z, e * JF + j + 1)
                        for m in range(2):
                            w = ring[:, m, :].rearrange("p (k n) -> p k n", k=KD)
                            for k in range(KD):
                                mm = eng.matmul(bank[2 + m][:, 0:OT], w[:, k, j * P:(j + 1) * P],
                                                oxgT[:, k, :], start=(k == 0), stop=(k == KD - 1))
                            mm.then_inc(o_prod, 1)
                    eng.wait_ge(o_z, e * JF + JF + 1)
                    eng.wait_ge(o_landed[2], e * 16 + 16)
                    w = ring[:, 2, :].rearrange("p (j n) -> p j n", j=JF)
                    for b in range(OB):
                        eng.wait_ge(o_y, e * (2 * OB) + 2 * b + 1)
                        for half in range(2):
                            for j in range(JF):
                                mm = eng.matmul(bank[4 + half][0:OC, :], oz[:, j, b * OC:(b + 1) * OC],
                                                w[:, j, half * 512:(half + 1) * 512],
                                                start=(j == 0), stop=(j == JF - 1))
                        mm.then_inc(o_down, 1)

        @block.scalar
        def _(eng):
            steps = [0]

            def then(ins):
                ins.then_inc(step_a, 1)
                steps[0] += 1
                eng.wait_ge(step_a, steps[0])

            def tile(name):
                n = N_OF[name]
                eng.wait_ge(tile_done, n + 1)
                return bank[n % BANKS], bank_free[n % BANKS]

            fed = [0]

            def feed(last_q):
                while fed[0] <= min(last_q, 4 * NSPLIT - 1):
                    q = fed[0]
                    src, pair = quarter(q)
                    if q % 4 == 0:
                        wait_chunk(eng, q // 4)
                    if q >= SUBS:
                        wait_quarter_used(eng, q - SUBS)
                    eng.activation(pair[:, 0], src, ACT.Copy).then_inc(hi_ready, 1)
                    fed[0] += 1

            def bias_row(j):
                if j >= 2 * ABUF:
                    wait_tile(eng, ("adaB", j - ABUF, 1))
                eng.dma_start(arow[4:5, j % ABUF, :], b_ada[0:1, j * CW:(j + 1) * CW])\
                    .then_inc(arow_bias_in[j % ABUF], 16)

            def ada_copies(j):
                for m in range(CT):
                    feed(4 * C_OF[("ada", j)] + m + SUBS)
                    if m == 0 and 6 <= j + 2 < 12:
                        bias_row(j + 2)
                ps, free = tile(("adaR", j))
                if j < 4:
                    eng.wait_ge(xs_ready, TT)
                elif j >= 2 * ABUF:
                    wait_tile(eng, ("adaB", j - ABUF, 1))
                eng.activation(arow[0:4, j % ABUF, :], ps[0:4, :], ACT.Copy)\
                    .then_inc(free, 1)

            def feed_behind(kind, k):
                feed(quarter_of(kind, k) + SUBS)

            def rows_of(dst, src, sem_):
                eng.dma_start(dst, src).then_inc(sem_, 16)

            a, b = par_rows[:, 0, :], par_rows[:, 1, :]
            rows_of(a[BADA:48, :], b_ada[0].rearrange("(r p) -> r p", p=P), params_in[0])
            rows_of(a[CCTX:CCTX + KD, :], c_ctx.rearrange("(r p) -> r p", p=P), params_in[0])
            rows_of(a[CSMP:CSMP + KD, :], c[0].rearrange("(r p) -> r p", p=P), params_in[0])
            rows_of(x_in_rows[:, 0, :], x_prompt[0], x_in)
            rows_of(x_in_rows[:, 1:TT, :], x_sample[0].rearrange("(t p) d -> p t d", p=P), x_in)
            rows_of(a[GN1:GN1 + KD, :], g_norm1[0].rearrange("(r p) -> r p", p=P), params_in[0])
            rows_of(a[GN2:GN2 + KD, :], g_norm2[0].rearrange("(r p) -> r p", p=P), params_in[0])
            for d in range(2):
                rows_of(a[STF + KD * d:STF + KD * (d + 1), :],
                        state_rnn[0, 0, d].rearrange("(r p) -> r p", p=P), params_in[0])
            o = CVW
            for src in (conv_w[0], rnn_conv_w[0]):
                n = src.shape[0] * KD
                rows_of(b[o - CVW:o - CVW + n, :], src.rearrange("w (r p) -> (w r) p", p=P), params_in[1])
                o += n
            rows_of(b[RCB - CVW:RCB - CVW + KD, :], rnn_conv_b[0].rearrange("(r p) -> r p", p=P), params_in[1])
            for at, src in ((BGA, b_gate_a), (BGX, b_gate_x), (LAM, lam)):
                rows_of(b[at - CVW:at - CVW + 2 * KD, :], src[0].rearrange("d (r p) -> (d r) p", p=P),
                        params_in[1])
            rows_of(wr[:, :, 0:NG], w_router_group[0].rearrange("(k p) n -> p k n", p=P), router_in)
            rows_of(wr[:, :, NG:], w_router_expert[0].rearrange("(k p) n -> p k n", p=P), router_in)
            rows_of(br[:, 0:NG], b_router_group[0].partition_broadcast(P), bias_in)
            rows_of(br[:, NG:], b_router_expert[0].partition_broadcast(P), bias_in)

            eng.wait_ge(x_in, 32)
            for t in range(TT):
                if t:
                    eng.wait_ge(ssq_ready, t)
                eng.activation(junk, x_in_rows[:, t, :], ACT.Square, accum_out=stat[:, 0, 0, t:t + 1])\
                    .then_inc(ssq_ready, 1)
            eng.wait_ge(mean_ready, 1)
            eng.activation(stat[:, 0, 2, :], stat[:, 0, 1, :], ACT.Sqrt).then_inc(rms_ready, 1)
            wait_read(eng, ("par", 0))
            wait_read(eng, ("par", 1))
            then(eng.activation(sp[:, 0, :], pT[:, LAM:NPAR], ACT.Abs))
            eng.activation(sp[:, 1, :], sp[:, 0, :], ACT.Exp, scale=-1.0).then_inc(lam_exp, 1)
            eng.activation(cvec[:, :, :], pT[:, CCTX:CCTX + 2 * KD].rearrange("p (c k) -> p k c", c=2),
                           ACT.Silu).then_inc(cvec_ready, 1)
            eng.wait_ge(cvec_ready, 1)
            eng.activation(cst[:, :, 0:2], cvec[:, :, :], ACT.Copy).then_inc(cvec_ready, 1)
            for k in range(KD):
                ps, free = tile(("xT", k))
                eng.activation(xTr[:, k, :], ps[:, 0:T], ACT.Copy).then_inc(free, 1)
                if k == 3:
                    feed(2)
            for j in range(4):
                ada_copies(j)
            for k in range(KD):
                eng.wait_ge(h_whole, k + 1)
                eng.activation(h_hl[:, 0, k, :], xTr[:, k, :], ACT.Copy).then_inc(act_hi, 1)

            eng.wait_ge(pads_zero, 2)

            def copy_xr(h):
                ps, free = tile(("xr", h))
                if h >= 2:
                    eng.wait_ge(xc_ready, h - 1)
                eng.activation(xrp[:, h % 2, 2:2 + NP_TOK], ps[:, 0:NP_TOK], ACT.Copy)
                eng.activation(xrp[:, h % 2, 2 + S0:2 + TG], ps[:, NP_TOK:T], ACT.Copy)\
                    .then_inc(free, 1)
                feed_behind("xr", h)

            def gate_sigmoids(b):
                if b >= 1:
                    eng.wait_ge(batch_done, b)
                for h in (2 * b, 2 * b + 1):
                    for d in range(2):
                        for x, (dst, bias) in enumerate(((r_b, BGA), (i_b, BGX))):
                            ps, free = tile(("gate", h, d, x))
                            col = bias + d * KD + h
                            eng.activation(dst[:, d, h % 2, :], ps[:, 0:TG], ACT.Sigmoid,
                                           bias=pT[:, col:col + 1]).then_inc(free, 1)

            def gate_exps(b):
                for h in (2 * b, 2 * b + 1):
                    for d in range(2):
                        for x in range(2):
                            n = N_OF[("gate", h, d, x)]
                            eng.wait_ge(bank_free[n % BANKS], n // BANKS + 1)
                if b == 0:
                    eng.wait_ge(rate_ready, 1)
                for h in (2 * b, 2 * b + 1):
                    for d in range(2):
                        col = d * KD + h
                        eng.activation(a_b[:, d, h % 2, :], r_b[:, d, h % 2, :], ACT.Exp,
                                       scale=rate[:, 0, col:col + 1]).then_inc(exp_done, 1)
                for h in (2 * b, 2 * b + 1):
                    for d in range(2):
                        col = d * KD + h
                        eng.activation(r_b[:, d, h % 2, :], r_b[:, d, h % 2, :], ACT.Tanh,
                                       scale=rate[:, 1, col:col + 1]).then_inc(exp_done, 1)

            def gate_roots(b):
                eng.wait_ge(q_ready, b + 1)
                eng.activation(r_f, r_f, ACT.Sqrt).then_inc(root_done, 1)

            def copy_c(half):
                for m in range(CT):
                    ps, free = tile(("c", CT * half + m))
                    if half:
                        eng.wait_ge(conv_done, m + 1)
                    eng.activation(cpad[:, m, 1:1 + NP_TOK], ps[:, 0:NP_TOK], ACT.Copy)
                    eng.activation(cpad[:, m, 2 + NP_TOK:].rearrange("p (r q) -> p r q", r=ROWS)[:, :, 0:GRID_W],
                                   ps[:, NP_TOK:T].rearrange("p (r q) -> p r q", r=ROWS), ACT.Copy)\
                        .then_inc(free, 1)
                    feed_behind("c", CT * half + m)

            def gelus(half):
                for m in range(CT):
                    k = CT * half + m
                    ps, free = tile(("g", k))
                    if k >= 2:
                        eng.wait_ge(hg_ready, k - 1)
                    else:
                        eng.wait_ge(xc_ready, KD)
                    eng.activation(gtmp[:, k % 2, :], ps[:, 0:T], ACT.Gelu_apprx_tanh).then_inc(free, 1)
                    feed_behind("g", k)

            def follow(kind, half):
                for m in range(CT):
                    feed_behind(kind, CT * half + m)

            for h in range(4):
                copy_xr(h)
            gate_sigmoids(0)
            gate_exps(0)
            copy_xr(4)
            copy_xr(5)
            gate_roots(0)
            copy_xr(6)
            copy_xr(7)
            gate_sigmoids(1)
            gate_exps(1)
            feed_behind("c", 0)
            gate_roots(1)
            copy_c(0)
            follow("v", 0)
            gate_sigmoids(2)
            gate_exps(2)
            feed_behind("g", 0)
            gate_roots(2)
            gelus(0)
            copy_c(1)
            gate_sigmoids(3)
            gate_exps(3)
            feed_behind("b", 0)
            gate_roots(3)
            follow("b", 0)
            follow("v", 1)
            follow("b", 1)
            gelus(1)
            eng.wait_ge(batch_done, 4)
            for kind, dst in (("ma", SA), ("mb", SB)):
                for k in range(KD):
                    ps, free = tile((kind, k))
                    eng.activation(dst[:, k, :], ps[:, 0:T], ACT.Sigmoid).then_inc(free, 1)
                    feed_behind(kind, k)
                    if kind == "mb":
                        eng.wait_ge(hg_ready, KD)
                        eng.activation(hs_hl[:, 0, k, :], hs[:, k, :], ACT.Copy).then_inc(act_hi, 1)
            eng.wait_ge(hs_split, KD)
            rows_of(x_rows[:, 0, :], x_prompt[0], x_again)
            rows_of(x_rows[:, 1:TT, :], x_sample[0].rearrange("(t p) d -> p t d", p=P), x_again)
            for k in range(KD):
                feed_behind("yb", k)
                if k == 2:
                    for kk in range(KD):
                        wait_read(eng, ("b", kk))
                        eng.activation(h_hl[:, 0, kk, :], ya_in[:, kk, :], ACT.Copy).then_inc(act_hi, 1)
            follow("ya", 0)
            follow("ya", 1)
            for cnd in range(2):
                eng.dma_start(A2[:, cnd, :], g_norm2[0].partition_broadcast(P)).then_inc(gn2_in, 16)
            eng.dma_start(gfin, g_final.partition_broadcast(P)).then_inc(gfin_in, 16)
            eng.wait_ge(ya_split, KD)
            bias_row(4)
            bias_row(5)
            for j in range(4, 12):
                ada_copies(j)
                if j > 4:
                    ada_rows_of(eng, j - 1, 0)
            ada_rows_of(eng, 11, 0)
            ps, free = tile(("state",))
            eng.activation(st_sb, ps[0:16, 0:P], ACT.Copy).then_inc(free, 1)
            wait_read(eng, ("state",))
            eng.dma_start(state_new[0, 0].rearrange("d (k p) -> (d k) p", p=P), st_sb)\
                .then_inc(state_out, 16)

            def route_copies(t):
                for half in range(2):
                    ps, free = tile(("h2T", t, half))
                    if half == 0 and t >= 1:
                        wait_tile(eng, ("route", t - 1))
                    eng.activation(h2T[:, 4 * half:4 * half + 4, :].rearrange("p k t -> p (k t)"),
                                   ps[:, :], ACT.Copy).then_inc(free, 1)

            def norm_rows(t):
                eng.wait_ge(x1_ready, t + 1)
                eng.activation(row_junk, x_rows[:, t, :], ACT.Square, accum_out=stat[:, 1, 0, t:t + 1])\
                    .then_inc(ssq_ready, 1)
                eng.wait_ge(mean_ready, t + 2)
                eng.activation(stat[:, 1, 2, t:t + 1], stat[:, 1, 1, t:t + 1], ACT.Sqrt)\
                    .then_inc(rms_ready, 1)
                eng.wait_ge(h2_ready, t + 1)
                eng.dma_start(h2_dram[t * P:(t + 1) * P, :], h2[:, t % 2, :]).then_inc(h2_out[t], 16)

            def top_exps(t):
                eng.wait_ge(tops_ready, t + 1)
                eng.activation(rt[:, t, 0:NG], lg[:, t, 0:NG], ACT.Exp, bias=rt[:, t, 32:33],
                               accum_out=rt[:, t, 33:34])
                eng.activation(rt[:, t, 34:35], rt[:, t, 35:36], ACT.Exp).then_inc(texp_ready, 1)

            norm_rows(0)
            route_copies(0)
            norm_rows(1)
            top_exps(0)
            route_copies(1)
            norm_rows(2)
            top_exps(1)
            route_copies(2)
            top_exps(2)

            def transposed(e, s):
                eng.wait_ge(xg_used, e + 1)
                eng.activation(xgT[:, s, 0:4, :].rearrange("p k t -> p (k t)"), bank[0][:, 0:4 * CAP],
                               ACT.Copy).then_inc(xgT_a, 1)

            def expert_pair(i, first, last):
                for s in range(2):
                    e = i * 2 + s
                    eng.wait_ge(up_done, e + 1)
                    eng.activation(sil, bank[2][:, 0:JF * CAP], ACT.Silu).then_inc(silu_done, 1)
                    if not (last and s == 1):
                        transposed(e + 1, 1 - s)
                    eng.wait_ge(down_done, e + 1)
                    if not first:
                        eng.wait_ge(y_out[s], i * 16)
                    eng.activation(y_sb[0:CAP, s, 0:512], bank[4][0:CAP, :], ACT.Copy).then_inc(y_a, 1)
                    eng.wait_ge(y_a, e + 1)
                    eng.wait_ge(y_v, e + 1)
                    eng.dma_start(y_rows[e, 0:CAP, :], y_sb[0:CAP, s, :]).then_inc(y_out[s], 16)

            transposed(0, 0)
            expert_pair(0, True, False)
            with eng.Fori(1, PAIRS - 1) as i:
                expert_pair(i, False, False)
            expert_pair(PAIRS - 1, False, True)

            eng.wait_ge(flag_ready, 1)
            most = eng.value_load(flag[0:1, 0:1], min_val=0, max_val=T)
            with eng.If(most > CAP):
                with eng.Fori(0, NE) as e:
                    for b in range(OB):
                        eng.wait_ge(o_trans, e * OB + b + 1)
                        eng.activation(oxgT[:, 0:4, b * OC:(b + 1) * OC],
                                       bank[0][:, 0:4 * OC].rearrange("p (k t) -> p k t", k=4),
                                       ACT.Copy).then_inc(o_xgT, 1)
                    for j in range(JF):
                        eng.wait_ge(o_prod, e * (2 * JF) + 2 * j + 1)
                        eng.wait_ge(o_z, e * JF + j + 1)
                        eng.activation(osil, bank[2][:, 0:OT], ACT.Silu).then_inc(o_silu, 1)
                    for b in range(OB):
                        eng.wait_ge(o_down, e * OB + b + 1)
                        eng.activation(oy[0:OC, 0:512], bank[4][0:OC, :], ACT.Copy).then_inc(o_y, 1)
                        eng.wait_ge(o_y, e * (2 * OB) + 2 * b + 3)
                        eng.dma_start(oy_rows[e, b * OC:(b + 1) * OC, :], oy[0:OC, :]).then_inc(o_yout, 16)
                        eng.wait_ge(o_yout, e * (16 * OB) + 16 * b + 16)
                    eng.sem_inc(o_end, 1)

            for t in range(TT):
                eng.wait_ge(res_ready, t + 1)
                eng.activation(o_junk, x_rows[:, t, :], ACT.Square, accum_out=stat[:, 2, 0, t:t + 1])\
                    .then_inc(ssq_ready, 1)
                eng.wait_ge(mean_ready, TT + t + 2)
                eng.activation(stat[:, 2, 2, t:t + 1], stat[:, 2, 1, t:t + 1], ACT.Sqrt)\
                    .then_inc(rms_ready, 1)
                eng.wait_ge(out_ready, t + 1)
                dst = y_prompt[0] if t == 0 else y_sample[0, (t - 1) * P:t * P, :]
                eng.dma_start(dst, o_rows[:, t % 2, :]).then_inc(out_sent[t], 16)
            for t in range(TT):
                eng.wait_ge(out_sent[t], 16)
            eng.wait_ge(state_out, 16)

        @block.vector
        def _(eng):
            steps = [0]

            def then(ins):
                ins.then_inc(step_v, 1)
                steps[0] += 1
                eng.wait_ge(step_v, steps[0])

            def tile(name):
                n = N_OF[name]
                eng.wait_ge(tile_done, n + 1)
                return bank[n % BANKS], bank_free[n % BANKS]

            eng.memset(cpad, 0.0).then_inc(pads_zero, 1)
            eng.memset(lg[:, :, :], -3.0e38)

            def mean_square(norm, sl):
                eng.tensor_scalar(stat[:, norm, 1, sl], stat[:, norm, 0, sl], 1.0 / D, EPS,
                                  ALU.mult, ALU.add).then_inc(mean_ready, 1)

            eng.wait_ge(ssq_ready, TT)
            mean_square(0, slice(0, TT))
            eng.wait_ge(rms_ready, 1)
            then(eng.reciprocal(stat[:, 0, 0, :], stat[:, 0, 2, :]))
            for t in range(TT):
                eng.tensor_scalar(xs[:, t, :], x_in_rows[:, t, :], stat[:, 0, 0, t:t + 1], None, ALU.mult)\
                    .then_inc(xs_ready, 1)
            for j, (a, b) in enumerate(((0, NPA), (NPA, NPAR))):
                ps, free = tile(("par", j))
                eng.tensor_copy(pT[:, a:b], ps[:, 0:b - a]).then_inc(free, 1)
                wait_read(eng, ("par", j))

            eng.memset(xrp[:, :, :], 0.0).then_inc(pads_zero, 1)
            eng.wait_ge(cvec_ready, 2)
            eng.wait_ge(consts, 2)
            eng.tensor_scalar(cst_all[:, 4 * KD:], ones[:, :], 0.0, None, ALU.mult)
            eng.tensor_tensor(cst[:, :, 2:4], cvec[:, :, :], cst[:, :, 0:2].bitcast(F32), ALU.subtract)\
                .then_inc(cvec_ready, 1)

            eng.wait_ge(lam_exp, 1)
            then(eng.tensor_scalar(sp[:, 2, :], sp[:, 1, :], 2.0, None, ALU.add))
            then(eng.reciprocal(sp[:, 3, :], sp[:, 2, :]))
            then(eng.tensor_tensor(sp[:, 2, :], sp[:, 1, :], sp[:, 3, :], ALU.mult))
            then(eng.tensor_tensor(sp[:, 3, :], sp[:, 2, :], sp[:, 2, :], ALU.mult))
            then(eng.tensor_scalar(sp[:, 4, :], sp[:, 3, :], 1.0 / 17, None, ALU.mult))
            for odd in (15, 13, 11, 9, 7, 5, 3):
                then(eng.scalar_tensor_tensor(out=sp[:, 4, :], in0=sp[:, 4, :], scalar=1.0 / odd,
                                              in1=sp[:, 3, :], op0=ALU.add, op1=ALU.mult))
            then(eng.scalar_tensor_tensor(out=sp[:, 4, :], in0=sp[:, 4, :], scalar=1.0,
                                          in1=sp[:, 2, :], op0=ALU.add, op1=ALU.mult))
            then(eng.tensor_scalar(sp[:, 5, :], pT[:, LAM:NPAR], -1.0, 0.0, ALU.mult, ALU.max))
            then(eng.scalar_tensor_tensor(out=sp[:, 5, :], in0=sp[:, 4, :], scalar=2.0,
                                          in1=sp[:, 5, :], op0=ALU.mult, op1=ALU.add))
            eng.tensor_scalar(rate[:, 0, :], sp[:, 5, :], -RG_C, None, ALU.mult)
            eng.tensor_scalar(rate[:, 1, :], sp[:, 5, :], RG_C, None, ALU.mult).then_inc(rate_ready, 1)

            eng.wait_ge(consts, 6)
            eng.tensor_tensor(selc[:, :], ident[0:5, 0:2], ident[0:5, 2:4], ALU.add).then_inc(selectors, 1)
            eng.wait_ge(selectors, 1)
            eng.tensor_scalar(selv[:, :], selc[:, :], ident[0:5, 4:5], None, ALU.add).then_inc(selectors, 1)
            eng.wait_ge(selectors, 2)
            for cnd in range(2):
                eng.tensor_scalar(selb[:, cnd, :], ones[0:5, :], selv[:, cnd:cnd + 1], None, ALU.mult)\
                    .then_inc(selectors, 1)

            def ada_lo(j, ms):
                for m in ms:
                    write_lo(eng, 4 * C_OF[("ada", j)] + m, lo_v)

            def ada_columns(j):
                ps, free = tile(("adaC", j))
                bias = pT[:, BADA + CT * j:BADA + CT * (j + 1)]
                for cnd in range(2):
                    last = eng.tensor_tensor(
                        mod[:, CT * j:CT * (j + 1), cnd],
                        ps[:, 0:2 * CT].rearrange("p (m c) -> p m c", c=2)[:, :, cnd], bias, ALU.add)
                last.then_inc(free, 1)

            for j in range(4):
                ada_lo(j, range(0, 2))
                if j >= 2:
                    ada_columns(j - 2)
                ada_lo(j, range(2, CT))
            ada_columns(2)
            ada_columns(3)
            for j in range(4):
                wait_read(eng, ("adaC", j))
            for cnd in range(2):
                last = eng.scalar_tensor_tensor(out=A1[:, :, cnd], in0=mod[:, KD:2 * KD, cnd], scalar=1.0,
                                                in1=pT[:, GN1:GN1 + KD], op0=ALU.add, op1=ALU.mult)
            then(last)
            for k in range(KD):
                wait_read(eng, ("xT", k))
                for cnd, (a, b) in enumerate(((0, NP_TOK), (NP_TOK, T))):
                    last = eng.tensor_scalar(xTr[:, k, a:b], xTr[:, k, a:b], A1[:, k, cnd:cnd + 1],
                                             mod[:, k, cnd:cnd + 1], ALU.mult, ALU.add)
                last.then_inc(h_whole, 1)

            def split_lo(x_hl, x, k, count, done):
                eng.wait_ge(act_hi, count)
                eng.tensor_tensor(x_hl[:, 1, k, :], x[:, k, :], x_hl[:, 0, k, :].bitcast(F32), ALU.subtract)\
                    .then_inc(done, 1)

            for k in range(KD):
                eng.wait_ge(h_whole, k + 1)
                split_lo(h_hl, xTr, k, k + 1, h_ready)

            def conv_rnn(h):
                wait_read(eng, ("xr", h))
                src = xrp[:, h % 2, :]
                then(eng.tensor_scalar(xc[:, h, :], src[:, 0:TG], pT[:, RCW + h:RCW + h + 1],
                                       pT[:, RCB + h:RCB + h + 1], ALU.mult, ALU.add))
                for tap in range(1, 4):
                    col = RCW + tap * KD + h
                    ins = eng.scalar_tensor_tensor(out=xc[:, h, :], in0=src[:, tap:tap + TG],
                                                   scalar=pT[:, col:col + 1], in1=xc[:, h, :],
                                                   op0=ALU.mult, op1=ALU.add)
                    if tap < 3:
                        then(ins)
                ins.then_inc(xc_ready, 1)

            def gate_inputs(b):
                for h in (2 * b, 2 * b + 1):
                    for d in range(2):
                        n = N_OF[("gate", h, d, 1)]
                        eng.wait_ge(bank_free[n % BANKS], n // BANKS + 1)
                eng.wait_ge(xc_ready, 2 * b + 2)
                for d in range(2):
                    eng.tensor_tensor(i_b[:, d, :, :], i_b[:, d, :, :], xc[:, 2 * b:2 * b + 2, :], ALU.mult)
                eng.wait_ge(exp_done, 8 * (b + 1))
                then(eng.tensor_tensor(q_f, a_f, a_f, ALU.mult))
                eng.scalar_tensor_tensor(out=r_f, in0=q_f, scalar=1.0, in1=r_f, op0=ALU.add,
                                         op1=ALU.mult).then_inc(q_ready, 1)

            def scans(b):
                eng.wait_ge(root_done, b + 1)
                then(eng.tensor_tensor(i_f, i_f, r_f, ALU.mult))
                eng.memset(a_b[:, :, :, NP_TOK:S0], 0.0)
                then(eng.memset(i_b[:, :, :, NP_TOK:S0], 0.0))
                then(eng.tensor_copy(i_b[:, 0, :, S0 - 1], pT[:, STF + 2 * b:STF + 2 * b + 2]))
                for hh in range(2):
                    h = 2 * b + hh
                    eng.tensor_tensor_scan(r_b[:, 0, hh, :], a_b[:, 0, hh, :], i_b[:, 0, hh, :], 0.0,
                                           ALU.mult, ALU.add)
                    last = eng.tensor_tensor_scan(r_b[:, 1, hh, ::-1], a_b[:, 1, hh, ::-1],
                                                  i_b[:, 1, hh, ::-1], pT[:, STB + h:STB + h + 1],
                                                  ALU.mult, ALU.add)
                then(last)
                for a, z0, n in ((0, 0, NP_TOK), (NP_TOK, S0, NS_TOK)):
                    eng.tensor_tensor(hs[:, 2 * b:2 * b + 2, a:a + n], r_b[:, 0, :, z0:z0 + n],
                                      r_b[:, 1, :, z0:z0 + n], ALU.add)
                eng.tensor_copy(stc[:, 2 * b:2 * b + 2], r_b[:, 0, :, NP_TOK - 1])
                eng.tensor_copy(stc[:, KD + 2 * b:KD + 2 * b + 2], r_b[:, 1, :, 0]).then_inc(batch_done, 1)

            def conv_grid(half):
                for m in range(CT):
                    k = CT * half + m
                    n = N_OF[("c", k)]
                    eng.wait_ge(bank_free[n % BANKS], n // BANKS + 1)
                    ps, free = tile(("v", k))
                    src = cpad[:, m, :]
                    grid = src[:, 2 + NP_TOK:].rearrange("p (r q) -> p r q", r=ROWS)[:, :, 0:GRID_W]
                    eng.tensor_tensor(src[:, 1:1 + NP_TOK], ps[:, 0:NP_TOK], src[:, 1:1 + NP_TOK], ALU.mult)
                    eng.tensor_tensor(grid, ps[:, NP_TOK:T].rearrange("p (r q) -> p r q", r=ROWS), grid,
                                      ALU.mult).then_inc(free, 1)
                    eng.wait_ge(free, N_OF[("v", k)] // BANKS + 1)
                    if half:
                        wait_read(eng, ("b", m))
                    dst = ycv[:, m, 0:CG - 2]
                    then(eng.tensor_scalar(dst, src[:, 0:CG - 2], pT[:, CVW + k:CVW + k + 1], None, ALU.mult))
                    for tap in range(1, 3):
                        col = CVW + tap * KD + k
                        ins = eng.scalar_tensor_tensor(out=dst, in0=src[:, tap:tap + CG - 2],
                                                       scalar=pT[:, col:col + 1], in1=dst,
                                                       op0=ALU.mult, op1=ALU.add)
                        if tap < 2:
                            then(ins)
                    ins.then_inc(conv_done, 1)

            def times_b(half):
                for m in range(CT):
                    k = CT * half + m
                    eng.wait_ge(conv_done, k + 1)
                    ps, free = tile(("b", k))
                    y = ycv[:, m, :]
                    eng.tensor_tensor(ya_in[:, k, 0:NP_TOK], ps[:, 0:NP_TOK], y[:, 0:NP_TOK], ALU.mult)
                    eng.tensor_tensor(
                        ya_in[:, k, NP_TOK:T].rearrange("p (r q) -> p r q", r=ROWS),
                        ps[:, NP_TOK:T].rearrange("p (r q) -> p r q", r=ROWS),
                        y[:, 1 + NP_TOK:1 + NP_TOK + ROWS * (GRID_W + 1)]
                        .rearrange("p (r q) -> p r q", r=ROWS)[:, :, 0:GRID_W], ALU.mult)\
                        .then_inc(free, 1)

            def times_gelu(half):
                for m in range(CT):
                    k = CT * half + m
                    n = N_OF[("g", k)]
                    eng.wait_ge(bank_free[n % BANKS], n // BANKS + 1)
                    eng.wait_ge(batch_done, k // 2 + 1)
                    eng.tensor_tensor(hs[:, k, :], hs[:, k, :], gtmp[:, k % 2, :], ALU.mult)\
                        .then_inc(hg_ready, 1)

            for h in range(4):
                conv_rnn(h)
            gate_inputs(0)
            conv_rnn(4)
            scans(0)
            for h in range(5, KD):
                conv_rnn(h)
            gate_inputs(1)
            scans(1)
            conv_grid(0)
            gate_inputs(2)
            scans(2)
            times_gelu(0)
            gate_inputs(3)
            scans(3)
            times_b(0)
            conv_grid(1)
            times_b(1)
            times_gelu(1)
            for k in range(KD):
                eng.wait_ge(hg_ready, k + 1)
                split_lo(hs_hl, hs, k, KD + k + 1, hs_split)
            for k in range(KD):
                ps, free = tile(("yb", k))
                wait_read(eng, ("mb", k))
                eng.tensor_tensor(SB[:, k, :], ps[:, 0:T], SB[:, k, :], ALU.mult).then_inc(free, 1)
                if k == 2:
                    for kk in range(KD):
                        split_lo(h_hl, ya_in, kk, 2 * KD + kk + 1, ya_split)
            for k in range(KD):
                ps, free = tile(("ya", k))
                wait_read(eng, ("ma", k))
                eng.tensor_tensor(SA[:, k, :], ps[:, 0:T], SA[:, k, :], ALU.mult).then_inc(free, 1)
                wait_read(eng, ("ya", k))
                wait_read(eng, ("yb", k))
                eng.tensor_tensor(SA[:, k, :], SA[:, k, :], SB[:, k, :], ALU.add).then_inc(merged_ready, 1)
            eng.wait_ge(gn2_in, 32)
            for j in range(4, 12):
                ada_lo(j, range(0, 2))
                if j >= 6:
                    ada_rows_of(eng, j - 2, 1)
                ada_lo(j, range(2, CT))
            ada_rows_of(eng, 10, 1)
            ada_rows_of(eng, 11, 1)

            def residual(t):
                cnd = 0 if t == 0 else 1
                for half in range(2):
                    cols = slice(half * CW, (half + 1) * CW)
                    ps, free = tile(("wo", t, half))
                    eng.tensor_tensor(wo_tmp, ps[:, :], G1[:, cnd, cols], ALU.mult).then_inc(free, 1)
                    eng.wait_ge(free, N_OF[("wo", t, half)] // BANKS + 1)
                    ins = eng.tensor_tensor(x_rows[:, t, cols], x_rows[:, t, cols], wo_tmp, ALU.add)
                    if half == 0:
                        then(ins)
                ins.then_inc(x1_ready, 1)
                eng.wait_ge(ssq_ready, TT + t + 1)
                mean_square(1, slice(t, t + 1))

            def norm2(t):
                cnd = 0 if t == 0 else 1
                eng.wait_ge(rms_ready, t + 2)
                then(eng.reciprocal(stat[:, 1, 0, t:t + 1], stat[:, 1, 2, t:t + 1]))
                if t >= 2:
                    eng.wait_ge(h2_out[t - 2], 16)
                    eng.wait_ge(tile_done, N_OF[("h2T", t - 2, 1)] + 1)
                then(eng.scalar_tensor_tensor(out=h2[:, t % 2, :], in0=x_rows[:, t, :],
                                              scalar=stat[:, 1, 0, t:t + 1], in1=A2[:, cnd, :],
                                              op0=ALU.mult, op1=ALU.mult))
                eng.tensor_tensor(h2[:, t % 2, :], h2[:, t % 2, :], B2[:, cnd, :], ALU.add)\
                    .then_inc(h2_ready, 1)

            def choose(t):
                r, u = rt[:, t, :], rti[:, t, :]
                ps, free = tile(("route", t))
                eng.wait_ge(bias_in, 32)
                eng.tensor_tensor(lg[:, t, 0:NG], ps[:, 0:NG], br[:, 0:NG], ALU.add)
                eng.tensor_tensor(le[:, t, :], ps[:, NG:NG + NE], br[:, NG:], ALU.add).then_inc(free, 1)
                wait_read(eng, ("route", t))
                then(eng.max(r[:, 8:16], lg[:, t, :]))
                then(eng.max_index(u[:, 0:8], r[:, 8:16], lg[:, t, :]))
                then(eng.tensor_copy(r[:, 36:37], u[:, 0:1]))
                then(eng.tensor_scalar(r[:, 40:40 + NG], iota[:, 0:NG], r[:, 36:37], None, ALU.is_equal))
                then(eng.tensor_scalar(r[:, 16:24], le[:, t, 0:EG], r[:, 40:41], None, ALU.mult))
                for g in range(1, NG):
                    then(eng.scalar_tensor_tensor(out=r[:, 16:24], in0=le[:, t, g * EG:(g + 1) * EG],
                                                  scalar=r[:, 40 + g:41 + g], in1=r[:, 16:24],
                                                  op0=ALU.mult, op1=ALU.add))
                then(eng.max(r[:, 24:32], r[:, 16:24]))
                then(eng.max_index(u[:, 8:16], r[:, 24:32], r[:, 16:24]))
                eng.tensor_scalar(r[:, 32:33], r[:, 8:9], -1.0, None, ALU.mult)
                eng.tensor_tensor(r[:, 35:36], r[:, 25:26], r[:, 24:25], ALU.subtract)\
                    .then_inc(tops_ready, 1)
                eng.tensor_scalar(r[:, 37:38], r[:, 36:37], float(EG), None, ALU.mult)
                then(eng.tensor_copy(r[:, 44:46], u[:, 8:10]))
                then(eng.tensor_scalar(r[:, 46:48], r[:, 44:46], r[:, 37:38], None, ALU.add))
                for k in range(2):
                    last = eng.tensor_scalar(pick[:, t, k, :], iota[:, 0:NE], r[:, 46 + k:47 + k], None,
                                             ALU.is_equal)
                then(last)
                eng.tensor_tensor(both[:, t, :], pick[:, t, 0, :], pick[:, t, 1, :], ALU.add)\
                    .then_inc(both_ready, 1)
                for k in range(2):
                    last = eng.tensor_scalar(tok_oh[:, t, k, :], pick[:, t, k, :], tok[:, t:t + 1], None,
                                             ALU.mult)

            def weights(t):
                r = rt[:, t, :]
                eng.wait_ge(texp_ready, t + 1)
                then(eng.tensor_scalar(r[:, 48:49], r[:, 34:35], 1.0, None, ALU.add))
                then(eng.tensor_tensor(r[:, 49:50], r[:, 48:49], r[:, 33:34], ALU.mult))
                then(eng.reciprocal(wts[:, t, 0:1], r[:, 49:50]))
                then(eng.tensor_tensor(wts[:, t, 1:2], wts[:, t, 0:1], r[:, 34:35], ALU.mult))

            def place(t):
                ps, free = tile(("rank", t))
                for k in range(2):
                    ins = eng.tensor_tensor(rank_m[:, k, :], ps[:, 0:NE], pick[:, t, k, :], ALU.mult)
                ins.then_inc(free, 1)
                wait_read(eng, ("rank", t))
                then(eng.reduce_sum(rank[:, t, :], rank_m[:, :, :], AX_X))
                for k in range(2):
                    last = eng.tensor_scalar(rank_oh[:, t, k, :], iota[:, 0:CAP], rank[:, t, k:k + 1],
                                             None, ALU.is_equal)
                last.then_inc(onehots_ready, 1)

            def slots(t):
                eng.scalar_tensor_tensor(out=main_w[:, t, :], in0=rank[:, t, :], scalar=float(CAP),
                                         in1=wts[:, t, :], op0=ALU.is_lt, op1=ALU.mult)
                then(eng.tensor_scalar(slot_f[:, t, :], rank[:, t, :], float(CAP - 1), None, ALU.min))
                then(eng.scalar_tensor_tensor(out=slot_f[:, t, :], in0=rt[:, t, 46:48], scalar=float(CAP),
                                              in1=slot_f[:, t, :], op0=ALU.mult, op1=ALU.add))
                eng.tensor_copy(slot_u[:, t, :], slot_f[:, t, :]).then_inc(slots_ready, 1)

            for j in range(4, 12):
                for cnd in range(2):
                    wait_read(eng, ("adaB", j, cnd))
            eng.wait_ge(x_again, 32)
            eng.wait_ge(consts, 6)
            residual(0)
            norm2(0)
            residual(1)
            norm2(1)
            choose(0)
            residual(2)
            norm2(2)
            choose(1)
            place(0)
            choose(2)
            place(1)
            place(2)
            ps, free = tile(("count",))
            eng.reduce_max(cmax[:, :], ps[:, 0:NE], AX_X).then_inc(free, 1)
            wait_read(eng, ("count",))
            eng.tensor_copy(flag[:, :], cmax[:, :]).then_inc(flag_ready, 1)
            ps, free = tile(("list",))
            eng.tensor_copy(lists[:, :], ps[0:CAP, 0:NE]).then_inc(free, 1)
            for t in range(TT):
                weights(t)
                slots(t)

            def transposed(e, s):
                eng.wait_ge(xg_used, e + 1)
                eng.tensor_copy(xgT[:, s, 4:8, :].rearrange("p k t -> p (k t)"), bank[1][:, 0:4 * CAP])\
                    .then_inc(xgT_v, 1)

            def expert_pair(i, first, last):
                for s in range(2):
                    e = i * 2 + s
                    eng.wait_ge(silu_done, e + 1)
                    eng.wait_ge(gate_done, e + 1)
                    eng.tensor_tensor(z[:, s, :], bank[3][:, 0:JF * CAP], sil, ALU.mult).then_inc(z_ready, 1)
                    if not (last and s == 1):
                        transposed(e + 1, 1 - s)
                    eng.wait_ge(down_done, e + 1)
                    if not first:
                        eng.wait_ge(y_out[s], i * 16)
                    eng.tensor_copy(y_sb[0:CAP, s, 512:D], bank[5][0:CAP, :]).then_inc(y_v, 1)

            transposed(0, 0)
            expert_pair(0, True, False)
            with eng.Fori(1, PAIRS - 1) as i:
                expert_pair(i, False, False)
            expert_pair(PAIRS - 1, False, True)

            eng.wait_ge(gfin_in, 16)

            def add_experts(t, w, done, then):
                y0, y1 = yg[:, t % 2, 0, :], yg[:, t % 2, 1, :]
                then(eng.tensor_scalar(y0, y0, w[:, t, 0:1], None, ALU.mult))
                then(eng.scalar_tensor_tensor(out=y0, in0=y1, scalar=w[:, t, 1:2], in1=y0,
                                              op0=ALU.mult, op1=ALU.add))
                then(eng.tensor_tensor(y0, y0, G2[:, 0 if t == 0 else 1, :], ALU.mult))
                eng.tensor_tensor(x_rows[:, t, :], x_rows[:, t, :], y0, ALU.add).then_inc(done, 1)

            eng.wait_ge(flag_ready, 1)
            most = eng.value_load(flag[0:1, 0:1], min_val=0, max_val=T)
            with eng.If(most > CAP):
                for b in range(OB):
                    for t in range(TT):
                        for k in range(2):
                            n = (b * TT + t) * 2 + k
                            if n:
                                eng.wait_ge(o_table, n)
                            eng.tensor_scalar(orank[:, b * OC:(b + 1) * OC],
                                              iota[:, CAP + b * OC:CAP + (b + 1) * OC],
                                              rank[:, t, k:k + 1], None, ALU.is_equal)\
                                .then_inc(o_onehot, 1)
                eng.wait_ge(o_table, OB * TT * 2)
                eng.tensor_copy(olist_f, bank[0][0:OC, 0:OB * NE])\
                    .then_inc(o_list, 1)
                eng.wait_ge(o_list, 1)
                eng.sem_inc(o_end, 1)
                eng.sem_inc(o_xgT, 1)
                eng.sem_inc(o_z, 1)
                eng.sem_inc(o_y, 1)
                with eng.Fori(0, NE) as e:
                    for b in range(OB):
                        eng.wait_ge(o_xgT, e * (2 * OB) + 2 * b + 2)
                        eng.tensor_copy(oxgT[:, 4:8, b * OC:(b + 1) * OC],
                                        bank[1][:, 0:4 * OC].rearrange("p (k t) -> p k t", k=4))\
                            .then_inc(o_xgT, 1)
                    for j in range(JF):
                        eng.wait_ge(o_silu, e * JF + j + 1)
                        eng.wait_ge(o_prod, e * (2 * JF) + 2 * j + 2)
                        eng.tensor_tensor(oz[:, j, :], bank[3][:, 0:OT], osil, ALU.mult).then_inc(o_z, 1)
                    for b in range(OB):
                        eng.wait_ge(o_y, e * (2 * OB) + 2 * b + 2)
                        eng.tensor_copy(oy[0:OC, 512:D], bank[5][0:OC, :]).then_inc(o_y, 1)
                o_steps = [0]

                def then_o(ins):
                    ins.then_inc(step_o, 1)
                    o_steps[0] += 1
                    eng.wait_ge(step_o, o_steps[0])

                for t in range(TT):
                    then_o(eng.tensor_scalar(oslot_f[:, t, :], rank[:, t, :], float(CAP), 0.0,
                                           ALU.subtract, ALU.max))
                    then_o(eng.scalar_tensor_tensor(out=oslot_f[:, t, :], in0=rt[:, t, 46:48],
                                                  scalar=float(OT), in1=oslot_f[:, t, :],
                                                  op0=ALU.mult, op1=ALU.add))
                    then_o(eng.scalar_tensor_tensor(out=over_w[:, t, :], in0=rank[:, t, :],
                                                  scalar=float(CAP), in1=wts[:, t, :],
                                                  op0=ALU.is_ge, op1=ALU.mult))
                eng.tensor_copy(oslot_u, oslot_f[:, :, :]).then_inc(o_slots, 1)
                for t in range(TT):
                    eng.wait_ge(o_yg_in[t], 32)
                    add_experts(t, over_w, o_added, then_o)

            for t in range(TT):
                eng.wait_ge(yg_in[t], 32)
                add_experts(t, main_w, res_ready, then)
                eng.wait_ge(ssq_ready, 2 * TT + t + 1)
                mean_square(2, slice(t, t + 1))
                eng.wait_ge(rms_ready, TT + t + 2)
                then(eng.reciprocal(stat[:, 2, 0, t:t + 1], stat[:, 2, 2, t:t + 1]))
                if t >= 2:
                    eng.wait_ge(out_sent[t - 2], 16)
                eng.scalar_tensor_tensor(out=o_rows[:, t % 2, :], in0=x_rows[:, t, :],
                                         scalar=stat[:, 2, 0, t:t + 1], in1=gfin,
                                         op0=ALU.mult, op1=ALU.mult).then_inc(out_ready, 1)


_INS = ['x_prompt', 'x_sample', 'state_rnn', 'c', 'c_ctx', 'w_ada', 'b_ada', 'g_norm1', 'g_norm2', 'w_in',
        'conv_w', 'w_conv_out', 'rnn_conv_w', 'rnn_conv_b', 'w_gate_a', 'b_gate_a', 'w_gate_x',
        'b_gate_x', 'lam', 'w_rnn_out', 'w_o', 'w_router_group', 'b_router_group', 'w_router_expert',
        'b_router_expert', 'w1', 'w3', 'w2', 'g_final']


def kernel(**inputs):
    import numpy as _np
    import concourse.bacc as _bacc
    from concourse import mybir as _mybir
    from concourse.bass_utils import run_bass_kernel_spmd as _run

    nc = _bacc.Bacc("TRN2", target_bir_lowering=False, num_devices=1)
    arrays, args = {}, []
    for name in _INS:
        a = _np.ascontiguousarray(inputs[name])
        arrays[f"in_{name}"] = a
        args.append(nc.dram_tensor(f"in_{name}", a.shape, _mybir.dt.from_np(a.dtype), kind="ExternalInput").ap())
    d = inputs["c"].shape[1]
    outs = [inputs["x_prompt"].shape, inputs["x_sample"].shape, (inputs["x_prompt"].shape[0], 1, 2, d)]
    for i, shape in enumerate(outs):
        args.append(nc.dram_tensor(f"out_{i}", shape, _mybir.dt.float32, kind="ExternalOutput").ap())
    layer_program(nc, *args)
    r = _run(nc, [arrays], core_ids=[0])
    return tuple(r.results[0][f"out_{i}"] for i in range(len(outs)))
```

```python
from contextlib import ExitStack

import concourse.bass as bass
from concourse import mybir

F32 = mybir.dt.float32
F32R = mybir.dt.float32r
U32 = mybir.dt.uint32
I32 = mybir.dt.int32
ALU = mybir.AluOpType
ACT = mybir.ActivationFunctionType
AX_X = mybir.AxisListType.X

P = 128
EPS = 1e-6
RG_C = 8.0
GRID_W = 64


def layer_program(nc, x_prompt, x_sample, state_rnn, c, c_ctx, w_ada, b_ada, g_norm1, g_norm2, w_in,
                  conv_w, w_conv_out, rnn_conv_w, rnn_conv_b, w_gate_a, b_gate_a, w_gate_x, b_gate_x,
                  lam, w_rnn_out, w_o, w_router_group, b_router_group, w_router_expert,
                  b_router_expert, w1, w3, w2, g_final, y_prompt, y_sample, state_new):
    D = w_o.shape[1]
    NP_TOK = x_prompt.shape[1]
    NS_TOK = x_sample.shape[1]
    T = NP_TOK + NS_TOK
    TT = T // P
    KD = D // P
    NG = w_router_group.shape[2]
    NE = w_router_expert.shape[2]
    EG = NE // NG
    FE = w1.shape[3]
    JF = FE // P
    assert NP_TOK == P and D == 1024 and FE == 512 and NS_TOK % GRID_W == 0

    CW = 512
    CT = CW // P
    SLOTS = 4
    MSLOTS = 6
    ASUBS = 5
    SUBS = 3
    QUART = KD * CW // 4
    BANKS = 6

    GAP = 3
    S0 = NP_TOK + GAP
    TG = S0 + NS_TOK
    ROWS = NS_TOK // GRID_W
    CG = 1 + NP_TOK + 1 + ROWS * (GRID_W + 1)

    CAP = 80
    OB = 4
    OC = (T - CAP) // OB
    OT = OB * OC
    assert CAP + OT == T
    FEW = 40

    BADA, CCTX, CSMP, GN1, GN2, STF, STB = 0, 48, 56, 64, 72, 80, 88
    CVW, RCW, RCB, BGA, BGX, LAM, NPAR = 96, 120, 152, 160, 176, 192, 208
    NPA = 96

    h2_dram = nc.dram_tensor("h2_rows", [T, D], F32).ap()
    y_dram = nc.dram_tensor("expert_rows", [NE * CAP, D], F32).ap()
    oy_dram = nc.dram_tensor("overflow_rows", [NE * OT, D], F32).ap()

    ada_v = w_ada[0].rearrange("(k p) n -> p k n", p=P)
    win_v = w_in[0].rearrange("(k p) n -> p k n", p=P)
    wco_v = w_conv_out[0].rearrange("(k p) n -> p k n", p=P)
    wro_v = w_rnn_out[0].rearrange("(k p) n -> p k n", p=P)
    wo_v = w_o[0].rearrange("(k p) n -> p k n", p=P)
    w1_v = w1[0].rearrange("e (p k) n -> e p (k n)", p=P)
    w3_v = w3[0].rearrange("e (p k) n -> e p (k n)", p=P)
    w2_v = w2[0].rearrange("e (j p) n -> e p j n", p=P)
    U_COL = {"b": 0, "c": D, "v": 2 * D, "xr": 3 * D, "g": 4 * D, "ma": 5 * D, "mb": 6 * D}

    stream, chunks = [], []

    def add_chunk(kind, half):
        chunks.append((kind, half))
        for m in range(CT):
            stream.append((kind, CT * half + m))

    def add_gates(b):
        for h in (2 * b, 2 * b + 1):
            for d in range(2):
                for x in range(2):
                    stream.append(("gate", h, d, x))

    WO_ON = [("wo", 0, 0), ("wo", 0, 1), ("wo", 1, 0), ("h2T", 0, 0), ("h2T", 0, 1), ("wo", 1, 1), ("route", 0),
             ("wo", 2, 0), ("h2T", 1, 0), ("h2T", 1, 1), ("wo", 2, 1), ("route", 1), ("rank", 0),
             ("h2T", 2, 0), ("h2T", 2, 1), ("route", 2), ("rank", 1), ("rank", 2), ("count",), ("list",)]
    assert TT == 3
    W_IN = [("xr", 0), 0, ("xr", 1), ("c", 0), 1, ("v", 0), ("b", 0), 2, ("g", 0), ("c", 1), 3, ("v", 1),
            ("b", 1), ("g", 1), ("ma", 0), ("ma", 1), ("mb", 0), ("mb", 1)]
    START = [("par", 0), ("par", 1), ("adaR", 0), ("xT", 0), ("xT", 1), ("xT", 2), ("xT", 3), ("adaR", 1),
             ("adaC", 0), ("xT", 4), ("xT", 5), ("xT", 6), ("xT", 7), ("adaR", 2), ("adaC", 1),
             ("adaR", 3), ("adaC", 2), ("adaC", 3)]
    stream += START
    chunks += [("ada", j) for j in range(4)]
    for item in W_IN:
        if isinstance(item, int):
            add_gates(item)
        else:
            add_chunk(*item)
    for kind in ("yb", "ya"):
        add_chunk(kind, 0)
        add_chunk(kind, 1)
    for j in range(4, 12):
        chunks.append(("ada", j))
        stream.append(("adaR", j))
        if j > 4:
            stream += [("adaB", j - 1, 0), ("adaB", j - 1, 1)]
    stream += [("adaB", 11, 0), ("adaB", 11, 1), ("state",)]
    NSPLIT = len(chunks)
    chunks += [("wo", 0), ("wo", 1)]
    stream += WO_ON
    N_OF = {s: n for n, s in enumerate(stream)}
    C_OF = {s: n for n, s in enumerate(chunks)}
    N1 = len(chunks)
    PAIRS = NE // 2
    assert len(N_OF) == len(stream) and N1 % SLOTS == 0

    with ExitStack() as ctx:
        def sb(name, shape, dt=F32):
            return ctx.enter_context(nc.sbuf_tensor(name, shape, dt))

        def sem(name):
            return ctx.enter_context(nc.semaphore(name))

        CHUNK = 4 * KD * CW
        PAD = P - CAP
        XW, ZW = KD * CAP + PAD, JF * CAP + PAD
        MHL = 4 * 2 * (XW + ZW)
        sizes = {"ring": SLOTS * CHUNK, "gw": CHUNK, "cp": 4 * 2 * 4 * CG, "ra": CHUNK + MHL,
                 "xcy": 4 * KD * TG, "hg": 4 * KD * T, "lru": 4 * 4 * 4 * TG, "xrp": 4 * 2 * (TG + 3),
                 "sub": SUBS * 2 * 4 * QUART}
        sizes = {name: -(-size // 32) * 32 for name, size in sizes.items()}
        arena = sb("arena", [P, sum(sizes.values()) // 4])
        base, at = {}, nc.sbuf_base - sum(sizes.values())
        for name, size in sizes.items():
            base[name] = at
            at += size

        def over(name, region, shape, dt=F32, offset=0):
            return nc.alloc_sbuf_tensor_at(name, shape, dt, offset=base[region] + offset)

        ring = over("ring", "ring", [P, SLOTS, KD * CW])
        gate_w = over("gate_w", "gw", [P, KD * CW])
        cp = over("cp", "cp", [P, 2 * 4 * CG])
        h_hl = over("h_hl", "ra", [P, 2, KD, T], F32R)
        mod_sb = over("mod_sb", "ra", [P, 3, 2, D])
        moe_hl = over("moe_hl", "ra", [P, 2, XW + ZW], F32R)
        slot5 = over("slot5", "ra", [P, KD * CW], offset=MHL)
        hs_hl = over("hs_hl", "gw", [P, 2, KD, T], F32R)
        assert 4 * 2 * KD * T <= sizes["ra"] and 8 * KD * T <= sizes["gw"] + sizes["cp"]
        xcy = over("xcy", "xcy", [P, KD * TG])
        hg = over("hg", "hg", [P, KD * T])
        lru = over("lru", "lru", [P, 4 * 4 * TG])
        xrp = over("xrp", "xrp", [P, 2, TG + 3])
        subs = over("subs", "sub", [P, SUBS, 2, QUART], F32R)
        subs_more = over("subs_more", "gw", [P, ASUBS - SUBS, 2, QUART], F32R)
        sub3 = over("sub3", "lru", [P, 2, QUART], F32R, offset=4 * (2 * D + 2 * FE))
        oh = sb("oh", [P, 2 * TT * 2 * NE + TT * NE + TT * 2 * CAP])
        pT = sb("pT", [P, NPAR])
        ident = sb("ident", [P, P])
        ones = sb("ones", [P, P])
        before = sb("before", [P, P])
        iota = sb("iota", [P, T])
        tok = sb("tok", [P, TT])
        cvec = sb("cvec", [P, KD, 2])
        cst_all = sb("cst", [P, 4 * KD + P], F32R)
        selc = sb("selc", [5, 2])
        selv = sb("selv", [5, 2])
        selb = sb("selb", [5, 2, P])
        mod = sb("mod", [P, 2 * KD, 2])
        A1 = sb("A1", [P, KD, 2])
        sp = sb("sp", [P, 6, 16])
        rate = sb("rate", [P, 2, 16])
        stc = sb("stc", [P, 16])
        stat = sb("stat", [P, 3, 3, TT])
        wr = sb("wr", [P, KD, NG + NE])
        br = sb("br", [P, NG + NE])
        lg = sb("lg", [P, TT, 8])
        rt = sb("rt", [P, TT, 64])
        rti = sb("rti", [P, TT, 16], U32)
        rank = sb("rank", [P, TT, 2])
        wts = sb("wts", [P, TT, 2])
        slot_f = sb("slot_f", [P, TT, 2])
        slot_u = sb("slot_u", [P, TT, 2], U32)
        main_w = sb("main_w", [P, TT, 2])
        lists = sb("lists", [CAP, NE], U32)
        idx = [sb(f"idx{s}", [CAP, 1], U32) for s in range(2)]
        counts = sb("counts", [P, NE], I32)
        count_of = [sb(f"count_of{s}", [1, 1], I32) for s in range(2)]
        cmax = sb("cmax", [P, 1])
        flag = sb("flag", [P, 1], I32)
        oidx = [sb(f"oidx{b}", [OC, 1], U32) for b in range(OB)]
        bank = [ctx.enter_context(nc.psum_tensor(f"bank{i}", [P, 512], F32)) for i in range(BANKS + 1)]

        cst = cst_all[:, 0:4 * KD].rearrange("p (k n) -> p k n", k=KD)
        x_in_rows = xcy[:, 0:TT * D].rearrange("p (t d) -> p t d", t=TT)
        oh_u = oh[:, :].bitcast(U32)
        n_oh = TT * 2 * NE
        pick = oh[:, 0:n_oh].rearrange("p (t k e) -> p t k e", t=TT, k=2)
        tok_oh = oh[:, n_oh:2 * n_oh].rearrange("p (t k e) -> p t k e", t=TT, k=2)
        both = oh[:, 2 * n_oh:2 * n_oh + TT * NE].rearrange("p (t e) -> p t e", t=TT)
        rank_oh = oh[:, 2 * n_oh + TT * NE:2 * n_oh + TT * NE + TT * 2 * CAP]\
            .rearrange("p (t k r) -> p t k r", t=TT, k=2)
        xTr = hg[:, :].rearrange("p (k t) -> p k t", k=KD)
        gw = gate_w[:, :].rearrange("p (x d h j) -> p x d h j", x=2, d=2, h=KD)
        G1, A2, B2 = mod_sb[:, 0], mod_sb[:, 1], mod_sb[:, 2]
        x_rows = hg[:, :].rearrange("p (t d) -> p t d", t=TT)
        xc = xcy[:, :].rearrange("p (k t) -> p k t", k=KD)
        ya_in = xcy[:, 0:KD * T].rearrange("p (k t) -> p k t", k=KD)
        hs = hg[:, :].rearrange("p (k t) -> p k t", k=KD)
        lru_v = lru[:, :].rearrange("p (b d h t) -> p b d h t", b=4, d=2, h=2)
        r_b, i_b, a_b, q_b = (lru_v[:, n] for n in range(4))
        lru_f = lru[:, :].rearrange("p (b n) -> p b n", b=4)
        r_f, i_f, a_f, q_f = (lru_f[:, n] for n in range(4))
        xs = lru[:, 0:TT * D].rearrange("p (t d) -> p t d", t=TT)
        junk = lru[:, TT * D:TT * D + D]
        SA = lru[:, 0:KD * T].rearrange("p (k t) -> p k t", k=KD)
        SB = lru[:, KD * T:2 * KD * T].rearrange("p (k t) -> p k t", k=KD)
        cpad = cp[:, 0:4 * CG].rearrange("p (m t) -> p m t", m=4)
        ycv = cp[:, 4 * CG:].rearrange("p (m t) -> p m t", m=4)
        G2 = cp[:, 0:2 * D].rearrange("p (c d) -> p c d", c=2)
        gfin = cp[:, 2 * D:3 * D]
        gtmp = xrp[:, :, 0:T]
        xrp_f = xrp[:, :, :].rearrange("p b t -> p (b t)")
        wo_tmp = xrp_f[:, 0:CW]
        par_rows = xrp_f[:, 0:2 * P].rearrange("p (j n) -> p j n", j=2)
        ABUF = 4
        arow = xcy[0:5, 0:ABUF * CW].rearrange("p (s n) -> p s n", s=ABUF)
        st_sb = xrp_f[0:16, CW + P:CW + 2 * P]
        le = xrp_f[:, CW:CW + TT * NE].rearrange("p (t e) -> p t e", t=TT)
        rank_m = xrp_f[:, 0:2 * NE].rearrange("p (k e) -> p k e", k=2)
        h2 = xcy[:, 0:2 * D].rearrange("p (b d) -> p b d", b=2)
        h2T = xcy[:, 2 * D:3 * D].rearrange("p (k t) -> p k t", k=KD)
        row_junk = lru[:, 2 * D + 2 * FE + 2 * QUART:3 * D + 2 * FE + 2 * QUART]
        xg = xcy[:, 0:2 * D].rearrange("p (b d) -> p b d", b=2)
        y_sb = lru[:, 0:2 * D].rearrange("p (b d) -> p b d", b=2)
        sil = lru[0:CAP, 2 * D:2 * D + FE]
        z = lru[0:CAP, 2 * D + FE:2 * D + 2 * FE]
        xgT_hl = moe_hl[:, :, 0:XW]
        zT_hl = moe_hl[:, :, XW:]
        oxg = ring[:, 3, :].rearrange("p (b d) -> p b d", b=OB)
        oxgT = gate_w[:, 0:KD * OT].rearrange("p (k t) -> p k t", k=KD)
        orank = gate_w[:, 0:OT]
        oz = slot5[:, 0:JF * OT].rearrange("p (j t) -> p j t", j=JF)
        osil = slot5[:, JF * OT:JF * OT + OT]
        oy = slot5[:, 2048:2048 + D]
        olist_f = slot5[0:OC, 2048 + D:2048 + D + OB * NE].bitcast(U32)
        olist = olist_f.rearrange("p (b e) -> p b e", b=OB)
        yg = ring[:, 0:TT, :].rearrange("p b (k d) -> p b k d", k=KD * CW // D)
        o_rows = ring[:, 3, 0:TT * D].rearrange("p (b d) -> p b d", b=TT)
        o_junk = ring[:, 3, TT * D:(TT + 1) * D]

        landed = [sem(f"chunk_landed{s}") for s in range(MSLOTS)]
        hi_ready = sem("hi_ready")
        lo_v = sem("lo_by_vector")
        lo_p = sem("lo_by_gpsimd")
        act_hi = sem("activation_hi")
        ada_quarter = sem("ada_quarter_used")
        tile_done = sem("tile_done")
        bank_free = [sem(f"bank_free{s}") for s in range(BANKS)]
        params_in = [sem("params_a_in"), sem("params_b_in")]
        x_in = sem("x_in")
        x_again = sem("x_rows_again")
        gate_w_in = sem("gate_w_in")
        router_in = sem("router_in")
        consts = sem("consts")
        cvec_ready = sem("cvec_ready")
        lam_exp = sem("lam_exp")
        rate_ready = sem("rate_ready")
        ssq_ready = sem("ssq_ready")
        mean_ready = sem("mean_ready")
        rms_ready = sem("rms_ready")
        xs_ready = sem("xs_ready")
        xT_ready = sem("xT_ready")
        h_ready = sem("h_ready")
        h_whole = sem("h_before_split")
        ya_split = sem("ya_split")
        hs_split = sem("hs_split")
        pads_zero = sem("pads_zero")
        xr_ready = sem("xr_ready")
        xc_ready = sem("xc_ready")
        exp_done = sem("gate_exps")
        q_ready = sem("one_minus_a2")
        root_done = sem("gate_roots")
        batch_done = sem("scans_done")
        c_ready = sem("c_ready")
        conv_done = sem("conv_done")
        hg_ready = sem("hg_ready")
        merged_ready = sem("merged_ready")
        selectors = sem("selectors")
        arow_bias_in = [sem(f"ada_bias_in{s}") for s in range(ABUF)]
        gn2_in = sem("g_norm2_in")
        gfin_in = sem("g_final_in")
        state_out = sem("state_out")
        x1_ready = sem("x1_ready")
        h2_ready = sem("h2_ready")
        h2_out = [sem(f"h2_out{t}") for t in range(TT)]
        tops_ready = sem("tops_ready")
        texp_ready = sem("top_exps_ready")
        both_ready = sem("both_ready")
        onehots_ready = sem("onehots_ready")
        slots_ready = sem("slots_ready")
        bias_in = sem("router_bias_in")
        flag_ready = sem("flag_ready")
        idx_ready = sem("idx_ready")
        gathers_begun = sem("gathers_begun")
        xg_in = [sem(f"xg_in{s}") for s in range(2)]
        xg_used = sem("xg_transposed")
        xgT_a = sem("xgT_hi")
        xgT_v = sem("xgT_lo")
        moe_hi = sem("moe_hi_ready")
        moe_lo = sem("moe_lo_ready")
        moe_used = sem("moe_quarter_used")
        silu_done = sem("silu_done")
        z_ready = sem("z_ready")
        zT_done = sem("z_transposed")
        zT_a = sem("zT_hi")
        zT_v = sem("zT_lo")
        y_a = sem("y_by_scalar")
        y_v = sem("y_by_vector")
        y_defined = sem("y_rows_defined")
        y_out = [sem(f"y_out{s}") for s in range(2)]
        step_v = sem("vector_step")
        step_a = sem("scalar_step")
        step_o = sem("overflow_vector_step")
        yg_in = [sem(f"yg_in{s}") for s in range(TT)]
        y0_scaled = sem("y0_scaled")
        res_ready = sem("residual_ready")
        out_ready = sem("out_ready")
        out_sent = [sem(f"out_sent{t}") for t in range(TT)]
        o_landed = [sem(f"overflow_w{n}") for n in range(3)]
        o_onehot = sem("overflow_onehots")
        o_table = sem("overflow_table")
        o_list = sem("overflow_lists")
        o_idx = sem("overflow_idx")
        o_xg_in = sem("overflow_xg_in")
        o_trans = sem("overflow_transposed")
        o_xgT = sem("overflow_xgT")
        o_prod = sem("overflow_product")
        o_silu = sem("overflow_silu")
        o_z = sem("overflow_z")
        o_down = sem("overflow_down")
        o_y = sem("overflow_y")
        o_yout = sem("overflow_y_out")
        o_end = sem("overflow_expert_end")
        o_slots = sem("overflow_slots")
        o_yg_in = [sem(f"overflow_yg_in{t}") for t in range(TT)]
        o_added = sem("overflow_added")

        y_rows = y_dram.rearrange("(e r) d -> e r d", e=NE)
        oy_rows = oy_dram.rearrange("(e r) d -> e r d", e=NE)
        oslot_f, oslot_u, over_w = slot_f, oh_u[:, 0:TT * 2].rearrange("p (t k) -> p t k", t=TT), \
            oh[:, TT * 2:TT * 4].rearrange("p (t k) -> p t k", t=TT)

        block = ctx.enter_context(nc.Block())

        def wait_tile(eng, name):
            eng.wait_ge(tile_done, N_OF[name] + 1)

        def wait_read(eng, name):
            n = N_OF[name]
            eng.wait_ge(bank_free[n % BANKS], n // BANKS + 1)

        def quarter_of(kind, tile_):
            return 4 * C_OF[(kind, tile_ // CT)] + tile_ % CT

        def quarter(q):
            n, m = q // CT, q % CT
            pair = subs[:, sub_of(q)] if sub_of(q) < SUBS else subs_more[:, sub_of(q) - SUBS]
            if chunks[n][0] == "ada":
                return slot_k(n)[:, 2 * m:2 * m + 2, :], pair.rearrange("p x (k n) -> p x k n", k=2)
            return slot_k(n)[:, :, m * P:(m + 1) * P], pair.rearrange("p x (k n) -> p x k n", k=KD)

        def sub_of(q):
            first = quarter_of("ada", 4 * CT)
            r = (q - first) % ASUBS
            return q % SUBS if q < first else ((first + r) % SUBS if r < SUBS else r)

        def wait_sub_free(eng, q):
            users = [u for u in range(q) if sub_of(u) == sub_of(q)]
            if users:
                wait_quarter_used(eng, users[-1])
            elif sub_of(q) >= SUBS:
                wait_tile(eng, ("yb", KD - 1))

        def wait_quarter_used(eng, q):
            kind, half = chunks[q // CT]
            if kind != "ada":
                wait_tile(eng, (kind, CT * half + q % CT))
            elif q % CT == CT - 1:
                wait_tile(eng, ("adaR", half))
            else:
                eng.wait_ge(ada_quarter, (CT - 1) * half + q % CT + 1)

        def ada_rows_of(eng, j, share):
            v, cols = j // 2 - 2, slice(j % 2 * CW, (j % 2 + 1) * CW)
            dst = (G1, B2, A2, G2)[v]
            scaled = v == 2
            for cnd in range(2):
                if share == (1 if scaled else cnd):
                    ps, free = bank[N_OF[("adaB", j, cnd)] % BANKS], bank_free[N_OF[("adaB", j, cnd)] % BANKS]
                    wait_tile(eng, ("adaB", j, cnd))
                    out = dst[:, cnd, cols]
                    if scaled:
                        eng.wait_ge(gn2_in, 32)
                        eng.scalar_tensor_tensor(out=out, in0=ps[:, :], scalar=1.0, in1=out,
                                                 op0=ALU.add, op1=ALU.mult).then_inc(free, 1)
                    elif share == 0:
                        eng.activation(out, ps[:, :], ACT.Copy).then_inc(free, 1)
                    else:
                        eng.tensor_copy(out, ps[:, :]).then_inc(free, 1)

        VQ = [q for q in range(4 * NSPLIT) if chunks[q // CT][0] == "ada"]
        PQ = [q for q in range(4 * NSPLIT) if chunks[q // CT][0] != "ada"]

        def wait_split(eng, q):
            if q in VQ:
                eng.wait_ge(lo_v, VQ.index(q) + 1)
            else:
                eng.wait_ge(lo_p, PQ.index(q) + 1)

        def write_lo(eng, q, done):
            src, pair = quarter(q)
            eng.wait_ge(hi_ready, q + 1)
            eng.tensor_tensor(pair[:, 1], src, pair[:, 0].bitcast(F32), ALU.subtract).then_inc(done, 1)

        def wait_chunk(eng, n):
            eng.wait_ge(landed[n % SLOTS], 16 * (n // SLOTS + 1))

        def wait_chunk_used(eng, n):
            if n < NSPLIT:
                wait_split(eng, 4 * n + 3)
            else:
                wait_tile(eng, ("wo", TT - 1, chunks[n][1]))

        def chunk_src(kind, half):
            if kind == "ada":
                return ada_v[:, :, CW * half:CW * (half + 1)]
            if kind in U_COL:
                a = U_COL[kind] + CW * half
                return win_v[:, :, a:a + CW]
            src = {"ya": wco_v, "yb": wro_v, "wo": wo_v}[kind]
            return src[:, :, CW * half:CW * (half + 1)]

        def slot_k(n):
            return ring[:, n % SLOTS, :].rearrange("p (k n) -> p k n", k=KD)

        moe_slots = [ring[:, 0, :], ring[:, 1, :], gate_w[:, :], ring[:, 2, :], ring[:, 3, :], slot5[:, :]]
        moe_landed = [landed[0], landed[1], landed[4], landed[2], landed[3], landed[5]]
        MSUBS = SUBS + 1
        assert MSUBS == 4 and 4 * NSPLIT % SUBS == 0

        def slot_of(c):
            return (c - 1) % MSLOTS

        def moe_count(i, c):
            before_moe = 0 if slot_of(c) in (2, 5) else N1 // SLOTS
            return 16 * (i + before_moe + (0 if c == 0 else 1))

        def quarters_before(i, c):
            return i * (4 * MSLOTS) + 4 * (c - 1)

        def moe_sub(j):
            return sub3[:, :, :] if j == SUBS else subs[:, j, :, :]

        def pair_experts():
            return ((0, 1, 2), (3, 4, 5))

        def moe_write_lo(eng, i, c, js=range(4)):
            for j in js:
                sub = moe_sub(j)
                eng.wait_ge(moe_hi, quarters_before(i, c) + j + 1)
                eng.tensor_tensor(sub[:, 1, :], moe_slots[slot_of(c)][:, j * QUART:(j + 1) * QUART],
                                  sub[:, 0, :].bitcast(F32), ALU.subtract).then_inc(moe_lo, 1)

        @block.sync
        def _(eng):
            def rows_of(dst, src, sem_):
                eng.dma_start(dst, src).then_inc(sem_, 16)

            eng.dma_start(x_in_rows[:, 0, :], x_prompt[0]).then_inc(x_in, 16)
            eng.dma_start(x_in_rows[:, 1:TT, :], x_sample[0].rearrange("(t p) d -> p t d", p=P)).then_inc(x_in, 16)
            b = par_rows[:, 1, :]
            o = CVW
            for src in (conv_w[0], rnn_conv_w[0]):
                n = src.shape[0] * KD
                rows_of(b[o - CVW:o - CVW + n, :], src.rearrange("w (r p) -> (w r) p", p=P), params_in[1])
                o += n
            rows_of(b[RCB - CVW:RCB - CVW + KD, :], rnn_conv_b[0].rearrange("(r p) -> r p", p=P), params_in[1])
            for at, src in ((BGA, b_gate_a), (BGX, b_gate_x), (LAM, lam)):
                rows_of(b[at - CVW:at - CVW + 2 * KD, :], src[0].rearrange("d (r p) -> (d r) p", p=P),
                        params_in[1])
            for n, (kind, half) in enumerate(chunks):
                if n == SLOTS:
                    rows_of(wr[:, :, 0:NG], w_router_group[0].rearrange("(k p) n -> p k n", p=P), router_in)
                    rows_of(wr[:, :, NG:], w_router_expert[0].rearrange("(k p) n -> p k n", p=P), router_in)
                    rows_of(br[:, 0:NG], b_router_group[0].partition_broadcast(P), bias_in)
                    rows_of(br[:, NG:], b_router_expert[0].partition_broadcast(P), bias_in)
                if n == 8:
                    eng.wait_ge(consts, 2)
                    eng.dma_start(y_rows[:, FEW:CAP, :].rearrange("e r (a b) -> e (r a) b", b=P),
                                  ones[0:NE, :].unsqueeze(1)
                                  .to_broadcast([NE, (CAP - FEW) * D // P, P])).then_inc(y_defined, 16)
                if n == 6:
                    for x, src in enumerate((w_gate_a, w_gate_x)):
                        for d in range(2):
                            eng.dma_start(gw[:, x, d, :, :], src[0, d].rearrange("h i j -> i h j"))\
                                .then_inc(gate_w_in, 16)
                if n >= SLOTS:
                    wait_chunk_used(eng, n - SLOTS)
                eng.dma_start(slot_k(n), chunk_src(kind, half)).then_inc(landed[n % SLOTS], 16)

            def load(i, c, src, e):
                slot = moe_slots[slot_of(c)]
                if isinstance(i, int) and quarters_before(i, c) < 4 * MSLOTS:
                    if slot_of(c) == 2:
                        wait_tile(eng, ("adaR", 11))
                    elif slot_of(c) == 5:
                        eng.wait_ge(h2_ready, 2 * TT)
                    else:
                        wait_chunk_used(eng, N1 - SLOTS + (0, 1, None, 2, 3)[slot_of(c)])
                else:
                    eng.wait_ge(moe_lo, quarters_before(i, c) - 4 * MSLOTS + 4)
                if src is w2_v:
                    slot = slot.rearrange("p (j n) -> p j n", j=JF)
                eng.dma_start(slot, src[e]).then_inc(moe_landed[slot_of(c)], 16)

            def store(e, s):
                eng.wait_ge(y_a, e + 1)
                eng.wait_ge(y_v, e + 1)
                count = eng.value_load(counts[0:1, bass.ds(e, 1)], min_val=0, max_val=T)
                with eng.If(count > FEW):
                    eng.dma_start(y_rows[e, 0:CAP, :], y_sb[0:CAP, s, :]).then_inc(y_out[s], 16)
                with eng.If(count <= FEW):
                    eng.dma_start(y_rows[e, 0:FEW, :], y_sb[0:FEW, s, :]).then_inc(y_out[s], 16)

            def load_pair(i, stores=True):
                for s, (c1, c3, c2) in enumerate(pair_experts()):
                    load(i, c1, w1_v, i * 2 + s)
                    if stores:
                        store(i * 2 + (s - 4), s)
                    load(i, c3, w3_v, i * 2 + s)
                    load(i, c2, w2_v, i * 2 + s - 1)

            load(0, 1, w1_v, 0)
            load(0, 2, w3_v, 0)
            load(0, 3, w1_v, 1)
            load(0, 4, w3_v, 1)
            load(0, 5, w2_v, 0)
            load_pair(1, stores=False)
            eng.wait_ge(flag_ready, 1)
            eng.wait_ge(y_defined, 16)
            with eng.Fori(2, PAIRS) as i:
                load_pair(i)
            load(PAIRS, 0, w2_v, NE - 1)
            for e in range(NE - 4, NE):
                store(e, e % 2)
            eng.wait_ge(flag_ready, 1)
            most = eng.value_load(flag[0:1, 0:1], min_val=0, max_val=T)
            with eng.If(most > CAP):
                with eng.Fori(0, NE) as e:
                    eng.wait_ge(o_end, e + 1)
                    eng.dma_start(ring[:, 0, :], w1_v[e, :, :]).then_inc(o_landed[0], 16)
                    eng.dma_start(ring[:, 1, :], w3_v[e, :, :]).then_inc(o_landed[1], 16)
                    eng.dma_start(ring[:, 2, :].rearrange("p (j n) -> p j n", j=JF),
                                  w2_v[e, :, :, :]).then_inc(o_landed[2], 16)
            for t in range(TT):
                eng.wait_ge(out_ready, t + 1)
                dst = y_prompt[0] if t == 0 else y_sample[0, (t - 1) * P:t * P, :]
                eng.dma_start(dst, o_rows[:, t, :]).then_inc(out_sent[t], 16)
            for t in range(TT):
                eng.wait_ge(out_sent[t], 16)

        @block.gpsimd
        def _(eng):
            eng.memset(ident[:, :], 0.0).then_inc(consts, 1)
            eng.memset(ones[:, :], 1.0).then_inc(consts, 1)
            eng.wait_ge(consts, 2)
            eng.affine_select(out=ident[:, :], in_=ident[:, :], compare_op=ALU.not_equal, fill=1.0,
                              base=0, pattern=[[-1, P]], channel_multiplier=1).then_inc(consts, 1)
            eng.affine_select(out=before[:, :], in_=ones[:, :], compare_op=ALU.is_gt, fill=0.0,
                              base=0, pattern=[[1, P]], channel_multiplier=-1).then_inc(consts, 1)
            eng.iota(iota[:, :], pattern=[[1, T]], base=0, channel_multiplier=0,
                     allow_small_or_imprecise_dtypes=True).then_inc(consts, 1)
            eng.iota(tok[:, :], pattern=[[P, TT]], base=0, channel_multiplier=1,
                     allow_small_or_imprecise_dtypes=True).then_inc(consts, 1)

            def gather(e, s, all_rows=False):
                eng.tensor_copy(idx[s][:, :], lists[:, bass.ds(e, 1)]).then_inc(idx_ready, 1)
                eng.tensor_copy(count_of[s][:, :], counts[0:1, bass.ds(e, 1)]).then_inc(idx_ready, 1)
                eng.wait_ge(idx_ready, e * 2 + 2)
                eng.sem_inc(gathers_begun, 1)

                def rows(n):
                    eng.indirect_dma_start(out=xg[0:n, s, :], out_offset=None, in_=h2_dram[:, :],
                                           in_offset=bass.IndirectOffsetOnAxis(ap=idx[s][0:n, 0:1], axis=0),
                                           ).then_inc(xg_in[s], 16)

                if all_rows:
                    rows(CAP)
                    return
                count = eng.value_load(count_of[s][0:1, 0:1], min_val=0, max_val=T)
                with eng.If(count > FEW):
                    rows(CAP)
                with eng.If(count <= FEW):
                    rows(FEW)

            for q in PQ:
                write_lo(eng, q, lo_p)

            moe_write_lo(eng, 0, 1)

            wait_read(eng, ("list",))
            eng.wait_ge(flag_ready, 1)
            for t in range(TT):
                eng.wait_ge(h2_out[t], 16)
            for s in range(2):
                gather(s, s, all_rows=True)
            with eng.Fori(1, PAIRS) as i:
                for s in range(2):
                    eng.wait_ge(xg_used, i * 2 + (s - 1))
                    gather(i * 2 + s, s)

            eng.wait_ge(flag_ready, 1)
            most = eng.value_load(flag[0:1, 0:1], min_val=0, max_val=T)
            with eng.If(most > CAP):
                eng.wait_ge(o_list, 1)
                with eng.Fori(0, NE) as e:
                    eng.wait_ge(o_end, e + 1)
                    for b in range(OB):
                        eng.tensor_copy(oidx[b][:, :], olist[:, b, bass.ds(e, 1)]).then_inc(o_idx, 1)
                    eng.wait_ge(o_idx, e * OB + OB)
                    eng.sem_inc(gathers_begun, 1)
                    for b in range(OB):
                        eng.indirect_dma_start(
                            out=oxg[0:OC, b, :], out_offset=None, in_=h2_dram[:, :],
                            in_offset=bass.IndirectOffsetOnAxis(ap=oidx[b][:, 0:1], axis=0),
                        ).then_inc(o_xg_in, 16)
                eng.wait_ge(o_yout, 16 * NE * OB)
                eng.wait_ge(o_slots, 1)
                for t in range(TT):
                    for k in range(2):
                        eng.indirect_dma_start(
                            out=yg[:, t, k, :], out_offset=None, in_=oy_dram[:, :],
                            in_offset=bass.IndirectOffsetOnAxis(ap=oslot_u[:, t, k:k + 1], axis=0),
                        ).then_inc(o_yg_in[t], 16)
                eng.wait_ge(o_added, TT)
            eng.wait_ge(slots_ready, TT)
            for s in range(2):
                eng.wait_ge(y_out[s], 16 * PAIRS)
            for t in range(TT):
                for k in range(2):
                    eng.indirect_dma_start(
                        out=yg[:, t, k, :], out_offset=None, in_=y_dram[:, :],
                        in_offset=bass.IndirectOffsetOnAxis(ap=slot_u[:, t, k:k + 1], axis=0),
                    ).then_inc(yg_in[t], 16)

        @block.tensor
        def _(eng):
            def open_tile(name):
                n = N_OF[name]
                if n >= BANKS:
                    eng.wait_ge(bank_free[n % BANKS], n // BANKS)
                return bank[n % BANKS]

            def transpose_params(j):
                rows = (NPA, NPAR - NPA)[j]
                ps = open_tile(("par", j))
                eng.wait_ge(params_in[j], 16 * (7 if j == 0 else 6))
                eng.transpose(ps[:, 0:rows], par_rows[0:rows, j, :], ident[0:rows, 0:rows])\
                    .then_inc(tile_done, 1)

            def transpose_x(k):
                ps = open_tile(("xT", k))
                eng.wait_ge(xs_ready, TT)
                for t in range(TT):
                    mm = eng.transpose(ps[:, t * P:(t + 1) * P], xs[:, t, k * P:(k + 1) * P], ident[:, :])
                mm.then_inc(tile_done, 1)

            def ada_rows(j):
                ps = open_tile(("adaR", j))
                eng.wait_ge(cvec_ready, 3)
                for m in range(CT):
                    q = 4 * C_OF[("ada", j)] + m
                    _, pair = quarter(q)
                    wait_split(eng, q)
                    for kk in range(2):
                        k = 2 * m + kk
                        c4 = cst_all[:, 4 * k:4 * k + P]
                        eng.matmul(ps[:, :], c4, pair[:, 1, kk, :], start=(k == 0), stop=False)
                        mm = eng.matmul(ps[:, :], c4, pair[:, 0, kk, :], start=False, stop=(k == KD - 1))
                    mm.then_inc(tile_done if m == CT - 1 else ada_quarter, 1)

            def ada_columns(j):
                ps = open_tile(("adaC", j))
                eng.wait_ge(selectors, 4)
                wait_read(eng, ("adaR", j))
                for m in range(CT):
                    mm = eng.matmul(ps[:, 2 * m:2 * m + 2], arow[0:4, j % ABUF, m * P:(m + 1) * P],
                                    selc[0:4, :], start=True, stop=True)
                mm.then_inc(tile_done, 1)

            def ada_spread(j):
                for cnd in range(2):
                    ps = open_tile(("adaB", j, cnd))
                    if cnd == 0:
                        wait_read(eng, ("adaR", j))
                        eng.wait_ge(arow_bias_in[j % ABUF], 16 * (j // ABUF))
                    eng.matmul(ps[:, :], selb[:, cnd, :], arow[:, j % ABUF, :], start=True, stop=True)\
                        .then_inc(tile_done, 1)

            def project(kind, half, x, ready=None):
                for m in range(CT):
                    ps = open_tile((kind, CT * half + m))
                    q = quarter_of(kind, CT * half + m)
                    _, pair = quarter(q)
                    wait_split(eng, q)
                    for k in range(KD):
                        if ready is not None and m == 0:
                            eng.wait_ge(ready, k + 1)
                        eng.matmul(ps[:, 0:T], pair[:, 1, k, :], x[:, 0, k, :], start=(k == 0), stop=False)
                        eng.matmul(ps[:, 0:T], pair[:, 0, k, :], x[:, 1, k, :], start=False, stop=False)
                        mm = eng.matmul(ps[:, 0:T], pair[:, 0, k, :], x[:, 0, k, :],
                                        start=False, stop=(k == KD - 1))
                    mm.then_inc(tile_done, 1)

            def gates(b):
                for h in (2 * b, 2 * b + 1):
                    eng.wait_ge(xc_ready, h + 1)
                    for d in range(2):
                        for x in range(2):
                            ps = open_tile(("gate", h, d, x))
                            eng.matmul(ps[:, 0:TG], gw[:, x, d, h, :], xc[:, h, :],
                                       start=True, stop=True).then_inc(tile_done, 1)

            eng.wait_ge(consts, 6)
            start_work = {"par": transpose_params, "xT": transpose_x, "adaR": ada_rows, "adaC": ada_columns}
            for name, number in START:
                start_work[name](number)
            for n, item in enumerate(W_IN):
                if isinstance(item, int):
                    if item == 0:
                        eng.wait_ge(gate_w_in, 64)
                    gates(item)
                else:
                    project(item[0], item[1], h_hl, h_ready if n == 0 else None)
            project("yb", 0, hs_hl, hs_split)
            project("yb", 1, hs_hl)
            project("ya", 0, h_hl, ya_split)
            project("ya", 1, h_hl)
            for j in range(4, 12):
                ada_rows(j)
                if j > 4:
                    ada_spread(j - 1)
            ada_spread(11)
            ps = open_tile(("state",))
            eng.wait_ge(batch_done, 4)
            eng.transpose(ps[0:16, 0:P], stc[:, :], ident[:, :]).then_inc(tile_done, 1)

            def out_rows(t, half):
                ps = open_tile(("wo", t, half))
                n = C_OF[("wo", half)]
                wait_chunk(eng, n)
                for k in range(KD):
                    if t == 0 and half == 0:
                        eng.wait_ge(merged_ready, k + 1)
                    mm = eng.matmul(ps[:, :], SA[:, k, t * P:(t + 1) * P], slot_k(n)[:, k, :],
                                    start=(k == 0), stop=(k == KD - 1))
                mm.then_inc(tile_done, 1)

            def transpose_h2(t, half):
                ps = open_tile(("h2T", t, half))
                eng.wait_ge(h2_ready, 2 * t + half + 1)
                for m in range(4):
                    k = 4 * half + m
                    mm = eng.transpose(ps[:, m * P:(m + 1) * P], h2[:, t % 2, k * P:(k + 1) * P], ident[:, :])
                mm.then_inc(tile_done, 1)

            def route(t):
                ps = open_tile(("route", t))
                eng.wait_ge(router_in, 32)
                wait_read(eng, ("h2T", t, 0))
                wait_read(eng, ("h2T", t, 1))
                for k in range(KD):
                    mm = eng.matmul(ps[:, 0:NG + NE], h2T[:, k, :], wr[:, k, :],
                                    start=(k == 0), stop=(k == KD - 1))
                mm.then_inc(tile_done, 1)

            def rank_tokens(t):
                ps = open_tile(("rank", t))
                eng.wait_ge(both_ready, t + 1)
                for u in range(t):
                    eng.matmul(ps[:, 0:NE], ones[:, :], both[:, u, :], start=(u == 0), stop=False)
                eng.matmul(ps[:, 0:NE], before[:, :], both[:, t, :], start=(t == 0), stop=True)\
                    .then_inc(tile_done, 1)

            def count_tokens():
                ps = open_tile(("count",))
                for t in range(TT):
                    mm = eng.matmul(ps[:, 0:NE], ones[:, :], both[:, t, :], start=(t == 0),
                                    stop=(t == TT - 1))
                mm.then_inc(tile_done, 1)

            def list_tokens():
                ps = open_tile(("list",))
                eng.wait_ge(onehots_ready, TT)
                for t in range(TT):
                    for k in range(2):
                        mm = eng.matmul(ps[0:CAP, 0:NE], rank_oh[:, t, k, :], tok_oh[:, t, k, :],
                                        start=(t == 0 and k == 0), stop=(t == TT - 1 and k == 1))
                mm.then_inc(tile_done, 1)

            tile_work = {"wo": out_rows, "h2T": transpose_h2, "route": route, "rank": rank_tokens,
                         "count": count_tokens, "list": list_tokens}
            for name in WO_ON:
                tile_work[name[0]](*name[1:])

            for b in range(BANKS):
                uses = (len(stream) - b + BANKS - 1) // BANKS
                eng.wait_ge(bank_free[b], uses)

            def transpose_rows(e, s, land):
                eng.wait_ge(xg_in[s], land)
                rows = xg[0:CAP, s, :].rearrange("t (p k) -> t k p", k=KD)
                for k in range(KD):
                    b, m = k // 4, k % 4
                    mm = eng.transpose(bank[b][:, m * CAP:(m + 1) * CAP], rows[:, k, :],
                                       ident[0:CAP, 0:CAP])
                mm.then_inc(xg_used, 1)

            def rows_times(i, c, out):
                for j in range(4):
                    eng.wait_ge(moe_lo, quarters_before(i, c) + j + 1)
                    w = moe_sub(j).rearrange("p x (k n) -> p x k n", k=2)
                    for kk in range(2):
                        k = 2 * j + kk
                        x_hi, x_lo = (xgT_hl[:, n, k * CAP:k * CAP + P] for n in range(2))
                        eng.matmul(out[:, :], x_lo, w[:, 0, kk, :], start=(k == 0), stop=False)
                        eng.matmul(out[:, :], x_hi, w[:, 1, kk, :], start=False, stop=False)
                        mm = eng.matmul(out[:, :], x_hi, w[:, 0, kk, :], start=False, stop=(k == KD - 1))
                    mm.then_inc(moe_used, 1)

            def z_times(i, c, e, first):
                eng.wait_ge(zT_a, e + 1)
                eng.wait_ge(zT_v, e + 1)
                if not first:
                    eng.wait_ge(y_a, e)
                    eng.wait_ge(y_v, e)
                for j in range(JF):
                    eng.wait_ge(moe_lo, quarters_before(i, c) + j + 1)
                    w = moe_sub(j)
                    z_hi, z_lo = (zT_hl[:, n, j * CAP:j * CAP + P] for n in range(2))
                    for half in range(2):
                        cols = slice(half * 512, (half + 1) * 512)
                        out = bank[4 + half]
                        eng.matmul(out[:, :], z_lo, w[:, 0, cols], start=(j == 0), stop=False)
                        eng.matmul(out[:, :], z_hi, w[:, 1, cols], start=False, stop=False)
                        mm = eng.matmul(out[:, :], z_hi, w[:, 0, cols], start=False, stop=(j == JF - 1))
                    mm.then_inc(moe_used, 1)

            def transpose_z(e):
                eng.wait_ge(z_ready, e + 1)
                for j in range(JF):
                    mm = eng.transpose(bank[6][:, j * CAP:(j + 1) * CAP], z[:, j * P:(j + 1) * P],
                                       ident[0:CAP, 0:CAP])
                mm.then_inc(zT_done, 1)

            def expert(i, s, chunks3, e0=False, e1=False, last=False):
                e = i * 2 + s
                c1, c3, c2 = chunks3
                eng.wait_ge(xgT_a, e + 1)
                eng.wait_ge(xgT_v, e + 1)
                if not e0:
                    eng.wait_ge(silu_done, e)
                rows_times(i, c1, bank[2])
                rows_times(i, c3, bank[3])
                if not last:
                    transpose_rows(e + 1, 1 - s, 16 * (i + s + 1))
                if not e0:
                    z_times(i, c2, e - 1, e1)
                transpose_z(e)

            transpose_rows(0, 0, 16)
            expert(0, 0, (1, 2, None), e0=True)
            expert(0, 1, (3, 4, 5), e1=True)
            for s, cs in enumerate(pair_experts()):
                expert(1, s, cs)
            with eng.Fori(2, PAIRS - 1) as i:
                for s, cs in enumerate(pair_experts()):
                    expert(i, s, cs)
            for s, cs in enumerate(pair_experts()):
                expert(PAIRS - 1, s, cs, last=(s == 1))
            z_times(PAIRS, 0, NE - 1, False)

            eng.wait_ge(flag_ready, 1)
            most = eng.value_load(flag[0:1, 0:1], min_val=0, max_val=T)
            with eng.If(most > CAP):
                eng.wait_ge(y_a, NE)
                eng.wait_ge(y_v, NE)
                for b in range(OB):
                    for t in range(TT):
                        for k in range(2):
                            eng.wait_ge(o_onehot, (b * TT + t) * 2 + k + 1)
                            mm = eng.matmul(bank[0][0:OC, b * NE:(b + 1) * NE],
                                            orank[:, b * OC:(b + 1) * OC], tok_oh[:, t, k, :],
                                            start=(t == 0 and k == 0), stop=(t == TT - 1 and k == 1))
                            mm.then_inc(o_table, 1)
                eng.wait_ge(o_list, 1)
                with eng.Fori(0, NE) as e:
                    eng.wait_ge(o_xg_in, e * (16 * OB) + 16 * OB)
                    for b in range(OB):
                        rows = oxg[0:OC, b, :].rearrange("t (p k) -> t k p", k=KD)
                        eng.wait_ge(o_xgT, e * (2 * OB) + 2 * b + 1)
                        for k in range(KD):
                            mm = eng.transpose(bank[k // 4][:, (k % 4) * OC:(k % 4 + 1) * OC],
                                               rows[:, k, :], ident[0:OC, 0:OC])
                        mm.then_inc(o_trans, 1)
                    eng.wait_ge(o_xgT, e * (2 * OB) + 2 * OB + 1)
                    eng.wait_ge(o_landed[0], e * 16 + 16)
                    eng.wait_ge(o_landed[1], e * 16 + 16)
                    for j in range(JF):
                        eng.wait_ge(o_z, e * JF + j + 1)
                        for m in range(2):
                            w = ring[:, m, :].rearrange("p (k n) -> p k n", k=KD)
                            for k in range(KD):
                                mm = eng.matmul(bank[2 + m][:, 0:OT], w[:, k, j * P:(j + 1) * P],
                                                oxgT[:, k, :], start=(k == 0), stop=(k == KD - 1))
                            mm.then_inc(o_prod, 1)
                    eng.wait_ge(o_z, e * JF + JF + 1)
                    eng.wait_ge(o_landed[2], e * 16 + 16)
                    w = ring[:, 2, :].rearrange("p (j n) -> p j n", j=JF)
                    for b in range(OB):
                        eng.wait_ge(o_y, e * (2 * OB) + 2 * b + 1)
                        for half in range(2):
                            for j in range(JF):
                                mm = eng.matmul(bank[4 + half][0:OC, :], oz[:, j, b * OC:(b + 1) * OC],
                                                w[:, j, half * 512:(half + 1) * 512],
                                                start=(j == 0), stop=(j == JF - 1))
                        mm.then_inc(o_down, 1)

        @block.scalar
        def _(eng):
            steps = [0]

            def then(ins):
                ins.then_inc(step_a, 1)
                steps[0] += 1
                eng.wait_ge(step_a, steps[0])

            def tile(name):
                n = N_OF[name]
                eng.wait_ge(tile_done, n + 1)
                return bank[n % BANKS], bank_free[n % BANKS]

            fed = [0]

            def feed(last_q):
                while fed[0] <= min(last_q, 4 * NSPLIT - 1):
                    q = fed[0]
                    src, pair = quarter(q)
                    if q % 4 == 0:
                        wait_chunk(eng, q // 4)
                    wait_sub_free(eng, q)
                    eng.activation(pair[:, 0], src, ACT.Copy).then_inc(hi_ready, 1)
                    fed[0] += 1

            def bias_row(j):
                if j >= 2 * ABUF:
                    wait_tile(eng, ("adaB", j - ABUF, 1))
                eng.dma_start(arow[4:5, j % ABUF, :], b_ada[0:1, j * CW:(j + 1) * CW])\
                    .then_inc(arow_bias_in[j % ABUF], 16)

            def ada_copies(j):
                for m in range(CT):
                    feed(4 * C_OF[("ada", j)] + m + (SUBS if j < 4 else ASUBS))
                    if m == 0 and 6 <= j + 2 < 12:
                        bias_row(j + 2)
                ps, free = tile(("adaR", j))
                if j < 4:
                    eng.wait_ge(xs_ready, TT)
                elif j >= 2 * ABUF:
                    wait_tile(eng, ("adaB", j - ABUF, 1))
                eng.activation(arow[0:4, j % ABUF, :], ps[0:4, :], ACT.Copy)\
                    .then_inc(free, 1)

            def feed_behind(kind, k):
                feed(quarter_of(kind, k) + SUBS)

            def rows_of(dst, src, sem_):
                eng.dma_start(dst, src).then_inc(sem_, 16)

            a = par_rows[:, 0, :]
            rows_of(a[BADA:48, :], b_ada[0].rearrange("(r p) -> r p", p=P), params_in[0])
            rows_of(a[CCTX:CCTX + KD, :], c_ctx.rearrange("(r p) -> r p", p=P), params_in[0])
            rows_of(a[CSMP:CSMP + KD, :], c[0].rearrange("(r p) -> r p", p=P), params_in[0])
            rows_of(a[GN1:GN1 + KD, :], g_norm1[0].rearrange("(r p) -> r p", p=P), params_in[0])
            rows_of(a[GN2:GN2 + KD, :], g_norm2[0].rearrange("(r p) -> r p", p=P), params_in[0])
            for d in range(2):
                rows_of(a[STF + KD * d:STF + KD * (d + 1), :],
                        state_rnn[0, 0, d].rearrange("(r p) -> r p", p=P), params_in[0])
            eng.wait_ge(x_in, 32)
            for t in range(TT):
                if t:
                    eng.wait_ge(ssq_ready, t)
                eng.activation(junk, x_in_rows[:, t, :], ACT.Square, accum_out=stat[:, 0, 0, t:t + 1])\
                    .then_inc(ssq_ready, 1)
            eng.wait_ge(mean_ready, 1)
            eng.activation(stat[:, 0, 2, :], stat[:, 0, 1, :], ACT.Sqrt).then_inc(rms_ready, 1)
            wait_read(eng, ("par", 0))
            wait_read(eng, ("par", 1))
            eng.activation(cvec[:, :, :], pT[:, CCTX:CCTX + 2 * KD].rearrange("p (c k) -> p k c", c=2),
                           ACT.Silu).then_inc(cvec_ready, 1)
            eng.wait_ge(cvec_ready, 1)
            eng.activation(cst[:, :, 0:2], cvec[:, :, :], ACT.Copy).then_inc(cvec_ready, 1)
            feed(SUBS - 1)
            for name, number in START[2:]:
                if name == "xT":
                    ps, free = tile(("xT", number))
                    eng.activation(xTr[:, number, :], ps[:, 0:T], ACT.Copy).then_inc(free, 1)
                elif name == "adaR":
                    ada_copies(number)
            for k in range(KD):
                eng.wait_ge(h_whole, k + 1)
                eng.activation(h_hl[:, 0, k, :], xTr[:, k, :], ACT.Copy).then_inc(act_hi, 1)

            eng.wait_ge(pads_zero, 2)

            def copy_xr(h):
                ps, free = tile(("xr", h))
                if h >= 2:
                    eng.wait_ge(xc_ready, h - 1)
                eng.activation(xrp[:, h % 2, 2:2 + NP_TOK], ps[:, 0:NP_TOK], ACT.Copy)
                eng.activation(xrp[:, h % 2, 2 + S0:2 + TG], ps[:, NP_TOK:T], ACT.Copy)\
                    .then_inc(free, 1)
                feed_behind("xr", h)

            def gate_sigmoids(b):
                if b >= 1:
                    eng.wait_ge(batch_done, b)
                for h in (2 * b, 2 * b + 1):
                    for d in range(2):
                        for x, (dst, bias) in enumerate(((r_b, BGA), (i_b, BGX))):
                            ps, free = tile(("gate", h, d, x))
                            col = bias + d * KD + h
                            eng.activation(dst[:, d, h % 2, :], ps[:, 0:TG], ACT.Sigmoid,
                                           bias=pT[:, col:col + 1]).then_inc(free, 1)

            def gate_exps(b):
                for h in (2 * b, 2 * b + 1):
                    for d in range(2):
                        for x in range(2):
                            n = N_OF[("gate", h, d, x)]
                            eng.wait_ge(bank_free[n % BANKS], n // BANKS + 1)
                if b == 0:
                    eng.wait_ge(rate_ready, 1)
                for h in (2 * b, 2 * b + 1):
                    for d in range(2):
                        col = d * KD + h
                        eng.activation(a_b[:, d, h % 2, :], r_b[:, d, h % 2, :], ACT.Exp,
                                       scale=rate[:, 0, col:col + 1]).then_inc(exp_done, 1)
                for h in (2 * b, 2 * b + 1):
                    for d in range(2):
                        col = d * KD + h
                        eng.activation(r_b[:, d, h % 2, :], r_b[:, d, h % 2, :], ACT.Tanh,
                                       scale=rate[:, 1, col:col + 1]).then_inc(exp_done, 1)

            def gate_roots(b):
                eng.wait_ge(q_ready, b + 1)
                eng.activation(r_f, r_f, ACT.Sqrt).then_inc(root_done, 1)

            def copy_c(half):
                for m in range(CT):
                    ps, free = tile(("c", CT * half + m))
                    if half:
                        eng.wait_ge(conv_done, m + 1)
                    eng.activation(cpad[:, m, 1:1 + NP_TOK], ps[:, 0:NP_TOK], ACT.Copy)
                    eng.activation(cpad[:, m, 2 + NP_TOK:].rearrange("p (r q) -> p r q", r=ROWS)[:, :, 0:GRID_W],
                                   ps[:, NP_TOK:T].rearrange("p (r q) -> p r q", r=ROWS), ACT.Copy)\
                        .then_inc(free, 1)
                    feed_behind("c", CT * half + m)

            def gelus(half):
                for m in range(CT):
                    k = CT * half + m
                    ps, free = tile(("g", k))
                    if k >= 2:
                        eng.wait_ge(hg_ready, k - 1)
                    else:
                        eng.wait_ge(xc_ready, KD)
                    eng.activation(gtmp[:, k % 2, :], ps[:, 0:T], ACT.Gelu_apprx_tanh).then_inc(free, 1)
                    feed_behind("g", k)

            def follow(kind, half):
                for m in range(CT):
                    feed_behind(kind, CT * half + m)

            copy_xr(0)
            copy_xr(1)
            then(eng.activation(sp[:, 0, :], pT[:, LAM:NPAR], ACT.Abs))
            eng.activation(sp[:, 1, :], sp[:, 0, :], ACT.Exp, scale=-1.0).then_inc(lam_exp, 1)
            copy_xr(2)
            copy_xr(3)
            gate_sigmoids(0)
            gate_exps(0)
            copy_xr(4)
            copy_xr(5)
            gate_roots(0)
            copy_xr(6)
            copy_xr(7)
            copy_c(0)
            gate_sigmoids(1)
            gate_exps(1)
            feed_behind("v", 0)
            gate_roots(1)
            follow("v", 0)
            follow("b", 0)
            gate_sigmoids(2)
            gate_exps(2)
            feed_behind("g", 0)
            gate_roots(2)
            gelus(0)
            copy_c(1)
            gate_sigmoids(3)
            gate_exps(3)
            feed_behind("v", 4)
            gate_roots(3)
            follow("v", 1)
            follow("b", 1)
            gelus(1)
            eng.wait_ge(batch_done, 4)
            for kind, dst in (("ma", SA), ("mb", SB)):
                for k in range(KD):
                    ps, free = tile((kind, k))
                    eng.activation(dst[:, k, :], ps[:, 0:T], ACT.Sigmoid).then_inc(free, 1)
                    feed_behind(kind, k)
                    if kind == "mb":
                        eng.wait_ge(hg_ready, KD)
                        eng.activation(hs_hl[:, 0, k, :], hs[:, k, :], ACT.Copy).then_inc(act_hi, 1)
            eng.wait_ge(hs_split, KD)
            rows_of(x_rows[:, 0, :], x_prompt[0], x_again)
            rows_of(x_rows[:, 1:TT, :], x_sample[0].rearrange("(t p) d -> p t d", p=P), x_again)
            for k in range(KD):
                feed_behind("yb", k)
                if k == 2:
                    for kk in range(KD):
                        wait_read(eng, ("b", kk))
                        eng.activation(h_hl[:, 0, kk, :], ya_in[:, kk, :], ACT.Copy).then_inc(act_hi, 1)
            follow("ya", 0)
            follow("ya", 1)
            for cnd in range(2):
                eng.dma_start(A2[:, cnd, :], g_norm2[0].partition_broadcast(P)).then_inc(gn2_in, 16)
            eng.dma_start(gfin, g_final.partition_broadcast(P)).then_inc(gfin_in, 16)
            eng.wait_ge(ya_split, KD)
            bias_row(4)
            bias_row(5)
            for j in range(4, 12):
                ada_copies(j)
                if j > 4:
                    ada_rows_of(eng, j - 1, 0)
            ada_rows_of(eng, 11, 0)
            ps, free = tile(("state",))
            eng.activation(st_sb, ps[0:16, 0:P], ACT.Copy).then_inc(free, 1)
            wait_read(eng, ("state",))
            eng.dma_start(state_new[0, 0].rearrange("d (k p) -> (d k) p", p=P), st_sb)\
                .then_inc(state_out, 16)

            def route_copies(t):
                for half in range(2):
                    ps, free = tile(("h2T", t, half))
                    if half == 0 and t >= 1:
                        wait_tile(eng, ("route", t - 1))
                    eng.activation(h2T[:, 4 * half:4 * half + 4, :].rearrange("p k t -> p (k t)"),
                                   ps[:, :], ACT.Copy).then_inc(free, 1)

            def norm_rows(t):
                eng.wait_ge(x1_ready, t + 1)
                eng.activation(row_junk, x_rows[:, t, :], ACT.Square, accum_out=stat[:, 1, 0, t:t + 1])\
                    .then_inc(ssq_ready, 1)
                eng.wait_ge(mean_ready, t + 2)
                eng.activation(stat[:, 1, 2, t:t + 1], stat[:, 1, 1, t:t + 1], ACT.Sqrt)\
                    .then_inc(rms_ready, 1)
                eng.wait_ge(h2_ready, 2 * t + 2)
                eng.dma_start(h2_dram[t * P:(t + 1) * P, :], h2[:, t % 2, :]).then_inc(h2_out[t], 16)

            def top_exps(t):
                eng.wait_ge(tops_ready, t + 1)
                eng.activation(rt[:, t, 0:NG], lg[:, t, 0:NG], ACT.Exp, bias=rt[:, t, 32:33],
                               accum_out=rt[:, t, 33:34])
                eng.activation(rt[:, t, 34:35], rt[:, t, 35:36], ACT.Exp).then_inc(texp_ready, 1)

            def hi(i, c, js=range(4)):
                for j in js:
                    q = quarters_before(i, c) + j
                    if j == 0:
                        eng.wait_ge(moe_landed[slot_of(c)], moe_count(i, c))
                    if isinstance(i, int) and q < SUBS:
                        last = max(u for u in range(4 * NSPLIT) if sub_of(u) == q)
                        wait_quarter_used(eng, last)
                    elif not isinstance(i, int) or q > SUBS:
                        eng.wait_ge(moe_used, q - MSUBS + 1)
                    eng.activation(moe_sub(j)[:, 0, :], moe_slots[slot_of(c)][:, j * QUART:(j + 1) * QUART],
                                   ACT.Copy).then_inc(moe_hi, 1)

            hi(0, 1)
            norm_rows(0)
            route_copies(0)
            norm_rows(1)
            route_copies(1)
            norm_rows(2)
            route_copies(2)
            for t in range(TT):
                top_exps(t)

            def rows_hi(e):
                eng.wait_ge(xg_used, e + 1)
                for b in range(2):
                    ins = eng.activation(xgT_hl[:, 0, b * 4 * CAP:(b + 1) * 4 * CAP], bank[b][:, 0:4 * CAP],
                                         ACT.Copy)
                ins.then_inc(xgT_a, 1)

            def z_hi(e):
                eng.wait_ge(zT_done, e + 1)
                eng.activation(zT_hl[:, 0, 0:JF * CAP], bank[6][:, 0:JF * CAP], ACT.Copy).then_inc(zT_a, 1)

            def y_half(s, used, stores):
                eng.wait_ge(moe_used, used)
                if stores is not None:
                    eng.wait_ge(y_out[s], stores)
                eng.activation(y_sb[0:CAP, s, 0:512], bank[4][0:CAP, :], ACT.Copy).then_inc(y_a, 1)

            def expert(i, s, chunks3, e0=False, e1=False, last=False, js=range(4)):
                e = i * 2 + s
                c1, c3, c2 = chunks3
                hi(i, c1, js)
                if not e0:
                    z_hi(e - 1)
                if not e0 and not e1:
                    no_store = isinstance(i, int) and i == 1
                    y_half(s, quarters_before(i, c1), None if no_store else (i - 1) * 16)
                hi(i, c3)
                eng.wait_ge(moe_used, quarters_before(i, c1) + 4)
                if not e0:
                    eng.wait_ge(z_ready, e)
                eng.activation(sil, bank[2][0:CAP, :], ACT.Silu).then_inc(silu_done, 1)
                if not e0:
                    hi(i, c2)
                if not last:
                    rows_hi(e + 1)

            rows_hi(0)
            expert(0, 0, (1, 2, None), e0=True, js=())
            expert(0, 1, (3, 4, 5), e1=True)
            for s, cs in enumerate(pair_experts()):
                expert(1, s, cs)
            with eng.Fori(2, PAIRS - 1) as i:
                for s, cs in enumerate(pair_experts()):
                    expert(i, s, cs)
            for s, cs in enumerate(pair_experts()):
                expert(PAIRS - 1, s, cs, last=(s == 1))
            hi(PAIRS, 0, range(SUBS))
            z_hi(NE - 1)
            y_half(0, quarters_before(PAIRS, 0), (PAIRS - 1) * 16)
            hi(PAIRS, 0, range(SUBS, 4))
            y_half(1, quarters_before(PAIRS, 0) + 4, (PAIRS - 1) * 16)

            eng.wait_ge(flag_ready, 1)
            most = eng.value_load(flag[0:1, 0:1], min_val=0, max_val=T)
            with eng.If(most > CAP):
                with eng.Fori(0, NE) as e:
                    for b in range(OB):
                        eng.wait_ge(o_trans, e * OB + b + 1)
                        eng.activation(oxgT[:, 0:4, b * OC:(b + 1) * OC],
                                       bank[0][:, 0:4 * OC].rearrange("p (k t) -> p k t", k=4),
                                       ACT.Copy).then_inc(o_xgT, 1)
                    for j in range(JF):
                        eng.wait_ge(o_prod, e * (2 * JF) + 2 * j + 1)
                        eng.wait_ge(o_z, e * JF + j + 1)
                        eng.activation(osil, bank[2][:, 0:OT], ACT.Silu).then_inc(o_silu, 1)
                    for b in range(OB):
                        eng.wait_ge(o_down, e * OB + b + 1)
                        eng.activation(oy[0:OC, 0:512], bank[4][0:OC, :], ACT.Copy).then_inc(o_y, 1)
                        eng.wait_ge(o_y, e * (2 * OB) + 2 * b + 3)
                        eng.dma_start(oy_rows[e, b * OC:(b + 1) * OC, :], oy[0:OC, :]).then_inc(o_yout, 16)
                        eng.wait_ge(o_yout, e * (16 * OB) + 16 * b + 16)
                    eng.sem_inc(o_end, 1)

            for t in range(TT):
                eng.wait_ge(yg_in[t], 32)
                eng.wait_ge(slots_ready, t + 1)
                eng.activation(yg[:, t, 0, :], yg[:, t, 0, :], ACT.Copy, scale=main_w[:, t, 0:1])\
                    .then_inc(y0_scaled, 1)
            for t in range(TT):
                eng.wait_ge(res_ready, t + 1)
                if t:
                    eng.wait_ge(ssq_ready, 2 * TT + t)
                eng.activation(o_junk, x_rows[:, t, :], ACT.Square, accum_out=stat[:, 2, 0, t:t + 1])\
                    .then_inc(ssq_ready, 1)
                eng.wait_ge(mean_ready, TT + t + 2)
                eng.activation(stat[:, 2, 2, t:t + 1], stat[:, 2, 1, t:t + 1], ACT.Sqrt)\
                    .then_inc(rms_ready, 1)
            eng.wait_ge(state_out, 16)

        @block.vector
        def _(eng):
            steps = [0]

            def then(ins):
                ins.then_inc(step_v, 1)
                steps[0] += 1
                eng.wait_ge(step_v, steps[0])

            def tile(name):
                n = N_OF[name]
                eng.wait_ge(tile_done, n + 1)
                return bank[n % BANKS], bank_free[n % BANKS]

            eng.memset(cpad, 0.0).then_inc(pads_zero, 1)
            eng.memset(lg[:, :, :], -3.0e38)

            def copy_params():
                for j, (a, b) in enumerate(((0, NPA), (NPA, NPAR))):
                    ps, free = tile(("par", j))
                    eng.tensor_copy(pT[:, a:b], ps[:, 0:b - a]).then_inc(free, 1)
                    wait_read(eng, ("par", j))

            def mean_square(norm, sl):
                eng.tensor_scalar(stat[:, norm, 1, sl], stat[:, norm, 0, sl], 1.0 / D, EPS,
                                  ALU.mult, ALU.add).then_inc(mean_ready, 1)

            eng.wait_ge(ssq_ready, TT)
            mean_square(0, slice(0, TT))
            eng.wait_ge(rms_ready, 1)
            then(eng.reciprocal(stat[:, 0, 0, :], stat[:, 0, 2, :]))
            for t in range(TT):
                eng.tensor_scalar(xs[:, t, :], x_in_rows[:, t, :], stat[:, 0, 0, t:t + 1], None, ALU.mult)\
                    .then_inc(xs_ready, 1)
                if t == 1:
                    copy_params()
            eng.wait_ge(cvec_ready, 2)
            eng.wait_ge(consts, 2)
            eng.tensor_scalar(cst_all[:, 4 * KD:], ones[:, :], 0.0, None, ALU.mult)
            eng.tensor_tensor(cst[:, :, 2:4], cvec[:, :, :], cst[:, :, 0:2].bitcast(F32), ALU.subtract)\
                .then_inc(cvec_ready, 1)
            eng.memset(xrp[:, :, :], 0.0).then_inc(pads_zero, 1)

            eng.wait_ge(consts, 6)
            eng.tensor_tensor(selc[:, :], ident[0:5, 0:2], ident[0:5, 2:4], ALU.add).then_inc(selectors, 1)
            eng.wait_ge(selectors, 1)
            eng.tensor_scalar(selv[:, :], selc[:, :], ident[0:5, 4:5], None, ALU.add).then_inc(selectors, 1)
            eng.wait_ge(selectors, 2)
            for cnd in range(2):
                eng.tensor_scalar(selb[:, cnd, :], ones[0:5, :], selv[:, cnd:cnd + 1], None, ALU.mult)\
                    .then_inc(selectors, 1)

            def ada_lo(j, ms):
                for m in ms:
                    write_lo(eng, 4 * C_OF[("ada", j)] + m, lo_v)

            def ada_columns(j):
                ps, free = tile(("adaC", j))
                bias = pT[:, BADA + CT * j:BADA + CT * (j + 1)]
                for cnd in range(2):
                    last = eng.tensor_tensor(
                        mod[:, CT * j:CT * (j + 1), cnd],
                        ps[:, 0:2 * CT].rearrange("p (m c) -> p m c", c=2)[:, :, cnd], bias, ALU.add)
                last.then_inc(free, 1)

            for j in range(4):
                ada_lo(j, range(0, 2))
                if j >= 2:
                    ada_columns(j - 2)
                ada_lo(j, range(2, CT))
            ada_columns(2)
            ada_columns(3)
            for j in range(4):
                wait_read(eng, ("adaC", j))
            for cnd in range(2):
                last = eng.scalar_tensor_tensor(out=A1[:, :, cnd], in0=mod[:, KD:2 * KD, cnd], scalar=1.0,
                                                in1=pT[:, GN1:GN1 + KD], op0=ALU.add, op1=ALU.mult)
            then(last)
            def split_lo(x_hl, x, k, count, done):
                eng.wait_ge(act_hi, count)
                eng.tensor_tensor(x_hl[:, 1, k, :], x[:, k, :], x_hl[:, 0, k, :].bitcast(F32), ALU.subtract)\
                    .then_inc(done, 1)

            for k in range(KD + 1):
                if k < KD:
                    wait_read(eng, ("xT", k))
                    for cnd, (a, b) in enumerate(((0, NP_TOK), (NP_TOK, T))):
                        last = eng.tensor_scalar(xTr[:, k, a:b], xTr[:, k, a:b], A1[:, k, cnd:cnd + 1],
                                                 mod[:, k, cnd:cnd + 1], ALU.mult, ALU.add)
                    last.then_inc(h_whole, 1)
                if k:
                    eng.wait_ge(h_whole, k)
                    split_lo(h_hl, xTr, k - 1, k, h_ready)

            def conv_rnn(h):
                wait_read(eng, ("xr", h))
                src = xrp[:, h % 2, :]
                then(eng.tensor_scalar(xc[:, h, :], src[:, 0:TG], pT[:, RCW + h:RCW + h + 1],
                                       pT[:, RCB + h:RCB + h + 1], ALU.mult, ALU.add))
                for tap in range(1, 4):
                    col = RCW + tap * KD + h
                    ins = eng.scalar_tensor_tensor(out=xc[:, h, :], in0=src[:, tap:tap + TG],
                                                   scalar=pT[:, col:col + 1], in1=xc[:, h, :],
                                                   op0=ALU.mult, op1=ALU.add)
                    if tap < 3:
                        then(ins)
                ins.then_inc(xc_ready, 1)

            def decay_rates():
                eng.wait_ge(lam_exp, 1)
                then(eng.tensor_scalar(sp[:, 2, :], sp[:, 1, :], 2.0, None, ALU.add))
                then(eng.reciprocal(sp[:, 3, :], sp[:, 2, :]))
                then(eng.tensor_tensor(sp[:, 2, :], sp[:, 1, :], sp[:, 3, :], ALU.mult))
                then(eng.tensor_tensor(sp[:, 3, :], sp[:, 2, :], sp[:, 2, :], ALU.mult))
                then(eng.tensor_scalar(sp[:, 4, :], sp[:, 3, :], 1.0 / 17, None, ALU.mult))
                for odd in (15, 13, 11, 9, 7, 5, 3):
                    then(eng.scalar_tensor_tensor(out=sp[:, 4, :], in0=sp[:, 4, :], scalar=1.0 / odd,
                                                  in1=sp[:, 3, :], op0=ALU.add, op1=ALU.mult))
                then(eng.scalar_tensor_tensor(out=sp[:, 4, :], in0=sp[:, 4, :], scalar=1.0,
                                              in1=sp[:, 2, :], op0=ALU.add, op1=ALU.mult))
                then(eng.tensor_scalar(sp[:, 5, :], pT[:, LAM:NPAR], -1.0, 0.0, ALU.mult, ALU.max))
                then(eng.scalar_tensor_tensor(out=sp[:, 5, :], in0=sp[:, 4, :], scalar=2.0,
                                              in1=sp[:, 5, :], op0=ALU.mult, op1=ALU.add))
                eng.tensor_scalar(rate[:, 0, :], sp[:, 5, :], -RG_C, None, ALU.mult)
                eng.tensor_scalar(rate[:, 1, :], sp[:, 5, :], RG_C, None, ALU.mult).then_inc(rate_ready, 1)

            def gate_inputs(b):
                for h in (2 * b, 2 * b + 1):
                    for d in range(2):
                        n = N_OF[("gate", h, d, 1)]
                        eng.wait_ge(bank_free[n % BANKS], n // BANKS + 1)
                eng.wait_ge(xc_ready, 2 * b + 2)
                for d in range(2):
                    eng.tensor_tensor(i_b[:, d, :, :], i_b[:, d, :, :], xc[:, 2 * b:2 * b + 2, :], ALU.mult)
                eng.wait_ge(exp_done, 8 * (b + 1))
                then(eng.tensor_tensor(q_f, a_f, a_f, ALU.mult))
                eng.scalar_tensor_tensor(out=r_f, in0=q_f, scalar=1.0, in1=r_f, op0=ALU.add,
                                         op1=ALU.mult).then_inc(q_ready, 1)

            def scans(b):
                eng.wait_ge(root_done, b + 1)
                then(eng.tensor_tensor(i_f, i_f, r_f, ALU.mult))
                eng.memset(a_b[:, :, :, NP_TOK:S0], 0.0)
                then(eng.memset(i_b[:, :, :, NP_TOK:S0], 0.0))
                then(eng.tensor_copy(i_b[:, 0, :, S0 - 1], pT[:, STF + 2 * b:STF + 2 * b + 2]))
                for hh in range(2):
                    h = 2 * b + hh
                    eng.tensor_tensor_scan(r_b[:, 0, hh, :], a_b[:, 0, hh, :], i_b[:, 0, hh, :], 0.0,
                                           ALU.mult, ALU.add)
                    last = eng.tensor_tensor_scan(r_b[:, 1, hh, ::-1], a_b[:, 1, hh, ::-1],
                                                  i_b[:, 1, hh, ::-1], pT[:, STB + h:STB + h + 1],
                                                  ALU.mult, ALU.add)
                then(last)
                for a, z0, n in ((0, 0, NP_TOK), (NP_TOK, S0, NS_TOK)):
                    eng.tensor_tensor(hs[:, 2 * b:2 * b + 2, a:a + n], r_b[:, 0, :, z0:z0 + n],
                                      r_b[:, 1, :, z0:z0 + n], ALU.add)
                eng.tensor_copy(stc[:, 2 * b:2 * b + 2], r_b[:, 0, :, NP_TOK - 1])
                eng.tensor_copy(stc[:, KD + 2 * b:KD + 2 * b + 2], r_b[:, 1, :, 0]).then_inc(batch_done, 1)

            def conv_grid(half):
                for m in range(CT):
                    k = CT * half + m
                    n = N_OF[("c", k)]
                    eng.wait_ge(bank_free[n % BANKS], n // BANKS + 1)
                    ps, free = tile(("v", k))
                    src = cpad[:, m, :]
                    grid = src[:, 2 + NP_TOK:].rearrange("p (r q) -> p r q", r=ROWS)[:, :, 0:GRID_W]
                    eng.tensor_tensor(src[:, 1:1 + NP_TOK], ps[:, 0:NP_TOK], src[:, 1:1 + NP_TOK], ALU.mult)
                    eng.tensor_tensor(grid, ps[:, NP_TOK:T].rearrange("p (r q) -> p r q", r=ROWS), grid,
                                      ALU.mult).then_inc(free, 1)
                    eng.wait_ge(free, N_OF[("v", k)] // BANKS + 1)
                    if half:
                        wait_read(eng, ("b", m))
                    dst = ycv[:, m, 0:CG - 2]
                    then(eng.tensor_scalar(dst, src[:, 0:CG - 2], pT[:, CVW + k:CVW + k + 1], None, ALU.mult))
                    for tap in range(1, 3):
                        col = CVW + tap * KD + k
                        ins = eng.scalar_tensor_tensor(out=dst, in0=src[:, tap:tap + CG - 2],
                                                       scalar=pT[:, col:col + 1], in1=dst,
                                                       op0=ALU.mult, op1=ALU.add)
                        if tap < 2:
                            then(ins)
                    ins.then_inc(conv_done, 1)

            def times_b(half):
                for m in range(CT):
                    k = CT * half + m
                    eng.wait_ge(conv_done, k + 1)
                    ps, free = tile(("b", k))
                    y = ycv[:, m, :]
                    eng.tensor_tensor(ya_in[:, k, 0:NP_TOK], ps[:, 0:NP_TOK], y[:, 0:NP_TOK], ALU.mult)
                    eng.tensor_tensor(
                        ya_in[:, k, NP_TOK:T].rearrange("p (r q) -> p r q", r=ROWS),
                        ps[:, NP_TOK:T].rearrange("p (r q) -> p r q", r=ROWS),
                        y[:, 1 + NP_TOK:1 + NP_TOK + ROWS * (GRID_W + 1)]
                        .rearrange("p (r q) -> p r q", r=ROWS)[:, :, 0:GRID_W], ALU.mult)\
                        .then_inc(free, 1)

            def times_gelu(half):
                for m in range(CT):
                    k = CT * half + m
                    n = N_OF[("g", k)]
                    eng.wait_ge(bank_free[n % BANKS], n // BANKS + 1)
                    eng.wait_ge(batch_done, k // 2 + 1)
                    eng.tensor_tensor(hs[:, k, :], hs[:, k, :], gtmp[:, k % 2, :], ALU.mult)\
                        .then_inc(hg_ready, 1)

            conv_rnn(0)
            conv_rnn(1)
            decay_rates()
            conv_rnn(2)
            conv_rnn(3)
            gate_inputs(0)
            conv_rnn(4)
            scans(0)
            for h in range(5, KD):
                conv_rnn(h)
            gate_inputs(1)
            scans(1)
            conv_grid(0)
            times_b(0)
            gate_inputs(2)
            scans(2)
            times_gelu(0)
            gate_inputs(3)
            scans(3)
            conv_grid(1)
            times_b(1)
            times_gelu(1)
            for k in range(KD):
                eng.wait_ge(hg_ready, k + 1)
                split_lo(hs_hl, hs, k, KD + k + 1, hs_split)
            for k in range(KD):
                ps, free = tile(("yb", k))
                wait_read(eng, ("mb", k))
                eng.tensor_tensor(SB[:, k, :], ps[:, 0:T], SB[:, k, :], ALU.mult).then_inc(free, 1)
                if k == 2:
                    for kk in range(KD):
                        split_lo(h_hl, ya_in, kk, 2 * KD + kk + 1, ya_split)
            for k in range(KD):
                ps, free = tile(("ya", k))
                wait_read(eng, ("ma", k))
                eng.tensor_tensor(SA[:, k, :], ps[:, 0:T], SA[:, k, :], ALU.mult).then_inc(free, 1)
                wait_read(eng, ("ya", k))
                wait_read(eng, ("yb", k))
                eng.tensor_tensor(SA[:, k, :], SA[:, k, :], SB[:, k, :], ALU.add).then_inc(merged_ready, 1)
            for j in range(4, 12):
                ada_lo(j, range(0, 2))
                if j >= 6:
                    ada_rows_of(eng, j - 2, 1)
                ada_lo(j, range(2, CT))
            ada_rows_of(eng, 10, 1)
            ada_rows_of(eng, 11, 1)

            def residual(t):
                cnd = 0 if t == 0 else 1
                for half in range(2):
                    cols = slice(half * CW, (half + 1) * CW)
                    ps, free = tile(("wo", t, half))
                    eng.tensor_tensor(wo_tmp, ps[:, :], G1[:, cnd, cols], ALU.mult).then_inc(free, 1)
                    eng.wait_ge(free, N_OF[("wo", t, half)] // BANKS + 1)
                    ins = eng.tensor_tensor(x_rows[:, t, cols], x_rows[:, t, cols], wo_tmp, ALU.add)
                    if half == 0:
                        then(ins)
                ins.then_inc(x1_ready, 1)
                eng.wait_ge(ssq_ready, TT + t + 1)
                mean_square(1, slice(t, t + 1))

            def norm2(t):
                cnd = 0 if t == 0 else 1
                eng.wait_ge(rms_ready, t + 2)
                then(eng.reciprocal(stat[:, 1, 0, t:t + 1], stat[:, 1, 2, t:t + 1]))
                if t >= 2:
                    eng.wait_ge(h2_out[t - 2], 16)
                    eng.wait_ge(tile_done, N_OF[("h2T", t - 2, 1)] + 1)
                halves = [slice(a, a + CW) for a in range(0, D, CW)]
                for cols in halves:
                    last = eng.scalar_tensor_tensor(out=h2[:, t % 2, cols], in0=x_rows[:, t, cols],
                                                    scalar=stat[:, 1, 0, t:t + 1], in1=A2[:, cnd, cols],
                                                    op0=ALU.mult, op1=ALU.mult)
                then(last)
                for cols in halves:
                    eng.tensor_tensor(h2[:, t % 2, cols], h2[:, t % 2, cols], B2[:, cnd, cols], ALU.add)\
                        .then_inc(h2_ready, 1)

            def choose(t):
                r, u = rt[:, t, :], rti[:, t, :]
                ps, free = tile(("route", t))
                eng.wait_ge(bias_in, 32)
                eng.tensor_tensor(lg[:, t, 0:NG], ps[:, 0:NG], br[:, 0:NG], ALU.add)
                eng.tensor_tensor(le[:, t, :], ps[:, NG:NG + NE], br[:, NG:], ALU.add).then_inc(free, 1)
                wait_read(eng, ("route", t))
                then(eng.max(r[:, 8:16], lg[:, t, :]))
                then(eng.max_index(u[:, 0:8], r[:, 8:16], lg[:, t, :]))
                then(eng.tensor_copy(r[:, 36:37], u[:, 0:1]))
                then(eng.tensor_scalar(r[:, 40:40 + NG], iota[:, 0:NG], r[:, 36:37], None, ALU.is_equal))
                then(eng.tensor_scalar(r[:, 16:24], le[:, t, 0:EG], r[:, 40:41], None, ALU.mult))
                for g in range(1, NG):
                    then(eng.scalar_tensor_tensor(out=r[:, 16:24], in0=le[:, t, g * EG:(g + 1) * EG],
                                                  scalar=r[:, 40 + g:41 + g], in1=r[:, 16:24],
                                                  op0=ALU.mult, op1=ALU.add))
                then(eng.max(r[:, 24:32], r[:, 16:24]))
                then(eng.max_index(u[:, 8:16], r[:, 24:32], r[:, 16:24]))
                eng.tensor_scalar(r[:, 32:33], r[:, 8:9], -1.0, None, ALU.mult)
                eng.tensor_tensor(r[:, 35:36], r[:, 25:26], r[:, 24:25], ALU.subtract)\
                    .then_inc(tops_ready, 1)
                eng.tensor_scalar(r[:, 37:38], r[:, 36:37], float(EG), None, ALU.mult)
                then(eng.tensor_copy(r[:, 44:46], u[:, 8:10]))
                then(eng.tensor_scalar(r[:, 46:48], r[:, 44:46], r[:, 37:38], None, ALU.add))
                for k in range(2):
                    last = eng.tensor_scalar(pick[:, t, k, :], iota[:, 0:NE], r[:, 46 + k:47 + k], None,
                                             ALU.is_equal)
                then(last)
                eng.tensor_tensor(both[:, t, :], pick[:, t, 0, :], pick[:, t, 1, :], ALU.add)\
                    .then_inc(both_ready, 1)
                for k in range(2):
                    last = eng.tensor_scalar(tok_oh[:, t, k, :], pick[:, t, k, :], tok[:, t:t + 1], None,
                                             ALU.mult)

            def weights(t):
                r = rt[:, t, :]
                eng.wait_ge(texp_ready, t + 1)
                then(eng.tensor_scalar(r[:, 48:49], r[:, 34:35], 1.0, None, ALU.add))
                then(eng.tensor_tensor(r[:, 49:50], r[:, 48:49], r[:, 33:34], ALU.mult))
                then(eng.reciprocal(wts[:, t, 0:1], r[:, 49:50]))
                then(eng.tensor_tensor(wts[:, t, 1:2], wts[:, t, 0:1], r[:, 34:35], ALU.mult))

            def place(t):
                ps, free = tile(("rank", t))
                for k in range(2):
                    ins = eng.tensor_tensor(rank_m[:, k, :], ps[:, 0:NE], pick[:, t, k, :], ALU.mult)
                ins.then_inc(free, 1)
                wait_read(eng, ("rank", t))
                then(eng.reduce_sum(rank[:, t, :], rank_m[:, :, :], AX_X))
                for k in range(2):
                    last = eng.tensor_scalar(rank_oh[:, t, k, :], iota[:, 0:CAP], rank[:, t, k:k + 1],
                                             None, ALU.is_equal)
                last.then_inc(onehots_ready, 1)

            def slots(t):
                eng.scalar_tensor_tensor(out=main_w[:, t, :], in0=rank[:, t, :], scalar=float(CAP),
                                         in1=wts[:, t, :], op0=ALU.is_lt, op1=ALU.mult)
                then(eng.tensor_scalar(slot_f[:, t, :], rank[:, t, :], float(CAP - 1), None, ALU.min))
                then(eng.scalar_tensor_tensor(out=slot_f[:, t, :], in0=rt[:, t, 46:48], scalar=float(CAP),
                                              in1=slot_f[:, t, :], op0=ALU.mult, op1=ALU.add))
                eng.tensor_copy(slot_u[:, t, :], slot_f[:, t, :]).then_inc(slots_ready, 1)

            for j in range(4, 12):
                for cnd in range(2):
                    wait_read(eng, ("adaB", j, cnd))
            eng.wait_ge(x_again, 32)
            eng.wait_ge(consts, 6)
            residual(0)
            norm2(0)
            residual(1)
            norm2(1)
            choose(0)
            residual(2)
            norm2(2)
            choose(1)
            place(0)
            choose(2)
            place(1)
            place(2)
            ps, free = tile(("count",))
            eng.tensor_copy(counts[:, :], ps[:, 0:NE])
            eng.reduce_max(cmax[:, :], ps[:, 0:NE], AX_X).then_inc(free, 1)
            wait_read(eng, ("count",))
            eng.tensor_copy(flag[:, :], cmax[:, :]).then_inc(flag_ready, 1)
            ps, free = tile(("list",))
            eng.tensor_copy(lists[:, :], ps[0:CAP, 0:NE]).then_inc(free, 1)
            for a in (KD * CAP, XW + JF * CAP):
                eng.tensor_scalar(moe_hl[:, :, a:a + PAD], ones[:, 0:2 * PAD].rearrange("p (x n) -> p x n", x=2),
                                  0.0, None, ALU.mult)

            def rows_lo(e):
                eng.wait_ge(xgT_a, e + 1)
                for b in range(2):
                    cols = slice(b * 4 * CAP, (b + 1) * 4 * CAP)
                    ins = eng.tensor_tensor(xgT_hl[:, 1, cols], bank[b][:, 0:4 * CAP],
                                            xgT_hl[:, 0, cols].bitcast(F32), ALU.subtract)
                ins.then_inc(xgT_v, 1)

            def z_lo(e):
                eng.wait_ge(zT_a, e + 1)
                eng.tensor_tensor(zT_hl[:, 1, 0:JF * CAP], bank[6][:, 0:JF * CAP],
                                  zT_hl[:, 0, 0:JF * CAP].bitcast(F32), ALU.subtract).then_inc(zT_v, 1)

            def y_half(s, used, stores):
                eng.wait_ge(moe_used, used)
                if stores is not None:
                    eng.wait_ge(y_out[s], stores)
                eng.tensor_copy(y_sb[0:CAP, s, 512:D], bank[5][0:CAP, :]).then_inc(y_v, 1)

            def hidden(i, e, c3, e0):
                eng.wait_ge(silu_done, e + 1)
                eng.wait_ge(moe_used, quarters_before(i, c3) + 4)
                if not e0:
                    eng.wait_ge(zT_done, e)
                eng.tensor_tensor(z, bank[3][0:CAP, :], sil, ALU.mult).then_inc(z_ready, 1)

            def expert(i, s, chunks3, e0=False, e1=False, last=False, js=range(4)):
                e = i * 2 + s
                c1, c3, c2 = chunks3
                moe_write_lo(eng, i, c1, js)
                if not e0:
                    z_lo(e - 1)
                if not e0 and not e1:
                    no_store = isinstance(i, int) and i == 1
                    y_half(s, quarters_before(i, c1), None if no_store else (i - 1) * 16)
                moe_write_lo(eng, i, c3)
                if e0:
                    hidden(i, e, c3, True)
                else:
                    moe_write_lo(eng, i, c2, range(0, 3))
                    hidden(i, e, c3, False)
                    moe_write_lo(eng, i, c2, range(3, 4))
                if not last:
                    rows_lo(e + 1)

            eng.wait_ge(moe_lo, 4)
            rows_lo(0)
            for t in range(TT):
                weights(t)
                slots(t)
            expert(0, 0, (1, 2, None), e0=True, js=())
            expert(0, 1, (3, 4, 5), e1=True)
            for s, cs in enumerate(pair_experts()):
                expert(1, s, cs)
            with eng.Fori(2, PAIRS - 1) as i:
                for s, cs in enumerate(pair_experts()):
                    expert(i, s, cs)
            for s, cs in enumerate(pair_experts()):
                expert(PAIRS - 1, s, cs, last=(s == 1))
            moe_write_lo(eng, PAIRS, 0, range(SUBS))
            z_lo(NE - 1)
            y_half(0, quarters_before(PAIRS, 0), (PAIRS - 1) * 16)
            moe_write_lo(eng, PAIRS, 0, range(SUBS, 4))
            y_half(1, quarters_before(PAIRS, 0) + 4, (PAIRS - 1) * 16)

            eng.wait_ge(gfin_in, 16)

            def add_experts(t, w, done, then):
                y0, y1 = yg[:, t, 0, :], yg[:, t, 1, :]
                then(eng.scalar_tensor_tensor(out=y0, in0=y1, scalar=w[:, t, 1:2], in1=y0,
                                              op0=ALU.mult, op1=ALU.add))
                then(eng.tensor_tensor(y0, y0, G2[:, 0 if t == 0 else 1, :], ALU.mult))
                eng.tensor_tensor(x_rows[:, t, :], x_rows[:, t, :], y0, ALU.add).then_inc(done, 1)

            eng.wait_ge(flag_ready, 1)
            most = eng.value_load(flag[0:1, 0:1], min_val=0, max_val=T)
            with eng.If(most > CAP):
                for b in range(OB):
                    for t in range(TT):
                        for k in range(2):
                            n = (b * TT + t) * 2 + k
                            if n:
                                eng.wait_ge(o_table, n)
                            eng.tensor_scalar(orank[:, b * OC:(b + 1) * OC],
                                              iota[:, CAP + b * OC:CAP + (b + 1) * OC],
                                              rank[:, t, k:k + 1], None, ALU.is_equal)\
                                .then_inc(o_onehot, 1)
                eng.wait_ge(o_table, OB * TT * 2)
                eng.tensor_copy(olist_f, bank[0][0:OC, 0:OB * NE])\
                    .then_inc(o_list, 1)
                eng.wait_ge(o_list, 1)
                eng.sem_inc(o_end, 1)
                eng.sem_inc(o_xgT, 1)
                eng.sem_inc(o_z, 1)
                eng.sem_inc(o_y, 1)
                with eng.Fori(0, NE) as e:
                    for b in range(OB):
                        eng.wait_ge(o_xgT, e * (2 * OB) + 2 * b + 2)
                        eng.tensor_copy(oxgT[:, 4:8, b * OC:(b + 1) * OC],
                                        bank[1][:, 0:4 * OC].rearrange("p (k t) -> p k t", k=4))\
                            .then_inc(o_xgT, 1)
                    for j in range(JF):
                        eng.wait_ge(o_silu, e * JF + j + 1)
                        eng.wait_ge(o_prod, e * (2 * JF) + 2 * j + 2)
                        eng.tensor_tensor(oz[:, j, :], bank[3][:, 0:OT], osil, ALU.mult).then_inc(o_z, 1)
                    for b in range(OB):
                        eng.wait_ge(o_y, e * (2 * OB) + 2 * b + 2)
                        eng.tensor_copy(oy[0:OC, 512:D], bank[5][0:OC, :]).then_inc(o_y, 1)
                o_steps = [0]

                def then_o(ins):
                    ins.then_inc(step_o, 1)
                    o_steps[0] += 1
                    eng.wait_ge(step_o, o_steps[0])

                for t in range(TT):
                    then_o(eng.tensor_scalar(oslot_f[:, t, :], rank[:, t, :], float(CAP), 0.0,
                                           ALU.subtract, ALU.max))
                    then_o(eng.scalar_tensor_tensor(out=oslot_f[:, t, :], in0=rt[:, t, 46:48],
                                                  scalar=float(OT), in1=oslot_f[:, t, :],
                                                  op0=ALU.mult, op1=ALU.add))
                    then_o(eng.scalar_tensor_tensor(out=over_w[:, t, :], in0=rank[:, t, :],
                                                  scalar=float(CAP), in1=wts[:, t, :],
                                                  op0=ALU.is_ge, op1=ALU.mult))
                eng.tensor_copy(oslot_u, oslot_f[:, :, :]).then_inc(o_slots, 1)
                for t in range(TT):
                    eng.wait_ge(o_yg_in[t], 32)
                    then_o(eng.tensor_scalar(yg[:, t, 0, :], yg[:, t, 0, :], over_w[:, t, 0:1], None, ALU.mult))
                    add_experts(t, over_w, o_added, then_o)

            def combine(t):
                eng.wait_ge(yg_in[t], 32)
                eng.wait_ge(y0_scaled, t + 1)
                add_experts(t, main_w, res_ready, then)

            def last_mean(t):
                eng.wait_ge(ssq_ready, 2 * TT + t + 1)
                mean_square(2, slice(t, t + 1))

            def last_norm(t):
                eng.wait_ge(rms_ready, TT + t + 2)
                then(eng.reciprocal(stat[:, 2, 0, t:t + 1], stat[:, 2, 2, t:t + 1]))
                eng.scalar_tensor_tensor(out=o_rows[:, t, :], in0=x_rows[:, t, :],
                                         scalar=stat[:, 2, 0, t:t + 1], in1=gfin,
                                         op0=ALU.mult, op1=ALU.mult).then_inc(out_ready, 1)

            combine(0)
            combine(1)
            last_mean(0)
            combine(2)
            last_mean(1)
            last_norm(0)
            last_mean(2)
            last_norm(1)
            last_norm(2)


_INS = ['x_prompt', 'x_sample', 'state_rnn', 'c', 'c_ctx', 'w_ada', 'b_ada', 'g_norm1', 'g_norm2', 'w_in',
        'conv_w', 'w_conv_out', 'rnn_conv_w', 'rnn_conv_b', 'w_gate_a', 'b_gate_a', 'w_gate_x',
        'b_gate_x', 'lam', 'w_rnn_out', 'w_o', 'w_router_group', 'b_router_group', 'w_router_expert',
        'b_router_expert', 'w1', 'w3', 'w2', 'g_final']


def kernel(**inputs):
    import numpy as _np
    import concourse.bacc as _bacc
    from concourse import mybir as _mybir
    from concourse.bass_utils import run_bass_kernel_spmd as _run

    nc = _bacc.Bacc("TRN2", target_bir_lowering=False, num_devices=1)
    arrays, args = {}, []
    for name in _INS:
        a = _np.ascontiguousarray(inputs[name])
        arrays[f"in_{name}"] = a
        args.append(nc.dram_tensor(f"in_{name}", a.shape, _mybir.dt.from_np(a.dtype), kind="ExternalInput").ap())
    d = inputs["c"].shape[1]
    outs = [inputs["x_prompt"].shape, inputs["x_sample"].shape, (inputs["x_prompt"].shape[0], 1, 2, d)]
    for i, shape in enumerate(outs):
        args.append(nc.dram_tensor(f"out_{i}", shape, _mybir.dt.float32, kind="ExternalOutput").ap())
    layer_program(nc, *args)
    r = _run(nc, [arrays], core_ids=[0])
    return tuple(r.results[0][f"out_{i}"] for i in range(len(outs)))
```
